# Optimizing a Trainium2 kernel written in Bass

```python
import jax, jax.numpy as jnp
from jax import lax
import numpy as np

D_MODEL = 1024
BATCH = 1
SEQ = 256
DEPTH = 2

CHUNK = 64
N_EVEN = (DEPTH + 1) // 2
N_ODD = DEPTH // 2
EPS = 1e-6
NEG_INF = -1e30

HEAD_DIM = 64
A_HEADS = 8
A_KV_HEADS = 2
A_GROUP = A_HEADS // A_KV_HEADS
A_WINDOW = 128
A_WIN_CHUNKS = A_WINDOW // CHUNK
B_HEADS = 8
B_LEFT_CHUNKS = 8
B_MAX_REL = 256
A_Q_W = A_HEADS * HEAD_DIM
A_KV_W = A_KV_HEADS * HEAD_DIM
B_W = B_HEADS * HEAD_DIM
IN_W = A_Q_W + 2 * A_KV_W + 3 * B_W
IN_SPLITS = [A_Q_W, A_Q_W + A_KV_W, A_Q_W + 2 * A_KV_W, A_Q_W + 2 * A_KV_W + B_W, A_Q_W + 2 * A_KV_W + 2 * B_W]
MIX_W = A_Q_W + B_W
C_HEADS = 16
C_Q_LORA = 384
C_KV_LORA = 256
C_NOPE = 64
C_ROPE = 32
C_QK = C_NOPE + C_ROPE
C_V = 64
ROPE_THETA = 10000.0
Q_BLOCK = 128
D_FF = 2816
N_EXPERTS = 8
TOP_K = 2
EXPERT_FF = 3584

kernel_name = "hybrid_chunk_causal_swa_u2_mla_moe"

def rms_norm(x, g):
    xf = x.astype(jnp.float32)
    y = xf * lax.rsqrt(jnp.mean(xf * xf, axis=-1, keepdims=True) + EPS)
    return (y * g.astype(jnp.float32)).astype(x.dtype)

def swiglu(h, w_gate, w_up, w_down):
    return (jax.nn.silu(h @ w_gate) * (h @ w_up)) @ w_down

def alibi_slopes(n):
    return jnp.asarray(2.0 ** (-8.0 * np.arange(1, n + 1) / n), dtype=jnp.float32)

def band_indices(n_chunks, back):
    band = (back + 1) * CHUNK
    idx = jnp.arange(n_chunks)[:, None] * CHUNK - back * CHUNK + jnp.arange(band)[None, :]
    return jnp.maximum(idx, 0), idx >= 0

def mixer_a(q, k, v, q_gain, k_gain, sinks):
    b, s = q.shape[:2]
    nc = s // CHUNK
    band = A_WIN_CHUNKS * CHUNK
    q = rms_norm(q, q_gain)
    k = rms_norm(k, k_gain)
    idx, valid = band_indices(nc, A_WIN_CHUNKS - 1)
    kb = jnp.take(k, idx, axis=1)
    vb = jnp.take(v, idx, axis=1)
    qc = q.reshape(b, nc, CHUNK, A_KV_HEADS, A_GROUP, HEAD_DIM)
    sc = jnp.einsum("bcikgd,bcjkd->bckgij", qc, kb).astype(jnp.float32) * (HEAD_DIM ** -0.5)
    dist = jnp.abs(jnp.arange(CHUNK)[:, None] - jnp.arange(band)[None, :] + (band - CHUNK)).astype(jnp.float32)
    slopes = alibi_slopes(A_HEADS).reshape(A_KV_HEADS, A_GROUP)
    sc = sc - slopes[:, :, None, None] * dist
    sc = jnp.where(valid[None, :, None, None, None, :], sc, NEG_INF)
    sink = sinks.astype(jnp.float32).reshape(A_KV_HEADS, A_GROUP)[:, :, None, None]
    m = jnp.maximum(jnp.max(sc, axis=-1, keepdims=True), sink)
    p = jnp.exp(sc - m)
    p = (p / (jnp.sum(p, axis=-1, keepdims=True) + jnp.exp(sink - m))).astype(v.dtype)
    o = jnp.einsum("bckgij,bcjkd->bcikgd", p, vb)
    return o.reshape(b, s, A_HEADS * HEAD_DIM)

def mixer_b(q, k, v, q_gain, k_gain, rel_bias):
    b, s = q.shape[:2]
    nc = s // CHUNK
    band = (B_LEFT_CHUNKS + 1) * CHUNK
    q = rms_norm(q, q_gain)
    k = rms_norm(k, k_gain)
    idx, valid = band_indices(nc, B_LEFT_CHUNKS)
    kb = jnp.take(k, idx, axis=1)
    vb = jnp.take(v, idx, axis=1)
    qc = q.reshape(b, nc, CHUNK, B_HEADS, HEAD_DIM)
    sc = jnp.einsum("bcihd,bcjhd->bchij", qc, kb).astype(jnp.float32) * (HEAD_DIM ** -0.5)
    rel = jnp.arange(CHUNK)[:, None] - jnp.arange(band)[None, :] + (band - CHUNK)
    rel = jnp.clip(rel, -B_MAX_REL, B_MAX_REL) + B_MAX_REL
    sc = sc + rel_bias.astype(jnp.float32)[:, rel]
    sc = jnp.where(valid[None, :, None, None, :], sc, NEG_INF)
    p = jax.nn.softmax(sc, axis=-1).astype(v.dtype)
    o = jnp.einsum("bchij,bcjhd->bcihd", p, vb)
    return o.reshape(b, s, B_HEADS * HEAD_DIM)

def rope_tables(s):
    pos = jnp.arange(s, dtype=jnp.float32)
    inv_freq = 1.0 / (ROPE_THETA ** (jnp.arange(0, C_ROPE, 2, dtype=jnp.float32) / C_ROPE))
    ang = pos[:, None] * inv_freq[None, :]
    ang = jnp.concatenate([ang, ang], axis=-1)
    return jnp.cos(ang), jnp.sin(ang)

def apply_rope(x, cos, sin):
    half = x.shape[-1] // 2
    rot = jnp.concatenate([-x[..., half:], x[..., :half]], axis=-1)
    return (x.astype(jnp.float32) * cos[None, :, None, :] + rot.astype(jnp.float32) * sin[None, :, None, :]).astype(x.dtype)

def mixer_c(h, w_dq, q_a_gain, w_uq, w_dkv, kv_a_gain, w_ukv, q_gain, k_gain, w_o):
    b, s, _ = h.shape
    cq = rms_norm(h @ w_dq, q_a_gain)
    q = (cq @ w_uq).reshape(b, s, C_HEADS, C_QK)
    ckv_kr = h @ w_dkv
    ckv = rms_norm(ckv_kr[..., :C_KV_LORA], kv_a_gain)
    k_rope = ckv_kr[..., C_KV_LORA:]
    kv = (ckv @ w_ukv).reshape(b, s, C_HEADS, C_NOPE + C_V)
    k_nope, v = kv[..., :C_NOPE], kv[..., C_NOPE:]
    k = jnp.concatenate([k_nope, jnp.broadcast_to(k_rope[:, :, None, :], (b, s, C_HEADS, C_ROPE))], axis=-1)
    q = rms_norm(q, q_gain)
    k = rms_norm(k, k_gain)
    cos, sin = rope_tables(s)
    q = jnp.concatenate([q[..., :C_NOPE], apply_rope(q[..., C_NOPE:], cos, sin)], axis=-1)
    k = jnp.concatenate([k[..., :C_NOPE], apply_rope(k[..., C_NOPE:], cos, sin)], axis=-1)
    nb = s // Q_BLOCK
    q_blocks = q.reshape(b, nb, Q_BLOCK, C_HEADS, C_QK).transpose(1, 0, 2, 3, 4)
    key_chunk = jnp.arange(s) // CHUNK
    scale = C_QK ** -0.5

    def block(args):
        qb, blk = args
        sc = jnp.einsum("bqhd,bkhd->bhqk", qb, k).astype(jnp.float32) * scale
        q_chunk = (blk * Q_BLOCK + jnp.arange(Q_BLOCK)) // CHUNK
        mask = key_chunk[None, :] <= q_chunk[:, None]
        sc = jnp.where(mask[None, None], sc, NEG_INF)
        p = jax.nn.softmax(sc, axis=-1).astype(v.dtype)
        return jnp.einsum("bhqk,bkhd->bqhd", p, v)

    o = lax.map(block, (q_blocks, jnp.arange(nb)))
    o = o.transpose(1, 0, 2, 3, 4).reshape(b, s, C_HEADS * C_V)
    return o @ w_o

def moe_swiglu(h, router, e_gate, e_up, e_down):
    b, s, d = h.shape
    xt = h.reshape(b * s, d)
    logits = (xt @ router).astype(jnp.float32)
    top_vals, top_idx = lax.top_k(logits, TOP_K)
    w = jax.nn.softmax(top_vals, axis=-1)
    gates = jnp.einsum("nk,nke->ne", w, jax.nn.one_hot(top_idx, N_EXPERTS, dtype=jnp.float32)).astype(h.dtype)
    out = jnp.zeros_like(xt)
    for e in range(N_EXPERTS):
        out = out + gates[:, e:e + 1] * swiglu(xt, e_gate[e], e_up[e], e_down[e])
    return out.reshape(b, s, d)

def setup_inputs(seed: int = 0) -> dict:
    key = jax.random.key(seed)
    ks = iter(jax.random.split(key, 32))

    def w(shape, fan_in):
        return jax.random.normal(next(ks), shape, jnp.float32) * (fan_in ** -0.5)

    def gain(shape):
        return 1.0 + 0.02 * jax.random.normal(next(ks), shape, jnp.float32)

    return {
        "x": jax.random.normal(next(ks), (BATCH, SEQ, D_MODEL), jnp.float32),
        "ev_attn_norm": gain((N_EVEN, D_MODEL)),
        "ev_w_in": w((N_EVEN, D_MODEL, IN_W), D_MODEL),
        "ev_a_q_norm": gain((N_EVEN, HEAD_DIM)),
        "ev_a_k_norm": gain((N_EVEN, HEAD_DIM)),
        "ev_a_sinks": 0.5 * jax.random.normal(next(ks), (N_EVEN, A_HEADS), jnp.float32),
        "ev_b_q_norm": gain((N_EVEN, HEAD_DIM)),
        "ev_b_k_norm": gain((N_EVEN, HEAD_DIM)),
        "ev_b_rel_bias": 0.1 * jax.random.normal(next(ks), (N_EVEN, B_HEADS, 2 * B_MAX_REL + 1), jnp.float32),
        "ev_w_out": w((N_EVEN, MIX_W, D_MODEL), MIX_W),
        "ev_ffn_norm": gain((N_EVEN, D_MODEL)),
        "ev_w_gate": w((N_EVEN, D_MODEL, D_FF), D_MODEL),
        "ev_w_up": w((N_EVEN, D_MODEL, D_FF), D_MODEL),
        "ev_w_down": w((N_EVEN, D_FF, D_MODEL), D_FF),
        "od_attn_norm": gain((N_ODD, D_MODEL)),
        "od_w_dq": w((N_ODD, D_MODEL, C_Q_LORA), D_MODEL),
        "od_q_a_norm": gain((N_ODD, C_Q_LORA)),
        "od_w_uq": w((N_ODD, C_Q_LORA, C_HEADS * C_QK), C_Q_LORA),
        "od_w_dkv": w((N_ODD, D_MODEL, C_KV_LORA + C_ROPE), D_MODEL),
        "od_kv_a_norm": gain((N_ODD, C_KV_LORA)),
        "od_w_ukv": w((N_ODD, C_KV_LORA, C_HEADS * (C_NOPE + C_V)), C_KV_LORA),
        "od_q_norm": gain((N_ODD, C_QK)),
        "od_k_norm": gain((N_ODD, C_QK)),
        "od_w_o": w((N_ODD, C_HEADS * C_V, D_MODEL), C_HEADS * C_V),
        "od_ffn_norm": gain((N_ODD, D_MODEL)),
        "od_router": w((N_ODD, D_MODEL, N_EXPERTS), D_MODEL),
        "od_e_gate": w((N_ODD, N_EXPERTS, D_MODEL, EXPERT_FF), D_MODEL),
        "od_e_up": w((N_ODD, N_EXPERTS, D_MODEL, EXPERT_FF), D_MODEL),
        "od_e_down": w((N_ODD, N_EXPERTS, EXPERT_FF, D_MODEL), EXPERT_FF),
    }

def reference(x, ev_attn_norm, ev_w_in, ev_a_q_norm, ev_a_k_norm, ev_a_sinks, ev_b_q_norm, ev_b_k_norm,
              ev_b_rel_bias, ev_w_out, ev_ffn_norm, ev_w_gate, ev_w_up, ev_w_down,
              od_attn_norm, od_w_dq, od_q_a_norm, od_w_uq, od_w_dkv, od_kv_a_norm, od_w_ukv,
              od_q_norm, od_k_norm, od_w_o, od_ffn_norm, od_router, od_e_gate, od_e_up, od_e_down):
    b, s, _ = x.shape
    for layer in range(DEPTH):
        i = layer // 2
        if layer % 2 == 0:
            h = rms_norm(x, ev_attn_norm[i])
            proj = h @ ev_w_in[i]
            a_q, a_k, a_v, b_q, b_k, b_v = jnp.split(proj, IN_SPLITS, axis=-1)
            out_a = mixer_a(a_q.reshape(b, s, A_HEADS, HEAD_DIM),
                            a_k.reshape(b, s, A_KV_HEADS, HEAD_DIM),
                            a_v.reshape(b, s, A_KV_HEADS, HEAD_DIM),
                            ev_a_q_norm[i], ev_a_k_norm[i], ev_a_sinks[i])
            out_b = mixer_b(b_q.reshape(b, s, B_HEADS, HEAD_DIM),
                            b_k.reshape(b, s, B_HEADS, HEAD_DIM),
                            b_v.reshape(b, s, B_HEADS, HEAD_DIM),
                            ev_b_q_norm[i], ev_b_k_norm[i], ev_b_rel_bias[i])
            x = x + jnp.concatenate([out_a, out_b], axis=-1) @ ev_w_out[i]
            h = rms_norm(x, ev_ffn_norm[i])
            x = x + swiglu(h, ev_w_gate[i], ev_w_up[i], ev_w_down[i])
        else:
            h = rms_norm(x, od_attn_norm[i])
            x = x + mixer_c(h, od_w_dq[i], od_q_a_norm[i], od_w_uq[i], od_w_dkv[i], od_kv_a_norm[i],
                            od_w_ukv[i], od_q_norm[i], od_k_norm[i], od_w_o[i])
            h = rms_norm(x, od_ffn_norm[i])
            x = x + moe_swiglu(h, od_router[i], od_e_gate[i], od_e_up[i], od_e_down[i])
    return x


_drawn_inputs = setup_inputs


def setup_inputs(seed=0):
    import zlib

    import numpy as np

    out = dict(_drawn_inputs(seed))
    spreads = {}
    factors = {'ev_attn_norm': 4.529,
     'ev_a_k_norm': 3.171,
     'ev_a_sinks': 5.145,
     'ev_b_q_norm': 7.709,
     'ev_b_k_norm': 3.019,
     'od_q_a_norm': 4.307,
     'od_kv_a_norm': 8.0,
     'od_q_norm': 4.085,
     'od_k_norm': 4.319,
     'od_ffn_norm': 8.0}
    for name, (base, spread) in spreads.items():
        noise = np.random.default_rng([zlib.crc32(name.encode()), seed]).standard_normal(out[name].shape)
        drawn = base * np.exp(spread * noise) if base else spread * noise
        out[name] = __import__('jax').numpy.asarray(drawn.astype(out[name].dtype))
    for name, factor in factors.items():
        out[name] = (out[name] * factor).astype(out[name].dtype)
    return out
```

```python
from contextlib import ExitStack

import numpy as np

import concourse.bass as bass
from concourse import mybir

ALU = mybir.AluOpType
ACT = mybir.ActivationFunctionType
AX = mybir.AxisListType
F32 = mybir.dt.float32
F32R = mybir.dt.float32r
I32 = mybir.dt.int32

P = 128
D = 1024
KD = D // P
SEQ = 256
TB = SEQ // P
CHUNK = 64
EPS = 1e-6
NEG = -1e30
HD = 64
A_HEADS, A_KV, B_HEADS = 8, 2, 8
IN_W = 2304
MAX_REL = 256
C_HEADS, C_NOPE, C_ROPE, C_V = 16, 64, 32, 64
C_QK = C_NOPE + C_ROPE
Q_LORA, KV_LORA = 384, 256
D_FF = 2816
N_EXP = 8
E_FF = 3584
CAP = 128
OVER = 3
SLOTS = N_EXP + OVER
NW = 512
RING = 7
PIECE = KD * NW
SPLITS = 4
QUARTER = PIECE // 4
LEAD = SPLITS
HEADS0 = A_HEADS + B_HEADS
HEADS = HEADS0 + C_HEADS
LANES = 128 + 256

A_Q, A_K, A_V, B_Q, B_K, B_V = 0, 512, 640, 768, 1280, 1792
C_ID, C_TRI, C_IOTA, C_DIST, C_MASK, C_ROT = 0, 128, 256, 384, 768, 1152
C_ALL = C_ROT + TB * 2 * C_ROPE


def constants():
    c = np.zeros((P, C_ALL), np.float32)
    c[:, C_ID:C_ID + P] = np.eye(P)
    c[:, C_TRI:C_TRI + P] = np.triu(np.ones((P, P)), 1)
    c[:, C_IOTA:C_IOTA + P] = np.arange(P)
    for b, at, keys in ((0, 0, P), (1, P, 2 * P)):
        q = (b * P + np.arange(P))[:, None]
        k = np.arange(keys)[None, :]
        qc, kc = q // CHUNK, k // CHUNK
        c[:, C_DIST + at:C_DIST + at + keys] = np.where((kc <= qc) & (kc >= qc - 1), -np.abs(q - k), NEG)
        c[:, C_MASK + at:C_MASK + at + keys] = np.where(kc <= qc, 0.0, NEG)
    pos = np.arange(SEQ, dtype=np.float32)
    power = np.arange(0, C_ROPE, 2, dtype=np.float32) / np.float32(C_ROPE)
    inv = (np.float32(1.0) / (np.float32(10000.0) ** power)).astype(np.float32)
    ang = (pos[:, None] * inv[None, :]).astype(np.float32)
    ang = np.concatenate([ang, ang], axis=-1)
    rot = np.stack([np.cos(ang), np.sin(ang)], axis=1).reshape(TB, P, 2 * C_ROPE)
    c[:, C_ROT:] = rot.transpose(1, 0, 2).reshape(P, -1)
    return c


def plan(w, last):
    pieces, quarters = [], []

    def add(stage, src, nk, n, place, kind="", c=0):
        per = 2 if n <= NW else 1
        first = len(quarters)
        for k in range(0, nk, per):
            quarters.append((len(pieces), k, min(per, nk - k)))
        pieces.append(dict(stage=stage, src=src, nk=nk, n=n, place=place, kind=kind, c=c, per=per,
                           q0=first, q1=len(quarters)))

    def cols(ap, c0, n):
        return ap[0, :, c0:c0 + n].rearrange("(k p) n -> p k n", p=P)

    for j, c0 in enumerate(range(0, IN_W, NW)):
        add("in", cols(w["w_in"], c0, min(NW, IN_W - c0)), KD, min(NW, IN_W - c0), j)
    for j in range(2):
        add("out", cols(w["w_out"], j * NW, NW), KD, NW, j)
    if last >= 2:
        place = 2
        chunks = [(c0, min(NW, D_FF - c0)) for c0 in range(0, D_FF, NW)]
        down = lambda c: w["w_down"][0, chunks[c][0]:sum(chunks[c]), :].rearrange("(k p) n -> p k n", p=P)
        for c, (c0, n) in enumerate(chunks):
            for kind, name in (("gate", "w_gate"), ("up", "w_up")):
                add("ffn", cols(w[name], c0, n), KD, n, place % RING, kind, c)
                place += 1
            for d in [c - 1] * (c > 0) + [c] * (c == len(chunks) - 1):
                add("ffn", down(d), chunks[d][1] // P, D, place % RING, "down", d)
                place += 1
    if last >= 3:
        small = [("dq", cols(w["w_dq"], 0, Q_LORA), KD, Q_LORA),
                 ("dkv", cols(w["w_dkv"], 0, KV_LORA + C_ROPE), KD, KV_LORA + C_ROPE)]
        small += [("uq", cols(w["w_uq"], j * NW, NW), Q_LORA // P, NW) for j in range(3)]
        small += [("ukv", cols(w["w_ukv"], j * NW, NW), KV_LORA // P, NW) for j in range(4)]
        for j, (stage, src, nk, n) in enumerate(small):
            add(stage, src, nk, n, j % 3)
        for j in range(2):
            add("o", cols(w["w_o"], j * NW, NW), KD, NW, 3 + j)
    return pieces, quarters


def expert_order():
    order = []
    n = E_FF // NW
    for c in range(n):
        order += [("gate", c), ("up", c)]
        order += [("down", c - 1)] * (c > 0) + [("down", c)] * (c == n - 1)
    return order


def trunk(nc, a, out, last=4):
    x_in, const = a["x"], a["const"]
    weights = {"w_in": a["ev_w_in"], "w_out": a["ev_w_out"], "w_gate": a["ev_w_gate"], "w_up": a["ev_w_up"],
               "w_down": a["ev_w_down"], "w_dq": a["od_w_dq"], "w_uq": a["od_w_uq"], "w_dkv": a["od_w_dkv"],
               "w_ukv": a["od_w_ukv"], "w_o": a["od_w_o"]}
    pieces, quarters = plan(weights, last)
    NQ = len(quarters)
    order = expert_order()
    EQ = 4 * len(order)
    NCH = E_FF // NW
    uses = [0] * RING
    for p in pieces:
        p["turn"] = uses[p["place"]]
        uses[p["place"]] += 1
    stage_pieces = lambda s: [n for n, p in enumerate(pieces) if p["stage"] == s]

    with ExitStack() as ctx:
        def sb(name, shape, dt=F32):
            return ctx.enter_context(nc.sbuf_tensor(name, shape, dt))

        def sem(name):
            return ctx.enter_context(nc.semaphore(name))

        ring = sb("ring", [P, RING, PIECE])
        w_hi = sb("w_hi", [P, SPLITS, QUARTER], F32R)
        w_lo = sb("w_lo", [P, SPLITS, QUARTER], F32R)
        xres = sb("xres", [P, TB, D])
        h = sb("h", [P, TB, D])
        hT_hi = sb("hT_hi", [P, KD, SEQ], F32R)
        hT_lo = sb("hT_lo", [P, KD, SEQ], F32R)
        aT_hi = sb("aT_hi", [P, 5, SEQ], F32R)
        aT_lo = sb("aT_lo", [P, 5, SEQ], F32R)
        gs = sb("gs", [P, TB, NW])
        act_t = sb("act_t", [P, TB, NW])
        y = sb("y", [P, D])
        cst = sb("cst", [P, C_ALL])
        ones = sb("ones", [P, P])
        g_rows = sb("g_rows", [33, P])
        g_cols = sb("g_cols", [P, 33])
        gq = sb("gq", [P, C_QK])
        gk = sb("gk", [P, C_QK])
        sinks = sb("sinks", [P, A_HEADS])
        eps = sb("eps", [P, 1])
        ss = sb("ss", [P, 66])
        rt = sb("rt", [P, 66])
        rinv = sb("rinv", [P, 66])
        nmax = sb("nmax", [P, 2, 4])
        mx = sb("mx", [P, 2, 2])
        esum = sb("esum", [P, 2, 4])
        den = sb("den", [P, 2, 2])
        kr = sb("kr", [P, TB, C_ROPE])

        ident = cst[:, C_ID:C_ID + P]
        g_fwd = {0: 0, 1: 8, 2: 16}
        G_QA, G_KVA, G_AQ, G_AK, G_BQ, G_BK = 24, 27, 29, 30, 31, 32

        scratch = ring[:, 5:7, :].rearrange("p a b -> p (a b)")
        proj = scratch[:, 0:TB * IN_W].rearrange("p (t n) -> p t n", t=TB)
        kv = scratch[:, 0:4096].rearrange("p (t n) -> p t n", t=TB)
        qc = scratch[:, 4096:7168].rearrange("p (t n) -> p t n", t=TB)
        kbuf = scratch[:, 7168:7168 + 2 * TB * C_QK].rearrange("p (b t n) -> p b t n", b=2, t=TB)
        hf = h[:, :, :].rearrange("p t n -> p (t n)")
        gsf = gs[:, :, :].rearrange("p t n -> p (t n)")
        acf = act_t[:, :, :].rearrange("p t n -> p (t n)")
        qkT = hf[:, 0:1024].rearrange("p (b n) -> p b n", b=2)
        sc = hf[:, 1024:1024 + 2 * LANES].rearrange("p (b n) -> p b n", b=2)
        pn = gsf[:, 0:2 * LANES].rearrange("p (b n) -> p b n", b=2)
        pT = y[:, 0:2 * LANES].rearrange("p (b n) -> p b n", b=2)
        bias = acf[:, 0:2 * LANES].rearrange("p (b n) -> p b n", b=2)
        kr_t = acf[:, 0:2 * C_ROPE].rearrange("p (m n) -> p m n", m=4)
        braw = [(acf[:, 768:896], y[:, 768:1024]), (acf[:, 896:1024], gsf[:, 768:1024])]
        lat = y[:, 0:TB * Q_LORA].rearrange("p (t n) -> p t n", t=TB)
        lkv = gsf[:, 0:TB * (KV_LORA + C_ROPE)].rearrange("p (t n) -> p t n", t=TB)

        bank = [ctx.enter_context(nc.psum_tensor(f"bank{i}", [P, NW], F32)) for i in range(8)]

        arrived = [sem(f"arrived{i}") for i in range(RING)]
        hi_ready = sem("hi_ready")
        lo_ready = sem("lo_ready")
        quarter_used = sem("quarter_used")
        x_loaded = sem("x_loaded")
        consts_loaded = sem("consts_loaded")
        rows_cleared = sem("rows_cleared")
        rows_loaded = sem("rows_loaded")
        gains_loaded = sem("gains_loaded")
        ones_set = sem("ones_set")
        gains_turned = sem("gains_turned")
        gain_cols_ready = sem("gain_cols_ready")
        act_step = sem("act_step")
        dve_step = sem("dve_step")
        pool_step = sem("pool_step")
        norm_sqrt = sem("norm_sqrt")
        rinv_ready = sem("rinv_ready")
        h_ready_dve = sem("h_ready_dve")
        h_ready_act = sem("h_ready_act")
        hT_turned = sem("hT_turned")
        hT_hi_ready = sem("hT_hi_ready")
        hT_lo_ready = sem("hT_lo_ready")
        copied_act = sem("copied_act")
        copied_dve = sem("copied_dve")
        x_added = sem("x_added")
        squared = sem("squared")
        head_ss = sem("head_ss")
        head_sqrt = sem("head_sqrt")
        head_rinv = sem("head_rinv")
        normed_dve = sem("normed_dve")
        normed_pool = sem("normed_pool")
        braw_loaded = [sem("braw_loaded0"), sem("braw_loaded1")]
        bias_ready = sem("bias_ready")
        k_ready = sem("k_ready")
        qk_turned = sem("qk_turned")
        qT_ready = sem("qT_ready")
        kT_ready = sem("kT_ready")
        scored = sem("scored")
        max_ready = sem("max_ready")
        exp_ready = sem("exp_ready")
        den_ready = sem("den_ready")
        p_ready = sem("p_ready")
        p_turned = sem("p_turned")
        pT_ready = sem("pT_ready")
        pv_done = sem("pv_done")
        o_hi = sem("o_hi")
        o_lo = sem("o_lo")
        silu_ready = sem("silu_ready")
        hidden_ready = sem("hidden_ready")
        hidden_turned = sem("hidden_turned")
        aT_hi_ready = sem("aT_hi_ready")
        aT_lo_ready = sem("aT_lo_ready")
        lat_ss = sem("lat_ss")
        lat_rinv = sem("lat_rinv")
        lat_ready = sem("lat_ready")
        lat_turned = sem("lat_turned")
        lat_hi = sem("lat_hi")
        lat_lo = sem("lat_lo")
        stored = sem("stored")

        lin = []
        na = nd = 0
        for s in ("in", "out", "dq", "dkv", "uq", "ukv", "o"):
            for j, n in enumerate(stage_pieces(s)):
                add = s in ("out", "o")
                na, nd = na + (not add), nd + (not add)
                lin.append(dict(stage=s, piece=n, j=j, n=pieces[n]["n"], add=add, na=na, nd=nd))
        dest = {"in": lambda t, j, n: proj[:, t, j * NW:j * NW + n], "dq": lambda t, j, n: lat[:, t, :],
                "dkv": lambda t, j, n: lkv[:, t, :], "uq": lambda t, j, n: qc[:, t, j * NW:j * NW + n],
                "ukv": lambda t, j, n: kv[:, t, j * NW:j * NW + n]}
        stage_lin = lambda s: [(i, c) for i, c in enumerate(lin) if c["stage"] == s]

        def sources(g):
            if g < A_HEADS:
                kvh = g // (A_HEADS // A_KV)
                return (lambda t: proj[:, t, A_Q + g * HD:A_Q + (g + 1) * HD],
                        lambda t: proj[:, t, A_K + kvh * HD:A_K + (kvh + 1) * HD],
                        lambda t: proj[:, t, A_V + kvh * HD:A_V + (kvh + 1) * HD], HD)
            if g < HEADS0:
                b = g - A_HEADS
                return (lambda t: proj[:, t, B_Q + b * HD:B_Q + (b + 1) * HD],
                        lambda t: proj[:, t, B_K + b * HD:B_K + (b + 1) * HD],
                        lambda t: proj[:, t, B_V + b * HD:B_V + (b + 1) * HD], HD)
            c = g - HEADS0
            return (lambda t: qc[:, t, c * C_QK:(c + 1) * C_QK],
                    lambda t: kbuf[:, g % 2, t, :],
                    lambda t: kv[:, t, c * 128 + C_NOPE:(c + 1) * 128], C_QK)

        def o_place(dst, g):
            m = g % HEADS0
            r = 64 * (m % 2)
            return dst[r:r + 64, m // 2, :]

        def o_psum(g):
            r = 64 * (g % 2)
            return bank[6 + g % 2][r:r + 64, 0:SEQ]

        if last >= 4:
            route = sb("route", [P, 16, TB * N_EXP])
            pos_t = sb("pos_t", [P, TB, SLOTS])
            gate_t = sb("gate_t", [P, TB, SLOTS])
            cnt = sb("cnt", [P, 4, N_EXP])
            ids_f = sb("ids_f", [P, 4])
            ids = sb("ids", [1, 4], I32)
            cur = sb("cur", [P, 2, TB])
            oh = act_t
            wT = act_t[:, :, 2 * CAP:2 * CAP + P]
            router = y[:, 0:KD * N_EXP]
            logits_done = sem("logits_done")
            mask_ready = sem("mask_ready")
            counted = sem("counted")
            route_ready = sem("route_ready")
            gain_row_loaded = sem("gain_row_loaded")
            cur_ready = sem("cur_ready")
            slot_ready = sem("slot_ready")
            gathered = sem("gathered")
            weight_turned = sem("weight_turned")
            e_hi = sem("e_hi")
            e_lo = sem("e_lo")
            wT_ready = sem("wT_ready")
            y_done = sem("y_done")
            y_act = sem("y_act")
            y_dve = sem("y_dve")
            combined = sem("combined")
            e_silu = sem("e_silu")
            e_hidden = sem("e_hidden")
            e_gate = sem("e_gate")
            e_up = sem("e_up")
            e_turned = sem("e_turned")
            e_aT_hi = sem("e_aT_hi")
            e_aT_lo = sem("e_aT_lo")
            e_added = sem("e_added")
            e_once = sem("e_once")

        X_ADDS = {0: 0, 1: 4, 2: 8, 3: 12}

        block = ctx.enter_context(nc.Block())

        @block.sync
        def _(sp):
            sp.dma_start(xres[:, :, :], x_in[0].rearrange("(t p) d -> p t d", p=P)).then_inc(x_loaded, 16)
            for n, p in enumerate(pieces):
                before = [m for m in range(n) if pieces[m]["place"] == p["place"]]
                if before:
                    sp.wait_ge(lo_ready, pieces[before[-1]]["q1"])
                if p["stage"] == "ffn" and p["place"] >= 5 and all(pieces[m]["stage"] != "ffn" for m in before):
                    sp.wait_ge(pv_done, HEADS0)
                dst = ring[:, p["place"], 0:p["nk"] * p["n"]].rearrange("p (k n) -> p k n", k=p["nk"])
                sp.dma_start(dst, p["src"]).then_inc(arrived[p["place"]], 16)
            if last >= 4:
                def load(e, i, kind, c):
                    if kind == "down":
                        src = a["od_e_down"][0, bass.ds(e, 1), c * NW:(c + 1) * NW, :].rearrange(
                            "o (k p) n -> p (o k) n", p=P)
                    else:
                        src = a["od_e_" + kind][0, bass.ds(e, 1), :, c * NW:(c + 1) * NW].rearrange(
                            "o (k p) n -> p (o k) n", p=P)
                    dst = ring[:, i % RING, :].rearrange("p (k n) -> p k n", k=src.shape[1])
                    sp.dma_start(dst, src).then_inc(arrived[i % RING], 16)

                for i, (kind, c) in enumerate(order):
                    if i < RING:
                        before = [m for m in range(len(pieces)) if pieces[m]["place"] == i]
                        sp.wait_ge(lo_ready, pieces[before[-1]]["q1"])
                        if i == 5:
                            sp.wait_ge(pv_done, HEADS)
                    else:
                        sp.wait_ge(lo_ready, NQ + 4 * (i - RING + 1))
                    load(0, i, kind, c)
                with sp.Fori(1, N_EXP) as e:
                    for i, (kind, c) in enumerate(order):
                        sp.wait_ge(lo_ready, e * EQ + (NQ + 4 * (i - RING + 1)))
                        load(e, i, kind, c)
                sp.wait_ge(route_ready, 1)
                over = sp.value_load(ids[0:1, 3:4], min_val=0, max_val=OVER)
                with sp.If(over > 0):
                    with sp.Fori(0, over) as o:
                        e = sp.value_load(ids[0:1, bass.ds(o, 1)], min_val=0, max_val=N_EXP - 1)
                        for i, (kind, c) in enumerate(order):
                            sp.wait_ge(lo_ready, o * EQ + (N_EXP * EQ + NQ + 4 * (i - RING + 1)))
                            load(e, i, kind, c)
                sp.wait_ge(e_added, over * 4 + 4 * N_EXP)
            else:
                sp.wait_ge(x_added, 4 * last)
            sp.dma_start(out[0].rearrange("(t p) d -> p t d", p=P), xres[:, :, :]).then_inc(stored, 16)
            sp.wait_ge(stored, 16)

        def experts_pe(pe, three):
            pe.wait_ge(h_ready_dve, 4)
            for b in range(4):
                for kk in range(2):
                    for t in range(TB):
                        k = 2 * b + kk
                        at = kk * SEQ + t * P
                        mm = pe.transpose(bank[b][:, at:at + P], h[:, t, k * P:(k + 1) * P], ident)
                mm.then_inc(hT_turned, 1)
            pe.wait_ge(hT_lo_ready, 4 * KD)
            for t in range(TB):
                for k in range(KD):
                    cols = slice(t * P, (t + 1) * P)
                    mm = three(bank[4][:, t * N_EXP:(t + 1) * N_EXP], hT_hi[:, k, cols], hT_lo[:, k, cols],
                               aT_hi[:, 0, k * N_EXP:(k + 1) * N_EXP], aT_lo[:, 0, k * N_EXP:(k + 1) * N_EXP],
                               k == 0, k == KD - 1)
            mm.then_inc(logits_done, 1)
            pe.wait_ge(mask_ready, 1)
            mask = lambda t: route[:, 0, t * N_EXP:(t + 1) * N_EXP]
            tri = cst[:, C_TRI:C_TRI + P]
            pe.matmul(bank[5][:, 0:8], tri, mask(0), start=True, stop=True)
            pe.matmul(bank[5][:, 8:16], ones[:, :], mask(0), start=True, stop=False)
            pe.matmul(bank[5][:, 8:16], tri, mask(1), start=False, stop=True)
            pe.matmul(bank[5][:, 16:24], ones[:, :], mask(0), start=True, stop=False)
            pe.matmul(bank[5][:, 16:24], ones[:, :], mask(1), start=False, stop=True).then_inc(counted, 1)

            pe.wait_ge(route_ready, 1)
            over = pe.value_load(ids[0:1, 3:4], min_val=0, max_val=OVER)
            slots = over + N_EXP
            with pe.Fori(0, slots) as s:
                pe.wait_ge(slot_ready, s + 1)
                for k in range(KD):
                    for t in range(TB):
                        mm = pe.matmul(bank[6 + k // 4][:, (k % 4) * P:(k % 4 + 1) * P],
                                       h[:, t, k * P:(k + 1) * P], oh[:, t, 0:CAP],
                                       start=(t == 0), stop=(t == 1))
                    if k % 4 == 3:
                        mm.then_inc(gathered, 1)
                for t in range(TB):
                    mm = pe.transpose(bank[2][:, t * P:(t + 1) * P], oh[:, t, CAP:2 * CAP], ident)
                mm.then_inc(weight_turned, 1)
                pe.wait_ge(e_lo, s * 2 + 2)

                def turn(c):
                    pe.wait_ge(e_hidden, s * NCH + (c + 1))
                    for b in range(4):
                        mm = pe.transpose(bank[6 + c % 2][:, b * P:(b + 1) * P],
                                          y[:, (c % 2) * NW + b * P:(c % 2) * NW + (b + 1) * P], ident)
                    mm.then_inc(e_turned, 1)

                for i, (kind, c) in enumerate(order):
                    if kind == "gate" and c == 1:
                        pe.wait_ge(wT_ready, s + 1)
                    if kind == "down":
                        if c == NCH - 1:
                            turn(c)
                        pe.wait_ge(e_aT_lo, s * NCH + (c + 1))
                    for j in range(4):
                        q = 4 * i + j
                        place = (NQ + q) % SPLITS
                        pe.wait_ge(lo_ready, s * EQ + (NQ + q + 1))
                        for m in range(2):
                            at = m * NW
                            wh, wl = w_hi[:, place, at:at + NW], w_lo[:, place, at:at + NW]
                            if kind == "down":
                                mm = three(bank[4 + m][:, :], aT_hi[:, j, 0:CAP], aT_lo[:, j, 0:CAP], wh, wl,
                                           c == 0 and j == 0, c == NCH - 1 and j == 3)
                            else:
                                k = 2 * j + m
                                b = 2 * (c % 2) + (kind == "up")
                                mm = three(bank[b][:, :], hT_hi[:, k, 0:CAP], hT_lo[:, k, 0:CAP], wh, wl,
                                           k == 0, k == KD - 1)
                        mm.then_inc(quarter_used, 1)
                    if kind == "up" and c == 0 or kind == "down" and c < NCH - 2:
                        turn(c if kind == "up" else c + 1)
                pe.wait_ge(y_act, s + 1)
                pe.wait_ge(y_dve, s + 1)
                for t in range(TB):
                    for half in range(2):
                        pe.matmul(bank[2 * t + half][:, :], wT[:, t, :],
                                  y[:, half * NW:(half + 1) * NW], start=True, stop=True).then_inc(combined, 1)

        @block.tensor
        def _(pe):
            def three(dst, hi, lo, whi, wlo, first, final):
                pe.matmul(dst, hi, whi, start=first, stop=False)
                pe.matmul(dst, lo, whi, start=False, stop=False)
                return pe.matmul(dst, hi, wlo, start=False, stop=final)

            def product(q, dst, s_hi, s_lo):
                n, k0, kn = quarters[q]
                p = pieces[n]
                pe.wait_ge(lo_ready, q + 1)
                for k in range(k0, k0 + kn):
                    for t in range(TB):
                        for o in range(0, p["n"], NW):
                            m = min(NW, p["n"] - o)
                            at = (k - k0) * p["n"] + o
                            mm = three(dst(t, o // NW)[:, 0:m], s_hi(k, t), s_lo(k, t),
                                       w_hi[:, q % SPLITS, at:at + m], w_lo[:, q % SPLITS, at:at + m],
                                       *flags(p, k))
                mm.then_inc(quarter_used, 1)
                return mm

            def flags(p, k):
                if p["kind"] != "down":
                    return k == 0, k == p["nk"] - 1
                lastc = max(x["c"] for x in pieces if x["kind"] == "down")
                return k == 0 and p["c"] == 0, k == p["nk"] - 1 and p["c"] == lastc

            def sT(buf):
                return lambda k, t: buf[:, k, t * P:(t + 1) * P]

            def turn_norm(n):
                pe.wait_ge(h_ready_dve, n + 1)
                pe.wait_ge(h_ready_act, n + 1)
                for b in range(4):
                    for kk in range(2):
                        for t in range(TB):
                            k = 2 * b + kk
                            at = kk * SEQ + t * P
                            mm = pe.transpose(bank[b][:, at:at + P], h[:, t, k * P:(k + 1) * P], ident)
                    mm.then_inc(hT_turned, 1)

            def projection(stage, s_hi, s_lo):
                for i, c in stage_lin(stage):
                    if i >= 2:
                        prev = lin[i - 2]
                        pe.wait_ge(copied_act, prev["na"])
                        pe.wait_ge(copied_dve, prev["nd"])
                    p = pieces[c["piece"]]
                    for q in range(p["q0"], p["q1"]):
                        product(q, lambda t, half: bank[4 + 2 * (i % 2) + t], s_hi, s_lo)

            def attention(g0, g1):
                for i in range(g0, g1 + 3):
                    if i < g1:
                        qs, ks, _, w = sources(i)
                        if i >= HEADS0:
                            pe.wait_ge(k_ready, i - HEADS0 + 1)
                        for j, src in enumerate((qs(0), qs(1), ks(0), ks(1))):
                            mm = pe.transpose(bank[i % 2][0:w, j * P:(j + 1) * P], src, ident)
                        mm.then_inc(qk_turned, 1)
                    j = i - 1
                    if g0 <= j < g1:
                        w = sources(j)[3]
                        pe.wait_ge(qT_ready, j + 1)
                        pe.wait_ge(kT_ready, j + 1)
                        s = bank[2 + j % 2]
                        buf = qkT[0:w, j % 2, :]
                        pe.matmul(s[:, 0:P], buf[:, 0:P], buf[:, SEQ:SEQ + P], start=True, stop=True)
                        pe.matmul(s[:, P:LANES], buf[:, P:SEQ], buf[:, SEQ:2 * SEQ], start=True, stop=True)\
                          .then_inc(scored, 1)
                    j = i - 2
                    if g0 <= j < g1:
                        pe.wait_ge(p_ready, j + 1)
                        for m in range(3):
                            mm = pe.transpose(bank[4 + j % 2][:, [0, P, 2 * P][m]:[0, P, 2 * P][m] + P],
                                              pn[:, j % 2, m * P:(m + 1) * P], ident)
                        mm.then_inc(p_turned, 1)
                    j = i - 3
                    if g0 <= j < g1:
                        vs = sources(j)[2]
                        pe.wait_ge(pT_ready, j + 1)
                        if j >= 2:
                            pe.wait_ge(o_lo, j - 1)
                        o = o_psum(j)
                        pe.matmul(o, vs(0), pT[:, j % 2, 0:SEQ], start=True, stop=False)
                        pe.matmul(o[:, P:SEQ], vs(1), pT[:, j % 2, SEQ:LANES], start=False, stop=True)\
                          .then_inc(pv_done, 1)

            def ffn():
                chunks = max(pieces[n]["c"] for n in stage_pieces("ffn")) + 1
                width = [min(NW, D_FF - c * NW) for c in range(chunks)]

                def turn(c):
                    pe.wait_ge(hidden_ready, c + 1)
                    for b in range(width[c] // P):
                        for t in range(TB):
                            at = (b % 2) * SEQ + t * P
                            mm = pe.transpose(bank[2 * (c % 2) + b // 2][:, at:at + P],
                                              act_t[:, t, b * P:(b + 1) * P], ident)
                    mm.then_inc(hidden_turned, 1)

                for n in stage_pieces("ffn"):
                    p = pieces[n]
                    c = p["c"]
                    if p["kind"] == "gate" and c >= 1:
                        pe.wait_ge(hidden_ready, c)
                    if p["kind"] == "up" and c >= 1:
                        pe.wait_ge(aT_lo_ready, c)
                    if p["kind"] == "down":
                        if c == chunks - 1:
                            turn(c)
                        pe.wait_ge(aT_lo_ready, c + 1)
                    base = {"gate": 2 * (c % 2), "up": 2 - 2 * (c % 2), "down": 4}[p["kind"]]
                    for q in range(p["q0"], p["q1"]):
                        if p["kind"] == "down":
                            product(q, lambda t, half: bank[4 + 2 * t + half], sT(aT_hi), sT(aT_lo))
                        else:
                            product(q, lambda t, half: bank[base + t], sT(hT_hi), sT(hT_lo))
                    if p["kind"] == "up" and c == 0 or p["kind"] == "down" and c < chunks - 2:
                        turn(c if p["kind"] == "up" else c + 1)

            pe.wait_ge(consts_loaded, 16)
            pe.wait_ge(gains_loaded, 16 * 9)
            pe.transpose(bank[7][:, 0:33], g_rows[:, :], ident[0:33, 0:33]).then_inc(gains_turned, 1)

            turn_norm(0)
            pe.wait_ge(hT_lo_ready, KD)
            projection("in", sT(hT_hi), sT(hT_lo))
            pe.wait_ge(normed_dve, 1)
            pe.wait_ge(normed_pool, 1)
            attention(0, HEADS0)
            pe.wait_ge(o_lo, HEADS0)
            projection("out", sT(hT_hi), sT(hT_lo))
            if last >= 2:
                turn_norm(1)
                pe.wait_ge(hT_lo_ready, 2 * KD)
                ffn()
            if last >= 3:
                turn_norm(2)
                pe.wait_ge(hT_lo_ready, 3 * KD)
                projection("dq", sT(hT_hi), sT(hT_lo))
                projection("dkv", sT(hT_hi), sT(hT_lo))
                pe.wait_ge(lat_ready, 1)
                for k in range(5):
                    for t in range(TB):
                        src = lat[:, t, k * P:(k + 1) * P] if k < 3 else lkv[:, t, (k - 3) * P:(k - 2) * P]
                        mm = pe.transpose(bank[k // 2][:, (k % 2) * SEQ + t * P:(k % 2) * SEQ + (t + 1) * P],
                                          src, ident)
                mm.then_inc(lat_turned, 1)
                pe.wait_ge(lat_lo, 5)
                projection("uq", sT(aT_hi), sT(aT_lo))
                projection("ukv", lambda k, t: aT_hi[:, 3 + k, t * P:(t + 1) * P],
                           lambda k, t: aT_lo[:, 3 + k, t * P:(t + 1) * P])
                pe.wait_ge(normed_dve, 2)
                attention(HEADS0, HEADS)
                pe.wait_ge(o_lo, HEADS)
                projection("o", sT(hT_hi), sT(hT_lo))
            if last >= 4:
                experts_pe(pe, three)

        def experts_act(act, norm):
            act.wait_ge(gain_row_loaded, 32)
            act.activation(aT_hi[:, 0, 0:KD * N_EXP], router, ACT.Copy)\
               .then_inc(e_once, 1)
            norm(3)
            act.wait_ge(mask_ready, 1)
            act.activation(route[:, 13, 0:TB], route[:, 12, 0:TB], ACT.Exp).then_inc(e_once, 1)
            act.wait_ge(route_ready, 1)
            over = act.value_load(ids[0:1, 3:4], min_val=0, max_val=OVER)
            slots = over + N_EXP
            with act.Fori(0, slots) as s:
                def split(q):
                    i, j = q // 4, q % 4
                    if j == 0:
                        turn = i // RING + 1
                        act.wait_ge(arrived[i % RING], s * (16 * len(order) // RING) + 16 * (uses[i % RING] + turn))
                    act.wait_ge(quarter_used, s * EQ + (NQ + q - SPLITS + 1))
                    act.activation(w_hi[:, (NQ + q) % SPLITS, :], ring[:, i % RING, j * QUARTER:(j + 1) * QUARTER],
                                   ACT.Copy).then_inc(hi_ready, 1)

                def turned(c):
                    act.wait_ge(e_turned, s * NCH + (c + 1))
                    act.activation(aT_hi[:, 0:4, 0:CAP], bank[6 + c % 2][:, :].rearrange("p (a n) -> p a n", a=4),
                                   ACT.Copy).then_inc(e_aT_hi, 1)

                for q in range(LEAD - 1):
                    split(q)
                for m in range(2):
                    act.wait_ge(gathered, s * 2 + (m + 1))
                    act.activation(hT_hi[:, 4 * m:4 * m + 4, 0:CAP],
                                   bank[6 + m][:, :].rearrange("p (a n) -> p a n", a=4), ACT.Copy)\
                       .then_inc(e_hi, 1)
                for i, (kind, c) in enumerate(order):
                    if kind == "down" and c == NCH - 1:
                        turned(c)
                    for j in range(4):
                        q = 4 * i + j + LEAD - 1
                        if q < EQ:
                            split(q)
                    if kind == "gate":
                        act.wait_ge(quarter_used, s * EQ + (NQ + 4 * (i + 1)))
                        act.activation(gsf[:, (c % 2) * NW:(c % 2 + 1) * NW], bank[2 * (c % 2)][:, :], ACT.Silu)\
                           .then_inc(e_silu, 1)
                    if kind == "up" and c == 0 or kind == "down" and c < NCH - 2:
                        turned(c if kind == "up" else c + 1)
                act.wait_ge(quarter_used, s * EQ + (NQ + EQ))
                act.activation(y[:, 0:NW], bank[4][:, :], ACT.Copy).then_inc(y_act, 1)

        @block.scalar
        def _(act):
            step = [0]

            def link(ins):
                step[0] += 1
                ins.then_inc(act_step, 1)
                act.wait_ge(act_step, step[0])

            split = [0]

            def split_to(q1):
                while split[0] < min(q1, NQ):
                    q = split[0]
                    n, k0, kn = quarters[q]
                    p = pieces[n]
                    if k0 == 0:
                        act.wait_ge(arrived[p["place"]], 16 * (p["turn"] + 1))
                    if q >= SPLITS:
                        act.wait_ge(quarter_used, q - SPLITS + 1)
                    m = kn * p["n"]
                    at = k0 * p["n"]
                    act.activation(w_hi[:, q % SPLITS, 0:m], ring[:, p["place"], at:at + m], ACT.Copy)\
                       .then_inc(hi_ready, 1)
                    split[0] += 1

            def norm(n):
                if n == 0:
                    act.wait_ge(x_loaded, 16)
                    act.wait_ge(ones_set, 1)
                else:
                    act.wait_ge(x_added, X_ADDS[n])
                for t in range(TB):
                    last_ = act.activation(h[:, t, :], xres[:, t, :], ACT.Square, accum_out=ss[:, t:t + 1])
                link(last_)
                act.activation(rt[:, 0:TB], ss[:, 0:TB], ACT.Sqrt, bias=eps[:, 0:1], scale=1.0 / D)\
                   .then_inc(norm_sqrt, 1)
                if n < 3:
                    act.wait_ge(rinv_ready, n + 1)
                    act.activation(h[:, 1, :], xres[:, 1, :], ACT.Copy, scale=rinv[:, 1:2])\
                       .then_inc(h_ready_act, 1)
                    if n == 0:
                        act.wait_ge(gain_cols_ready, 1)
                for k in range(KD):
                    if k % 2 == 0:
                        act.wait_ge(hT_turned, 4 * n + k // 2 + 1)
                    src = bank[k // 2][:, (k % 2) * SEQ:(k % 2 + 1) * SEQ]
                    gain = 1.0 if n == 3 else g_cols[:, g_fwd[n] + k:g_fwd[n] + k + 1]
                    act.activation(hT_hi[:, k, :], src, ACT.Copy, scale=gain).then_inc(hT_hi_ready, 1)

            def projection(stage):
                for i, c in stage_lin(stage):
                    p = pieces[c["piece"]]
                    for q in range(p["q0"], p["q1"]):
                        split_to(q + LEAD)
                    if not c["add"]:
                        act.wait_ge(quarter_used, p["q1"])
                        act.activation(dest[stage](0, c["j"], c["n"]), bank[4 + 2 * (i % 2)][:, 0:c["n"]],
                                       ACT.Copy).then_inc(copied_act, 1)

            def attention(g0, g1):
                act.wait_ge(rows_loaded, 48)
                for i in range(g0, g1 + 3):
                    if i < g1:
                        w = sources(i)[3]
                        act.wait_ge(qk_turned, i + 1)
                        gain = 1.0
                        if i < HEADS0:
                            col = G_AQ if i < A_HEADS else G_BQ
                            gain = g_cols[0:w, col:col + 1]
                        act.activation(qkT[0:w, i % 2, 0:SEQ], bank[i % 2][0:w, 0:SEQ], ACT.Copy, scale=gain)\
                           .then_inc(qT_ready, 1)
                    j = i - 2
                    if g0 <= j < g1:
                        act.wait_ge(p_turned, j + 1)
                        act.activation(pT[:, j % 2, :], bank[4 + j % 2][:, 0:LANES], ACT.Copy)\
                           .then_inc(pT_ready, 1)
                    j = i - 3
                    if g0 <= j < g1:
                        act.wait_ge(pv_done, j + 1)
                        act.activation(o_place(hT_hi, j), o_psum(j), ACT.Copy).then_inc(o_hi, 1)
                    j = i - 1
                    if g0 <= j < g1:
                        act.wait_ge(max_ready, j + 1)
                        b = j % 2
                        act.activation(sc[:, b, 0:P], sc[:, b, 0:P], ACT.Exp, bias=nmax[:, b, 0:1],
                                       accum_out=esum[:, b, 0:1])
                        e = act.activation(sc[:, b, P:LANES], sc[:, b, P:LANES], ACT.Exp, bias=nmax[:, b, 1:2],
                                           accum_out=esum[:, b, 1:2])
                        if j < A_HEADS:
                            e = act.activation(esum[:, b, 2:4], nmax[:, b, 0:2], ACT.Exp,
                                               bias=sinks[:, j:j + 1])
                        e.then_inc(exp_ready, 1)

            def ffn():
                for n in stage_pieces("ffn"):
                    p = pieces[n]
                    c = p["c"]
                    if p["kind"] == "down" and p["q1"] == pieces[stage_pieces("ffn")[-1]]["q1"]:
                        turned(c)
                    for q in range(p["q0"], p["q1"]):
                        split_to(q + LEAD)
                    if p["kind"] == "gate":
                        act.wait_ge(quarter_used, p["q1"])
                        for t in range(TB):
                            s = act.activation(gs[:, t, 0:p["n"]], bank[2 * (c % 2) + t][:, 0:p["n"]], ACT.Silu)
                        s.then_inc(silu_ready, 1)
                    if p["kind"] == "up" and c == 0 or p["kind"] == "down" and c < ffn_chunks - 2:
                        turned(c if p["kind"] == "up" else c + 1)

            ffn_chunks = (D_FF + NW - 1) // NW

            def turned(c):
                act.wait_ge(hidden_turned, c + 1)
                for m in range(min(NW, D_FF - c * NW) // (2 * P)):
                    o = act.activation(aT_hi[:, 2 * m:2 * m + 2, :].rearrange("p a n -> p (a n)"),
                                       bank[2 * (c % 2) + m][:, :], ACT.Copy)
                o.then_inc(aT_hi_ready, 1)

            norm(0)
            projection("in")
            act.wait_ge(copied_dve, lin[stage_lin("in")[-1][0]]["nd"])
            act.wait_ge(copied_act, lin[stage_lin("in")[-1][0]]["na"])
            for t in range(TB):
                j0, j1 = (hf[:, 0:640], hf[:, 640:1664]) if t == 0 else (gsf[:, 0:640], y[:, 0:1024])
                act.activation(j0, proj[:, t, 0:A_V], ACT.Square).then_inc(squared, 1)
                act.activation(j1, proj[:, t, B_Q:B_V], ACT.Square).then_inc(squared, 1)
            act.wait_ge(head_ss, 1)
            act.activation(rt[:, 0:52], ss[:, 0:52], ACT.Sqrt, bias=eps[:, 0:1], scale=1.0 / HD)\
               .then_inc(head_sqrt, 1)
            attention(0, HEADS0)
            projection("out")
            if last >= 2:
                norm(1)
                ffn()
            if last >= 3:
                norm(2)
                projection("dq")
                projection("dkv")
                act.wait_ge(copied_dve, lin[stage_lin("dkv")[-1][0]]["nd"])
                act.wait_ge(copied_act, lin[stage_lin("dkv")[-1][0]]["na"])
                for t in range(TB):
                    act.activation(hf[:, 0:Q_LORA], lat[:, t, :], ACT.Square, accum_out=ss[:, 2 + t:3 + t])
                    link(act.activation(hf[:, 384:384 + KV_LORA], lkv[:, t, 0:KV_LORA], ACT.Square,
                                        accum_out=ss[:, 4 + t:5 + t]))
                    link(act.activation(hf[:, 0:C_ROPE], lkv[:, t, KV_LORA:], ACT.Square,
                                        accum_out=ss[:, 64 + t:65 + t]))
                act.activation(rt[:, 2:4], ss[:, 2:4], ACT.Sqrt, bias=eps[:, 0:1], scale=1.0 / Q_LORA)
                act.activation(rt[:, 4:6], ss[:, 4:6], ACT.Sqrt, bias=eps[:, 0:1], scale=1.0 / KV_LORA)\
                   .then_inc(lat_ss, 1)
                act.wait_ge(lat_turned, 1)
                for k in range(5):
                    col = G_QA + k
                    act.activation(aT_hi[:, k, :], bank[k // 2][:, (k % 2) * SEQ:(k % 2 + 1) * SEQ], ACT.Copy,
                                   scale=g_cols[:, col:col + 1]).then_inc(lat_hi, 1)
                projection("uq")
                projection("ukv")
                act.wait_ge(copied_dve, lin[stage_lin("ukv")[-1][0]]["nd"])
                act.wait_ge(copied_act, lin[stage_lin("ukv")[-1][0]]["na"])
                act.wait_ge(lat_lo, 5)
                for t in range(TB):
                    if t:
                        act.wait_ge(head_ss, 2)
                    act.activation(hf[:, 0:1536], qc[:, t, :], ACT.Square).then_inc(squared, 1)
                    nope = kv[:, t, :].rearrange("p (h n) -> p h n", h=C_HEADS)[:, :, 0:C_NOPE]
                    act.activation(acf[:, 0:1024].rearrange("p (h n) -> p h n", h=C_HEADS), nope, ACT.Square)\
                       .then_inc(squared, 1)
                act.wait_ge(head_ss, 3)
                act.activation(rt[:, 0:64], ss[:, 0:64], ACT.Sqrt, bias=eps[:, 0:1], scale=1.0 / C_QK)\
                   .then_inc(head_sqrt, 1)
                attention(HEADS0, HEADS)
                projection("o")
            if last >= 4:
                experts_act(act, norm)

        def experts_dve(dve, norm, link):
            R = lambda i: route[:, i, :].rearrange("p (t e) -> p t e", e=N_EXP)
            dve.wait_ge(e_once, 1)
            dve.tensor_tensor(aT_lo[:, 0, 0:KD * N_EXP], router, aT_hi[:, 0, 0:KD * N_EXP].bitcast(F32), ALU.subtract)
            norm(3)
            dve.wait_ge(logits_done, 1)
            link(dve.tensor_copy(route[:, 1, :], bank[4][:, 0:TB * N_EXP]))
            below = cst[:, C_IOTA:C_IOTA + N_EXP].unsqueeze(1).to_broadcast([P, TB, N_EXP])
            link(dve.tensor_scalar(R(14), below, -float(N_EXP), None, ALU.add))
            wide = lambda v: v.unsqueeze(2).to_broadcast([P, TB, N_EXP])
            for n, (src, hot, top) in enumerate(((1, 2, 10), (3, 4, 11))):
                m = route[:, top, 0:TB]
                first = route[:, top, TB:2 * TB]
                link(dve.tensor_reduce(m, R(src), AX.X, ALU.max))
                link(dve.tensor_tensor(R(5), R(src), wide(m), ALU.is_equal))
                link(dve.tensor_tensor(R(5), R(5), R(14), ALU.mult))
                link(dve.tensor_reduce(first, R(5), AX.X, ALU.min))
                link(dve.tensor_tensor(R(hot), R(14), wide(first), ALU.is_equal))
                if n == 0:
                    link(dve.scalar_tensor_tensor(R(3), R(2), -3e38, R(1), ALU.mult, ALU.add))
            dve.tensor_tensor(R(0), R(2), R(4), ALU.add)
            dve.tensor_tensor(route[:, 12, 0:TB], route[:, 11, 0:TB], route[:, 10, 0:TB], ALU.subtract)\
               .then_inc(mask_ready, 1)
            dve.wait_ge(e_once, 2)
            w1, w2 = route[:, 15, 0:TB], route[:, 15, TB:2 * TB]
            link(dve.tensor_scalar(w1, route[:, 13, 0:TB], 1.0, None, ALU.add))
            link(dve.reciprocal(w1, w1))
            link(dve.tensor_tensor(w2, route[:, 13, 0:TB], w1, ALU.mult))
            dve.tensor_tensor(R(6), R(2), wide(w1), ALU.mult)
            link(dve.tensor_tensor(R(7), R(4), wide(w2), ALU.mult))
            link(dve.tensor_tensor(R(6), R(6), R(7), ALU.add))
            dve.wait_ge(counted, 1)
            link(dve.tensor_tensor(R(8), bank[5][:, 0:TB * N_EXP].rearrange("p (t e) -> p t e", e=N_EXP), R(0),
                                   ALU.mult))
            link(dve.tensor_tensor(R(8), R(8), R(0), ALU.add))
            link(dve.tensor_scalar(R(8), R(8), -1.0, None, ALU.add))
            link(dve.tensor_copy(cnt[:, 0, :], bank[5][:, 16:24]))
            link(dve.tensor_scalar(cnt[:, 1, :], cnt[:, 0, :], float(CAP) + 0.5, None, ALU.is_gt))
            link(dve.memset(cnt[:, 2, :], 0.0))
            for e in range(1, N_EXP):
                link(dve.tensor_tensor(cnt[:, 2, e:e + 1], cnt[:, 2, e - 1:e], cnt[:, 1, e - 1:e], ALU.add))
            dve.tensor_copy(pos_t[:, :, 0:N_EXP], R(8))
            dve.tensor_copy(gate_t[:, :, 0:N_EXP], R(6))
            for o in range(OVER):
                link(dve.tensor_scalar(cnt[:, 3, :], cnt[:, 2, :], float(o), None, ALU.is_equal))
                link(dve.tensor_tensor(cnt[:, 3, :], cnt[:, 3, :], cnt[:, 1, :], ALU.mult))
                pick = cnt[:, 3, :].unsqueeze(1).to_broadcast([P, TB, N_EXP])
                link(dve.scalar_tensor_tensor(R(9), R(8), 1.0 - CAP, pick, ALU.add, ALU.mult))
                link(dve.tensor_reduce(pos_t[:, :, N_EXP + o], R(9), AX.X, ALU.add))
                link(dve.tensor_scalar(pos_t[:, :, N_EXP + o], pos_t[:, :, N_EXP + o],
                                       -1.0, None, ALU.add))
                link(dve.tensor_tensor(R(9), R(6), pick, ALU.mult))
                link(dve.tensor_reduce(gate_t[:, :, N_EXP + o], R(9), AX.X, ALU.add))
                link(dve.tensor_tensor(cnt[:, 3, :], cnt[:, 3, :], cst[:, C_IOTA:C_IOTA + N_EXP], ALU.mult))
                link(dve.tensor_reduce(ids_f[:, o:o + 1], cnt[:, 3, :], AX.X, ALU.add))
            link(dve.tensor_reduce(ids_f[:, 3:4], cnt[:, 1, :], AX.X, ALU.add))
            dve.tensor_copy(ids[0:1, :], ids_f[0:1, :]).then_inc(route_ready, 1)
            dve.wait_ge(route_ready, 1)
            over = dve.value_load(ids[0:1, 3:4], min_val=0, max_val=OVER)
            slots = over + N_EXP
            iota = cst[:, C_IOTA:C_IOTA + CAP]
            with dve.Fori(0, slots) as s:
                def split(q):
                    i, j = q // 4, q % 4
                    place = (NQ + q) % SPLITS
                    dve.wait_ge(hi_ready, s * EQ + (NQ + q + 1))
                    dve.tensor_tensor(w_lo[:, place, :], ring[:, i % RING, j * QUARTER:(j + 1) * QUARTER],
                                      w_hi[:, place, :].bitcast(F32), ALU.subtract).then_inc(lo_ready, 1)

                def turned(c):
                    dve.wait_ge(e_aT_hi, s * NCH + (c + 1))
                    dve.tensor_tensor(aT_lo[:, 0:4, 0:CAP], bank[6 + c % 2][:, :].rearrange("p (a n) -> p a n", a=4),
                                      aT_hi[:, 0:4, 0:CAP].bitcast(F32), ALU.subtract).then_inc(e_aT_lo, 1)

                dve.tensor_copy(cur[:, 0, :].unsqueeze(2), pos_t[:, :, bass.ds(s, 1)])
                dve.tensor_copy(cur[:, 1, :].unsqueeze(2), gate_t[:, :, bass.ds(s, 1)]).then_inc(cur_ready, 1)
                dve.wait_ge(cur_ready, s + 1)
                for t in range(TB):
                    dve.tensor_scalar(oh[:, t, 0:CAP], iota, cur[:, 0, t:t + 1], None, ALU.is_equal)
                    o = dve.tensor_scalar(oh[:, t, CAP:2 * CAP], iota, cur[:, 0, t:t + 1], cur[:, 1, t:t + 1],
                                          ALU.is_equal, ALU.mult)
                o.then_inc(slot_ready, 1)
                for q in range(LEAD - 1):
                    split(q)
                for m in range(2):
                    dve.wait_ge(e_hi, s * 2 + (m + 1))
                    dve.tensor_tensor(hT_lo[:, 4 * m:4 * m + 4, 0:CAP],
                                      bank[6 + m][:, :].rearrange("p (a n) -> p a n", a=4),
                                      hT_hi[:, 4 * m:4 * m + 4, 0:CAP].bitcast(F32), ALU.subtract).then_inc(e_lo, 1)
                dve.wait_ge(weight_turned, s + 1)
                dve.tensor_copy(wT, bank[2][:, 0:SEQ].rearrange("p (t n) -> p t n", t=TB)).then_inc(wT_ready, 1)
                for i, (kind, c) in enumerate(order):
                    if kind == "down" and c == NCH - 1:
                        turned(c)
                    for j in range(4):
                        q = 4 * i + j + LEAD - 1
                        if q < EQ:
                            split(q)
                    if kind == "up":
                        dve.wait_ge(quarter_used, s * EQ + (NQ + 4 * (i + 1)))
                        dve.wait_ge(e_silu, s * NCH + (c + 1))
                        at = slice((c % 2) * NW, (c % 2 + 1) * NW)
                        dve.tensor_tensor(y[:, at], gsf[:, at], bank[2 * (c % 2) + 1][:, :], ALU.mult)\
                           .then_inc(e_hidden, 1)
                    if kind == "up" and c == 0 or kind == "down" and c < NCH - 2:
                        turned(c if kind == "up" else c + 1)
                dve.wait_ge(quarter_used, s * EQ + (NQ + EQ))
                dve.tensor_copy(y[:, NW:2 * NW], bank[5][:, :]).then_inc(y_dve, 1)
                for t in range(TB):
                    for half in range(2):
                        xs = xres[:, t, half * NW:(half + 1) * NW]
                        dve.wait_ge(combined, s * 4 + (2 * t + half + 1))
                        dve.tensor_tensor(xs, xs, bank[2 * t + half][:, :], ALU.add).then_inc(e_added, 1)

        @block.vector
        def _(dve):
            step = [0]

            def link(ins):
                step[0] += 1
                ins.then_inc(dve_step, 1)
                dve.wait_ge(dve_step, step[0])

            split = [0]

            def split_to(q1):
                while split[0] < min(q1, NQ):
                    q = split[0]
                    n, k0, kn = quarters[q]
                    p = pieces[n]
                    m = kn * p["n"]
                    at = k0 * p["n"]
                    dve.wait_ge(hi_ready, q + 1)
                    dve.tensor_tensor(w_lo[:, q % SPLITS, 0:m], ring[:, p["place"], at:at + m],
                                      w_hi[:, q % SPLITS, 0:m].bitcast(F32), ALU.subtract).then_inc(lo_ready, 1)
                    split[0] += 1

            def norm(n):
                dve.wait_ge(norm_sqrt, n + 1)
                dve.reciprocal(rinv[:, 0:TB], rt[:, 0:TB]).then_inc(rinv_ready, 1)
                dve.wait_ge(rinv_ready, n + 1)
                if n < 3:
                    dve.tensor_scalar(h[:, 0, :], xres[:, 0, :], rinv[:, 0:1], None, ALU.mult)\
                       .then_inc(h_ready_dve, 1)
                else:
                    dve.wait_ge(gain_row_loaded, 32)
                    for t in range(TB):
                        o = dve.scalar_tensor_tensor(h[:, t, :], xres[:, t, :], rinv[:, t:t + 1], acf[:, 0:D],
                                                     ALU.mult, ALU.mult)
                    o.then_inc(h_ready_dve, 1)
                if n == 0:
                    dve.wait_ge(gains_turned, 1)
                    link(dve.tensor_copy(g_cols[:, :], bank[7][:, 0:33]))
                    dve.tensor_scalar(g_cols[:, G_AQ:G_AQ + 1], g_cols[:, G_AQ:G_AQ + 1], HD ** -0.5, None, ALU.mult)
                    dve.tensor_scalar(g_cols[:, G_BQ:G_BQ + 1], g_cols[:, G_BQ:G_BQ + 1], HD ** -0.5, None, ALU.mult)\
                       .then_inc(gain_cols_ready, 1)
                    dve.wait_ge(gain_cols_ready, 1)
                for k in range(KD):
                    dve.wait_ge(hT_hi_ready, KD * n + 2 * (k // 2) + 2)
                    src = bank[k // 2][:, (k % 2) * SEQ:(k % 2 + 1) * SEQ]
                    hi = hT_hi[:, k, :].bitcast(F32)
                    if n == 3:
                        o = dve.tensor_tensor(hT_lo[:, k, :], src, hi, ALU.subtract)
                    else:
                        o = dve.scalar_tensor_tensor(hT_lo[:, k, :], src, g_cols[:, g_fwd[n] + k:g_fwd[n] + k + 1],
                                                     hi, ALU.mult, ALU.subtract)
                    o.then_inc(hT_lo_ready, 1)

            def projection(stage):
                for i, c in stage_lin(stage):
                    p = pieces[c["piece"]]
                    for q in range(p["q0"], p["q1"]):
                        split_to(q + LEAD)
                    dve.wait_ge(quarter_used, p["q1"])
                    if not c["add"]:
                        dve.tensor_copy(dest[stage](1, c["j"], c["n"]), bank[5 + 2 * (i % 2)][:, 0:c["n"]])\
                           .then_inc(copied_dve, 1)
                    else:
                        for t in range(TB):
                            xs = xres[:, t, c["j"] * NW:(c["j"] + 1) * NW]
                            dve.tensor_tensor(xs, xs, bank[4 + 2 * (i % 2) + t][:, :], ALU.add).then_inc(x_added, 1)

            def attention(g0, g1):
                dve.wait_ge(rows_loaded, 48)
                for i in range(g0, g1 + 3):
                    j = i - 2
                    if g0 <= j < g1:
                        b = j % 2
                        dve.wait_ge(exp_ready, j + 1)
                        if j < A_HEADS:
                            link(dve.tensor_tensor(den[:, b, :], esum[:, b, 0:2], esum[:, b, 2:4], ALU.add))
                            dve.reciprocal(den[:, b, :], den[:, b, :]).then_inc(den_ready, 1)
                        else:
                            dve.reciprocal(den[:, b, :], esum[:, b, 0:2]).then_inc(den_ready, 1)
                    if i < g1:
                        w = sources(i)[3]
                        dve.wait_ge(qT_ready, i + 1)
                        src, dst = bank[i % 2][0:w, SEQ:2 * SEQ], qkT[0:w, i % 2, SEQ:2 * SEQ]
                        if i < HEADS0:
                            col = G_AK if i < A_HEADS else G_BK
                            o = dve.tensor_scalar(dst, src, g_cols[0:w, col:col + 1], None, ALU.mult)
                        else:
                            o = dve.tensor_copy(dst, src)
                        o.then_inc(kT_ready, 1)
                    j = i - 1
                    if g0 <= j < g1:
                        b = j % 2
                        dve.wait_ge(scored, j + 1)
                        s = bank[2 + b][:, 0:LANES]
                        if j < A_HEADS:
                            o = dve.scalar_tensor_tensor(sc[:, b, :], cst[:, C_DIST:C_DIST + LANES],
                                                         2.0 ** (-8.0 * (j + 1) / A_HEADS), s, ALU.mult, ALU.add)
                        elif j < HEADS0:
                            dve.wait_ge(bias_ready, j - A_HEADS + 1)
                            o = dve.tensor_tensor(sc[:, b, :], s, bias[:, b, :], ALU.add)
                        else:
                            o = dve.scalar_tensor_tensor(sc[:, b, :], s, C_QK ** -0.5,
                                                         cst[:, C_MASK:C_MASK + LANES], ALU.mult, ALU.add)
                        link(o)
                        dve.tensor_reduce(mx[:, b, 0:1], sc[:, b, 0:P], AX.X, ALU.max)
                        link(dve.tensor_reduce(mx[:, b, 1:2], sc[:, b, P:LANES], AX.X, ALU.max))
                        if j < A_HEADS:
                            link(dve.tensor_scalar(mx[:, b, :], mx[:, b, :], sinks[:, j:j + 1], None, ALU.max))
                        dve.tensor_scalar(nmax[:, b, 0:2], mx[:, b, :], -1.0, None, ALU.mult).then_inc(max_ready, 1)
                    j = i - 3
                    if g0 <= j < g1:
                        dve.wait_ge(o_hi, j + 1)
                        dve.tensor_tensor(o_place(hT_lo, j), o_psum(j), o_place(hT_hi, j).bitcast(F32),
                                          ALU.subtract).then_inc(o_lo, 1)

            ffn_chunks = (D_FF + NW - 1) // NW

            def turned(c):
                dve.wait_ge(aT_hi_ready, c + 1)
                for m in range(min(NW, D_FF - c * NW) // (2 * P)):
                    two = lambda b: b[:, 2 * m:2 * m + 2, :].rearrange("p a n -> p (a n)")
                    o = dve.tensor_tensor(two(aT_lo), bank[2 * (c % 2) + m][:, :], two(aT_hi).bitcast(F32),
                                          ALU.subtract)
                o.then_inc(aT_lo_ready, 1)

            def ffn():
                for n in stage_pieces("ffn"):
                    p = pieces[n]
                    c = p["c"]
                    if p["kind"] == "down" and n == stage_pieces("ffn")[-1]:
                        turned(c)
                    for q in range(p["q0"], p["q1"]):
                        split_to(q + LEAD)
                    if p["kind"] == "up":
                        dve.wait_ge(quarter_used, p["q1"])
                        dve.wait_ge(silu_ready, c + 1)
                        for t in range(TB):
                            o = dve.tensor_tensor(act_t[:, t, 0:p["n"]], gs[:, t, 0:p["n"]],
                                                  bank[2 - 2 * (c % 2) + t][:, 0:p["n"]], ALU.mult)
                        o.then_inc(hidden_ready, 1)
                    if p["kind"] == "up" and c == 0 or p["kind"] == "down" and c < ffn_chunks - 2:
                        turned(c if p["kind"] == "up" else c + 1)
                dve.wait_ge(quarter_used, p["q1"])
                for t in range(TB):
                    for half in range(2):
                        xs = xres[:, t, half * NW:(half + 1) * NW]
                        dve.tensor_tensor(xs, xs, bank[4 + 2 * t + half][:, :], ALU.add).then_inc(x_added, 1)

            dve.memset(eps[:, :], EPS)
            dve.memset(ones[:, :], 1.0).then_inc(ones_set, 1)
            dve.wait_ge(x_loaded, 16)
            dve.wait_ge(consts_loaded, 16)
            norm(0)
            projection("in")
            for t in range(TB):
                j0, j1 = (hf[:, 0:640], hf[:, 640:1664]) if t == 0 else (gsf[:, 0:640], y[:, 0:1024])
                dve.wait_ge(squared, 2 * t + 1)
                dve.tensor_reduce(ss[:, 26 * t:26 * t + 10], j0.rearrange("p (h n) -> p h n", n=HD), AX.X, ALU.add)
                dve.wait_ge(squared, 2 * t + 2)
                o = dve.tensor_reduce(ss[:, 26 * t + 10:26 * t + 26], j1.rearrange("p (h n) -> p h n", n=HD),
                                      AX.X, ALU.add)
            o.then_inc(head_ss, 1)
            dve.wait_ge(head_sqrt, 1)
            dve.reciprocal(rinv[:, 0:52], rt[:, 0:52]).then_inc(head_rinv, 1)
            dve.wait_ge(head_rinv, 1)
            for c0, hs, r0 in ((A_Q, 10, 0), (B_Q, 16, 10)):
                v = proj[:, 0, c0:c0 + hs * HD].rearrange("p (h n) -> p h n", n=HD)
                o = dve.tensor_tensor(v, v, rinv[:, r0:r0 + hs].unsqueeze(2).to_broadcast([P, hs, HD]), ALU.mult)
            o.then_inc(normed_dve, 1)
            attention(0, HEADS0)
            projection("out")
            if last >= 2:
                norm(1)
                ffn()
            if last >= 3:
                norm(2)
                projection("dq")
                projection("dkv")
                dve.wait_ge(lat_ss, 1)
                dve.reciprocal(rinv[:, 2:6], rt[:, 2:6]).then_inc(lat_rinv, 1)
                dve.wait_ge(lat_rinv, 1)
                for t in range(TB):
                    dve.tensor_scalar(lat[:, t, :], lat[:, t, :], rinv[:, 2 + t:3 + t], None, ALU.mult)
                    o = dve.tensor_scalar(lkv[:, t, 0:KV_LORA], lkv[:, t, 0:KV_LORA], rinv[:, 4 + t:5 + t], None,
                                          ALU.mult)
                o.then_inc(lat_ready, 1)
                for t in range(TB):
                    cos, sin = (cst[:, C_ROT + 64 * t + c:C_ROT + 64 * t + c + 16] for c in (0, C_ROPE))
                    src = lkv[:, t, KV_LORA:]
                    dve.wait_ge(gains_loaded, 16 * 9)
                    link(dve.tensor_tensor(src, src, gk[:, C_NOPE:], ALU.mult))
                    k1, k2 = src[:, 0:16], src[:, 16:32]
                    for m, (u, v) in enumerate(((k1, cos), (k2, sin), (k2, cos), (k1, sin))):
                        o = dve.tensor_tensor(kr_t[:, m, :], u, v, ALU.mult)
                    link(o)
                    dve.tensor_tensor(kr[:, t, 0:16], kr_t[:, 0, :], kr_t[:, 1, :], ALU.subtract)
                    link(dve.tensor_tensor(kr[:, t, 16:32], kr_t[:, 2, :], kr_t[:, 3, :], ALU.add))
                for k in range(5):
                    dve.wait_ge(lat_hi, min(5, 2 * (k // 2) + 2))
                    col = G_QA + k
                    dve.scalar_tensor_tensor(aT_lo[:, k, :], bank[k // 2][:, (k % 2) * SEQ:(k % 2 + 1) * SEQ],
                                             g_cols[:, col:col + 1], aT_hi[:, k, :].bitcast(F32), ALU.mult,
                                             ALU.subtract).then_inc(lat_lo, 1)
                projection("uq")
                projection("ukv")
                for t in range(TB):
                    dve.wait_ge(squared, 4 + 2 * t + 1)
                    dve.tensor_reduce(ss[:, 16 * t:16 * t + 16],
                                      hf[:, 0:1536].rearrange("p (h n) -> p h n", n=C_QK), AX.X, ALU.add)
                    dve.wait_ge(squared, 4 + 2 * t + 2)
                    link(dve.tensor_reduce(ss[:, 32 + 16 * t:48 + 16 * t],
                                           acf[:, 0:1024].rearrange("p (h n) -> p h n", n=C_NOPE), AX.X, ALU.add))
                    dve.tensor_scalar(ss[:, 32 + 16 * t:48 + 16 * t], ss[:, 32 + 16 * t:48 + 16 * t],
                                      ss[:, 64 + t:65 + t], None, ALU.add).then_inc(head_ss, 1)
                dve.wait_ge(head_sqrt, 2)
                dve.reciprocal(rinv[:, 0:64], rt[:, 0:64]).then_inc(head_rinv, 1)
                dve.wait_ge(head_rinv, 2)
                half = C_ROPE // 2
                for t in range(TB):
                    v = qc[:, t, :].rearrange("p (h n) -> p h n", n=C_QK)
                    link(dve.tensor_tensor(v, v, rinv[:, 16 * t:16 * t + 16].unsqueeze(2).to_broadcast(
                        [P, C_HEADS, C_QK]), ALU.mult))
                    link(dve.tensor_tensor(v, v, gq[:, :].unsqueeze(1).to_broadcast([P, C_HEADS, C_QK]), ALU.mult))
                    cos, sin = (cst[:, C_ROT + 64 * t + c:C_ROT + 64 * t + c + 16].unsqueeze(1).to_broadcast(
                        [P, C_HEADS, half]) for c in (0, C_ROPE))
                    q1, q2 = v[:, :, C_NOPE:C_NOPE + half], v[:, :, C_NOPE + half:]
                    tmp = acf[:, :].rearrange("p (m h n) -> p m h n", m=4, h=C_HEADS)
                    for m, (u, w) in enumerate(((q1, cos), (q2, sin), (q2, cos), (q1, sin))):
                        o = dve.tensor_tensor(tmp[:, m], u, w, ALU.mult)
                    link(o)
                    dve.tensor_tensor(q1, tmp[:, 0], tmp[:, 1], ALU.subtract)
                    o = dve.tensor_tensor(q2, tmp[:, 2], tmp[:, 3], ALU.add)
                    if t == 0:
                        link(o)
                o.then_inc(normed_dve, 1)
                attention(HEADS0, HEADS)
                projection("o")
            if last >= 4:
                experts_dve(dve, norm, link)

        @block.gpsimd
        def _(pool):
            pool.memset(g_rows[:, :], 0.0).then_inc(rows_cleared, 1)
            pool.dma_start(cst[:, :], const).then_inc(consts_loaded, 16)
            pool.wait_ge(rows_cleared, 1)
            for n, name in enumerate(("ev_attn_norm", "ev_ffn_norm", "od_attn_norm")):
                pool.dma_start(g_rows[8 * n:8 * n + 8, :], a[name][0].rearrange("(k p) -> k p", p=P))\
                    .then_inc(gains_loaded, 16)
            pool.dma_start(g_rows[G_QA:G_QA + 3, :], a["od_q_a_norm"][0].rearrange("(k p) -> k p", p=P))\
                .then_inc(gains_loaded, 16)
            pool.dma_start(g_rows[G_KVA:G_KVA + 2, :], a["od_kv_a_norm"][0].rearrange("(k p) -> k p", p=P))\
                .then_inc(gains_loaded, 16)
            for row, name in ((G_AQ, "ev_a_q_norm"), (G_AK, "ev_a_k_norm"), (G_BQ, "ev_b_q_norm"),
                              (G_BK, "ev_b_k_norm")):
                pool.dma_start(g_rows[row:row + 1, 0:HD], a[name]).then_inc(gains_loaded, 16)
            pool.dma_start(sinks[:, :], a["ev_a_sinks"].to_broadcast([P, A_HEADS])).then_inc(rows_loaded, 16)
            pool.dma_start(gq[:, :], a["od_q_norm"].to_broadcast([P, C_QK])).then_inc(rows_loaded, 16)
            pool.dma_start(gk[:, :], a["od_k_norm"].to_broadcast([P, C_QK])).then_inc(rows_loaded, 16)

            def load_bias(b):
                base = b * (2 * MAX_REL + 1) + MAX_REL + 1 - P
                for dst, keys in zip(braw[b % 2], (P, 2 * P)):
                    src = bass.AP(a["ev_b_rel_bias"].tensor, base, [[1, P], [1, keys]])
                    pool.dma_start(dst, src).then_inc(braw_loaded[b % 2], 16)

            pool.wait_ge(head_rinv, 1)
            for c0, hs, r0 in ((A_Q, 10, 26), (B_Q, 16, 36)):
                v = proj[:, 1, c0:c0 + hs * HD].rearrange("p (h n) -> p h n", n=HD)
                o = pool.tensor_tensor(v, v, rinv[:, r0:r0 + hs].unsqueeze(2).to_broadcast([P, hs, HD]), ALU.mult)
            o.then_inc(normed_pool, 1)
            pool.wait_ge(normed_pool, 1)
            load_bias(0)
            load_bias(1)

            def make_bias(b):
                pool.wait_ge(braw_loaded[b % 2], 32 * (b // 2 + 1))
                if b >= 2:
                    pool.wait_ge(max_ready, A_HEADS + b - 1)
                lo, hi = braw[b % 2]
                pool.tensor_tensor(bias[:, b % 2, 0:P], lo[:, ::-1], cst[:, C_MASK:C_MASK + P], ALU.add)
                pool.tensor_tensor(bias[:, b % 2, P:LANES], hi[:, ::-1], cst[:, C_MASK + P:C_MASK + LANES], ALU.add)\
                    .then_inc(bias_ready, 1)
                if b + 2 < B_HEADS:
                    pool.wait_ge(bias_ready, b + 1)
                    load_bias(b + 2)

            def normalise(j):
                pool.wait_ge(den_ready, j + 1)
                b = j % 2
                pool.tensor_scalar(pn[:, b, 0:P], sc[:, b, 0:P], den[:, b, 0:1], None, ALU.mult)
                pool.tensor_scalar(pn[:, b, P:LANES], sc[:, b, P:LANES], den[:, b, 1:2], None, ALU.mult)\
                    .then_inc(p_ready, 1)

            for j in range(HEADS0):
                if j < B_HEADS and j < 2:
                    make_bias(j)
                normalise(j)
                b = j + 2 - A_HEADS
                if 2 <= b < B_HEADS:
                    make_bias(b)

            if last >= 3:
                def make_k(c):
                    if c >= 2:
                        pool.wait_ge(qk_turned, HEADS0 + c - 1)
                    b = (HEADS0 + c) % 2
                    for t in range(TB):
                        r = rinv[:, 32 + 16 * t + c:33 + 16 * t + c]
                        pool.tensor_scalar(kbuf[:, b, t, 0:C_NOPE], kv[:, t, c * 128:c * 128 + C_NOPE], r, None,
                                           ALU.mult).then_inc(pool_step, 1)
                        o = pool.tensor_scalar(kbuf[:, b, t, C_NOPE:], kr[:, t, :], r, None, ALU.mult)
                    o.then_inc(pool_step, 1)
                    pool.wait_ge(pool_step, 3 * c + 3)
                    v = kbuf[:, b, :, 0:C_NOPE]
                    pool.tensor_tensor(v, v, gk[:, 0:C_NOPE].unsqueeze(1).to_broadcast([P, TB, C_NOPE]), ALU.mult)\
                        .then_inc(k_ready, 1)

                pool.wait_ge(rows_loaded, 48)
                pool.wait_ge(head_rinv, 2)
                make_k(0)
                make_k(1)
                for j in range(HEADS0, HEADS):
                    normalise(j)
                    if j - HEADS0 + 2 < C_HEADS:
                        make_k(j - HEADS0 + 2)
            if last >= 4:
                pool.wait_ge(pv_done, HEADS)
                pool.dma_start(acf[:, 0:D], a["od_ffn_norm"].to_broadcast([P, D])).then_inc(gain_row_loaded, 16)
                pool.dma_start(router.rearrange("p (k e) -> p k e", e=N_EXP),
                               a["od_router"][0].rearrange("(k p) e -> p k e", p=P)).then_inc(gain_row_loaded, 16)

    return


_INS = ["x", "ev_attn_norm", "ev_w_in", "ev_a_q_norm", "ev_a_k_norm", "ev_a_sinks", "ev_b_q_norm", "ev_b_k_norm",
        "ev_b_rel_bias", "ev_w_out", "ev_ffn_norm", "ev_w_gate", "ev_w_up", "ev_w_down", "od_attn_norm", "od_w_dq",
        "od_q_a_norm", "od_w_uq", "od_w_dkv", "od_kv_a_norm", "od_w_ukv", "od_q_norm", "od_k_norm", "od_w_o",
        "od_ffn_norm", "od_router", "od_e_gate", "od_e_up", "od_e_down"]


def kernel(**inputs):
    import concourse.bacc as _bacc
    from concourse.bass_utils import run_bass_kernel_spmd as _run

    nc = _bacc.Bacc("TRN2", target_bir_lowering=False, num_devices=1)
    arrays, args = {}, {}
    given = {name: np.ascontiguousarray(inputs[name]) for name in _INS}
    given["const"] = constants()
    for name, v in given.items():
        arrays[f"in_{name}_dram"] = v
        args[name] = nc.dram_tensor(f"in_{name}_dram", v.shape, mybir.dt.from_np(v.dtype), kind="ExternalInput").ap()
    out = nc.dram_tensor("out_0_dram", (1, SEQ, D), F32, kind="ExternalOutput").ap()
    trunk(nc, args, out)
    r = _run(nc, [arrays], core_ids=[0])
    return r.results[0]["out_0_dram"]
```

```python
from contextlib import ExitStack

import numpy as np

import concourse.bass as bass
from concourse import mybir

ALU = mybir.AluOpType
ACT = mybir.ActivationFunctionType
AX = mybir.AxisListType
F32 = mybir.dt.float32
F32R = mybir.dt.float32r
I32 = mybir.dt.int32

P = 128
D = 1024
KD = D // P
SEQ = 256
TB = SEQ // P
CHUNK = 64
EPS = 1e-6
NEG = -1e30
HD = 64
A_HEADS, A_KV, B_HEADS = 8, 2, 8
IN_W = 2304
MAX_REL = 256
C_HEADS, C_NOPE, C_ROPE, C_V = 16, 64, 32, 64
C_QK = C_NOPE + C_ROPE
Q_LORA, KV_LORA = 384, 256
D_FF = 2816
N_EXP = 8
E_FF = 3584
CAP = 128
OVER = 3
SLOTS = N_EXP + OVER
NW = 512
RING = 7
PIECE = KD * NW
SPLITS = 4
QUARTER = PIECE // 4
LEAD = SPLITS
HEADS0 = A_HEADS + B_HEADS
HEADS = HEADS0 + C_HEADS
KBUFS = 4
LANES = 128 + 256

A_Q, A_K, A_V, B_Q, B_K, B_V = 0, 512, 640, 768, 1280, 1792
C_ID, C_TRI, C_IOTA, C_DIST, C_MASK, C_ROT = 0, 128, 256, 384, 768, 1152
C_ALL = C_ROT + TB * 2 * C_ROPE


def constants():
    c = np.zeros((P, C_ALL), np.float32)
    c[:, C_ID:C_ID + P] = np.eye(P)
    c[:, C_TRI:C_TRI + P] = np.triu(np.ones((P, P)), 1)
    c[:, C_IOTA:C_IOTA + P] = np.arange(P)
    for b, at, keys in ((0, 0, P), (1, P, 2 * P)):
        q = (b * P + np.arange(P))[:, None]
        k = np.arange(keys)[None, :]
        qc, kc = q // CHUNK, k // CHUNK
        c[:, C_DIST + at:C_DIST + at + keys] = np.where((kc <= qc) & (kc >= qc - 1), -np.abs(q - k), NEG)
        c[:, C_MASK + at:C_MASK + at + keys] = np.where(kc <= qc, 0.0, NEG)
    pos = np.arange(SEQ, dtype=np.float32)
    power = np.arange(0, C_ROPE, 2, dtype=np.float32) / np.float32(C_ROPE)
    inv = (np.float32(1.0) / (np.float32(10000.0) ** power)).astype(np.float32)
    ang = (pos[:, None] * inv[None, :]).astype(np.float32)
    ang = np.concatenate([ang, ang], axis=-1)
    rot = np.stack([np.cos(ang), np.sin(ang)], axis=1).reshape(TB, P, 2 * C_ROPE)
    c[:, C_ROT:] = rot.transpose(1, 0, 2).reshape(P, -1)
    return c


def plan(w, last):
    pieces, quarters = [], []

    def add(stage, src, nk, n, place, kind="", c=0):
        per = 2 if n <= NW else 1
        first = len(quarters)
        for k in range(0, nk, per):
            quarters.append((len(pieces), k, min(per, nk - k)))
        pieces.append(dict(stage=stage, src=src, nk=nk, n=n, place=place, kind=kind, c=c, per=per,
                           q0=first, q1=len(quarters)))

    def cols(ap, c0, n):
        return ap[0, :, c0:c0 + n].rearrange("(k p) n -> p k n", p=P)

    for j, c0 in enumerate(range(0, IN_W, NW)):
        add("in", cols(w["w_in"], c0, min(NW, IN_W - c0)), KD, min(NW, IN_W - c0), j)
    for j in range(2):
        add("out", cols(w["w_out"], j * NW, NW), KD, NW, j)
    if last >= 2:
        place = 2
        chunks = [(c0, min(NW, D_FF - c0)) for c0 in range(0, D_FF, NW)]
        down = lambda c: w["w_down"][0, chunks[c][0]:sum(chunks[c]), :].rearrange("(k p) n -> p k n", p=P)
        for c, (c0, n) in enumerate(chunks):
            for kind, name in (("gate", "w_gate"), ("up", "w_up")):
                add("ffn", cols(w[name], c0, n), KD, n, place % RING, kind, c)
                place += 1
            for d in [c - 1] * (c > 0) + [c] * (c == len(chunks) - 1):
                add("ffn", down(d), chunks[d][1] // P, D, place % RING, "down", d)
                place += 1
    if last >= 3:
        small = [("dq", cols(w["w_dq"], 0, Q_LORA), KD, Q_LORA),
                 ("dkv", cols(w["w_dkv"], 0, KV_LORA + C_ROPE), KD, KV_LORA + C_ROPE)]
        small += [("uq", cols(w["w_uq"], j * NW, NW), Q_LORA // P, NW) for j in range(3)]
        small += [("ukv", cols(w["w_ukv"], j * NW, NW), KV_LORA // P, NW) for j in range(4)]
        for j, (stage, src, nk, n) in enumerate(small):
            add(stage, src, nk, n, j % 3)
        for j in range(2):
            add("o", cols(w["w_o"], j * NW, NW), KD, NW, 3 + j)
    return pieces, quarters


def expert_order():
    order = []
    n = E_FF // NW
    for c in range(n):
        order += [("gate", c), ("up", c)]
        order += [("down", c - 1)] * (c > 0) + [("down", c)] * (c == n - 1)
    return order


def trunk(nc, a, out, last=4):
    x_in, const = a["x"], a["const"]
    weights = {"w_in": a["ev_w_in"], "w_out": a["ev_w_out"], "w_gate": a["ev_w_gate"], "w_up": a["ev_w_up"],
               "w_down": a["ev_w_down"], "w_dq": a["od_w_dq"], "w_uq": a["od_w_uq"], "w_dkv": a["od_w_dkv"],
               "w_ukv": a["od_w_ukv"], "w_o": a["od_w_o"]}
    pieces, quarters = plan(weights, last)
    NQ = len(quarters)
    order = expert_order()
    EQ = 4 * len(order)
    NCH = E_FF // NW
    uses = [0] * RING
    for p in pieces:
        p["turn"] = uses[p["place"]]
        uses[p["place"]] += 1
    stage_pieces = lambda s: [n for n, p in enumerate(pieces) if p["stage"] == s]

    with ExitStack() as ctx:
        def sb(name, shape, dt=F32):
            return ctx.enter_context(nc.sbuf_tensor(name, shape, dt))

        def sem(name):
            return ctx.enter_context(nc.semaphore(name))

        ring = sb("ring", [P, RING, PIECE])
        w_hi = sb("w_hi", [P, SPLITS, QUARTER], F32R)
        w_lo = sb("w_lo", [P, SPLITS, QUARTER], F32R)
        xres = sb("xres", [P, TB, D])
        h = sb("h", [P, TB, D])
        hT_hi = sb("hT_hi", [P, KD, SEQ], F32R)
        hT_lo = sb("hT_lo", [P, KD, SEQ], F32R)
        aT_hi = sb("aT_hi", [P, 5, SEQ], F32R)
        aT_lo = sb("aT_lo", [P, 5, SEQ], F32R)
        gs = sb("gs", [P, TB, NW])
        act_t = sb("act_t", [P, TB, NW])
        y = sb("y", [P, D])
        cst = sb("cst", [P, C_ALL])
        ones = sb("ones", [P, P])
        g_rows = sb("g_rows", [35, P])
        g_cols = sb("g_cols", [P, 35])
        gq = sb("gq", [P, C_QK])
        gk = sb("gk", [P, C_QK])
        sinks = sb("sinks", [P, A_HEADS])
        eps = sb("eps", [P, 1])
        ss = sb("ss", [P, 66])
        rt = sb("rt", [P, 66])
        rinv = sb("rinv", [P, 66])
        nmax = sb("nmax", [P, 2, 4])
        mx = sb("mx", [P, 2, 2])
        esum = sb("esum", [P, 2, 4])
        den = sb("den", [P, 2, 2])
        kr = sb("kr", [P, TB, C_ROPE])

        ident = cst[:, C_ID:C_ID + P]
        g_fwd = {0: 0, 1: 8, 2: 16}
        G_QA, G_KVA, G_AQ, G_AK, G_BQ, G_BK, G_CQ, G_CK = 24, 27, 29, 30, 31, 32, 33, 34

        scratch = ring[:, 5:7, :].rearrange("p a b -> p (a b)")
        proj = scratch[:, 0:TB * IN_W].rearrange("p (t n) -> p t n", t=TB)
        kv = scratch[:, 0:4096].rearrange("p (t n) -> p t n", t=TB)
        qc = scratch[:, 4096:7168].rearrange("p (t n) -> p t n", t=TB)
        kbuf = scratch[:, 7168:7168 + KBUFS * TB * C_QK].rearrange("p (b t n) -> p b t n", b=KBUFS, t=TB)
        hf = h[:, :, :].rearrange("p t n -> p (t n)")
        gsf = gs[:, :, :].rearrange("p t n -> p (t n)")
        acf = act_t[:, :, :].rearrange("p t n -> p (t n)")
        qkT = hf[:, 0:1024].rearrange("p (b n) -> p b n", b=2)
        sc = hf[:, 1024:1024 + 2 * LANES].rearrange("p (b n) -> p b n", b=2)
        pn = gsf[:, 0:2 * LANES].rearrange("p (b n) -> p b n", b=2)
        pT = y[:, 0:2 * LANES].rearrange("p (b n) -> p b n", b=2)
        kr_t = acf[:, 0:2 * C_ROPE].rearrange("p (m n) -> p m n", m=4)
        bias0 = scratch[:, 4608:4608 + B_HEADS * P].rearrange("p (h n) -> p h n", h=B_HEADS)
        bias1 = scratch[:, 5632:5632 + 2 * B_HEADS * P].rearrange("p (h n) -> p h n", h=B_HEADS)
        lat = y[:, 0:TB * Q_LORA].rearrange("p (t n) -> p t n", t=TB)
        lkv = gsf[:, 0:TB * (KV_LORA + C_ROPE)].rearrange("p (t n) -> p t n", t=TB)

        bank = [ctx.enter_context(nc.psum_tensor(f"bank{i}", [P, NW], F32)) for i in range(8)]

        arrived = [sem(f"arrived{i}") for i in range(RING)]
        hi_ready = sem("hi_ready")
        lo_ready = sem("lo_ready")
        quarter_used = sem("quarter_used")
        x_loaded = sem("x_loaded")
        consts_loaded = sem("consts_loaded")
        rows_cleared = sem("rows_cleared")
        rows_loaded = sem("rows_loaded")
        gains_loaded = sem("gains_loaded")
        ones_set = sem("ones_set")
        gains_turned = sem("gains_turned")
        gain_cols_ready = sem("gain_cols_ready")
        act_step = sem("act_step")
        dve_step = sem("dve_step")
        norm_sqrt = sem("norm_sqrt")
        rinv_ready = sem("rinv_ready")
        h_ready_dve = sem("h_ready_dve")
        h_ready_act = sem("h_ready_act")
        hT_turned = sem("hT_turned")
        hT_hi_ready = sem("hT_hi_ready")
        hT_lo_ready = sem("hT_lo_ready")
        copied_act = sem("copied_act")
        copied_dve = sem("copied_dve")
        x_added = sem("x_added")
        squared = sem("squared")
        head_ss = sem("head_ss")
        head_sqrt = sem("head_sqrt")
        head_rinv = sem("head_rinv")
        normed_dve = sem("normed_dve")
        normed_pool = sem("normed_pool")
        braw_loaded = sem("braw_loaded")
        bias_ready = sem("bias_ready")
        k_ready = sem("k_ready")
        qk_turned = sem("qk_turned")
        qkT_ready = sem("qkT_ready")
        scored = sem("scored")
        max_ready = sem("max_ready")
        exp_ready = sem("exp_ready")
        p_ready = sem("p_ready")
        p_turned = sem("p_turned")
        pT_ready = sem("pT_ready")
        pv_done = sem("pv_done")
        o_hi = sem("o_hi")
        o_lo = sem("o_lo")
        silu_ready = sem("silu_ready")
        hidden_ready = sem("hidden_ready")
        hidden_turned = sem("hidden_turned")
        aT_hi_ready = sem("aT_hi_ready")
        aT_lo_ready = sem("aT_lo_ready")
        lat_ss = sem("lat_ss")
        lat_rinv = sem("lat_rinv")
        lat_ready = sem("lat_ready")
        lat_turned = sem("lat_turned")
        lat_hi = sem("lat_hi")
        lat_lo = sem("lat_lo")
        stored = sem("stored")

        lin = []
        na = nd = 0
        for s in ("in", "out", "dq", "dkv", "uq", "ukv", "o"):
            for j, n in enumerate(stage_pieces(s)):
                add = s in ("out", "o")
                na, nd = na + (not add), nd + (not add)
                lin.append(dict(stage=s, piece=n, j=j, n=pieces[n]["n"], add=add, na=na, nd=nd))
        dest = {"in": lambda t, j, n: proj[:, t, j * NW:j * NW + n], "dq": lambda t, j, n: lat[:, t, :],
                "dkv": lambda t, j, n: lkv[:, t, :], "uq": lambda t, j, n: qc[:, t, j * NW:j * NW + n],
                "ukv": lambda t, j, n: kv[:, t, j * NW:j * NW + n]}
        stage_lin = lambda s: [(i, c) for i, c in enumerate(lin) if c["stage"] == s]

        def sources(g):
            if g < A_HEADS:
                kvh = g // (A_HEADS // A_KV)
                return (lambda t: proj[:, t, A_Q + g * HD:A_Q + (g + 1) * HD],
                        lambda t: proj[:, t, A_K + kvh * HD:A_K + (kvh + 1) * HD],
                        lambda t: proj[:, t, A_V + kvh * HD:A_V + (kvh + 1) * HD], HD)
            if g < HEADS0:
                b = g - A_HEADS
                return (lambda t: proj[:, t, B_Q + b * HD:B_Q + (b + 1) * HD],
                        lambda t: proj[:, t, B_K + b * HD:B_K + (b + 1) * HD],
                        lambda t: proj[:, t, B_V + b * HD:B_V + (b + 1) * HD], HD)
            c = g - HEADS0
            return (lambda t: qc[:, t, c * C_QK:(c + 1) * C_QK],
                    lambda t: kbuf[:, g % KBUFS, t, :],
                    lambda t: kv[:, t, c * 128 + C_NOPE:(c + 1) * 128], C_QK)

        def o_place(dst, g):
            m = g % HEADS0
            r = 64 * (m % 2)
            return dst[r:r + 64, m // 2, :]

        def o_psum(g):
            r = 64 * (g % 2)
            return bank[6 + g % 2][r:r + 64, 0:SEQ]

        if last >= 4:
            route = sb("route", [P, 16, TB * N_EXP])
            pos_t = sb("pos_t", [P, TB, SLOTS + 1])
            gate_t = sb("gate_t", [P, TB, SLOTS])
            cnt = sb("cnt", [P, 4, N_EXP])
            ids_f = sb("ids_f", [P, 4])
            ids = sb("ids", [1, 4], I32)
            cur = sb("cur", [P, 3, TB])
            oh = act_t
            wT = act_t[:, :, 2 * CAP:2 * CAP + P]
            router = y[:, 0:KD * N_EXP]
            logits_done = sem("logits_done")
            mask_ready = sem("mask_ready")
            counted = sem("counted")
            route_ready = sem("route_ready")
            gain_row_loaded = sem("gain_row_loaded")
            cur_ready = sem("cur_ready")
            slot_ready = sem("slot_ready")
            gathered = sem("gathered")
            weight_turned = sem("weight_turned")
            e_hi = sem("e_hi")
            e_lo = sem("e_lo")
            wT_ready = sem("wT_ready")
            y_done = sem("y_done")
            y_act = sem("y_act")
            y_dve = sem("y_dve")
            combined = sem("combined")
            e_silu = sem("e_silu")
            e_hidden = sem("e_hidden")
            e_gate = sem("e_gate")
            e_up = sem("e_up")
            e_turned = sem("e_turned")
            e_aT_hi = sem("e_aT_hi")
            e_aT_lo = sem("e_aT_lo")
            e_added = sem("e_added")
            e_once = sem("e_once")

        X_ADDS = {0: 0, 1: 4, 2: 8, 3: 12}

        block = ctx.enter_context(nc.Block())

        @block.sync
        def _(sp):
            sp.dma_start(xres[:, :, :], x_in[0].rearrange("(t p) d -> p t d", p=P)).then_inc(x_loaded, 16)
            sp.dma_start(cst[:, :], const).then_inc(consts_loaded, 16)
            sp.wait_ge(rows_cleared, 1)
            for n, name in enumerate(("ev_attn_norm", "ev_ffn_norm", "od_attn_norm")):
                sp.dma_start(g_rows[8 * n:8 * n + 8, :], a[name][0].rearrange("(k p) -> k p", p=P))\
                   .then_inc(gains_loaded, 16)
            sp.dma_start(g_rows[G_QA:G_QA + 3, :], a["od_q_a_norm"][0].rearrange("(k p) -> k p", p=P))\
               .then_inc(gains_loaded, 16)
            sp.dma_start(g_rows[G_KVA:G_KVA + 2, :], a["od_kv_a_norm"][0].rearrange("(k p) -> k p", p=P))\
               .then_inc(gains_loaded, 16)
            for row, name in ((G_AQ, "ev_a_q_norm"), (G_AK, "ev_a_k_norm"), (G_BQ, "ev_b_q_norm"),
                              (G_BK, "ev_b_k_norm")):
                sp.dma_start(g_rows[row:row + 1, 0:HD], a[name]).then_inc(gains_loaded, 16)
            for row, name in ((G_CQ, "od_q_norm"), (G_CK, "od_k_norm")):
                sp.dma_start(g_rows[row:row + 1, 0:C_NOPE], a[name][:, 0:C_NOPE]).then_inc(gains_loaded, 16)
            for n, p in enumerate(pieces):
                before = [m for m in range(n) if pieces[m]["place"] == p["place"]]
                if before:
                    sp.wait_ge(lo_ready, pieces[before[-1]]["q1"])
                if p["stage"] == "ffn" and p["place"] >= 5 and all(pieces[m]["stage"] != "ffn" for m in before):
                    sp.wait_ge(pv_done, HEADS0)
                dst = ring[:, p["place"], 0:p["nk"] * p["n"]].rearrange("p (k n) -> p k n", k=p["nk"])
                sp.dma_start(dst, p["src"]).then_inc(arrived[p["place"]], 16)
            if last >= 4:
                def load(e, i, kind, c):
                    if kind == "down":
                        src = a["od_e_down"][0, bass.ds(e, 1), c * NW:(c + 1) * NW, :].rearrange(
                            "o (k p) n -> p (o k) n", p=P)
                    else:
                        src = a["od_e_" + kind][0, bass.ds(e, 1), :, c * NW:(c + 1) * NW].rearrange(
                            "o (k p) n -> p (o k) n", p=P)
                    dst = ring[:, i % RING, :].rearrange("p (k n) -> p k n", k=src.shape[1])
                    sp.dma_start(dst, src).then_inc(arrived[i % RING], 16)

                for i, (kind, c) in enumerate(order):
                    if i < RING:
                        before = [m for m in range(len(pieces)) if pieces[m]["place"] == i]
                        sp.wait_ge(lo_ready, pieces[before[-1]]["q1"])
                        if i == 5:
                            sp.wait_ge(pv_done, HEADS)
                    else:
                        sp.wait_ge(lo_ready, NQ + 4 * (i - RING + 1))
                    load(0, i, kind, c)
                with sp.Fori(1, N_EXP) as e:
                    for i, (kind, c) in enumerate(order):
                        sp.wait_ge(lo_ready, e * EQ + (NQ + 4 * (i - RING + 1)))
                        load(e, i, kind, c)
                sp.wait_ge(route_ready, 1)
                over = sp.value_load(ids[0:1, 3:4], min_val=0, max_val=OVER)
                with sp.If(over > 0):
                    with sp.Fori(0, over) as o:
                        e = sp.value_load(ids[0:1, bass.ds(o, 1)], min_val=0, max_val=N_EXP - 1)
                        for i, (kind, c) in enumerate(order):
                            sp.wait_ge(lo_ready, o * EQ + (N_EXP * EQ + NQ + 4 * (i - RING + 1)))
                            load(e, i, kind, c)
                slots = over + N_EXP
                sp.wait_ge(lo_ready, slots * EQ + (NQ + 4 * (1 - RING)))
                load(0, 0, *order[0])
                sp.wait_ge(e_added, slots * 4 + 4)
            else:
                sp.wait_ge(x_added, 4 * last)
            sp.dma_start(out[0].rearrange("(t p) d -> p t d", p=P), xres[:, :, :]).then_inc(stored, 16)
            sp.wait_ge(stored, 16)

        def experts_pe(pe, three):
            pe.wait_ge(h_ready_dve, 4)
            for b in range(4):
                for kk in range(2):
                    for t in range(TB):
                        k = 2 * b + kk
                        at = kk * SEQ + t * P
                        mm = pe.transpose(bank[b][:, at:at + P], h[:, t, k * P:(k + 1) * P], ident)
                mm.then_inc(hT_turned, 1)
            pe.wait_ge(hT_lo_ready, 4 * KD)
            for t in range(TB):
                for k in range(KD):
                    cols = slice(t * P, (t + 1) * P)
                    mm = three(bank[4][:, t * N_EXP:(t + 1) * N_EXP], hT_hi[:, k, cols], hT_lo[:, k, cols],
                               aT_hi[:, 0, k * N_EXP:(k + 1) * N_EXP], aT_lo[:, 0, k * N_EXP:(k + 1) * N_EXP],
                               k == 0, k == KD - 1)
            mm.then_inc(logits_done, 1)
            pe.wait_ge(mask_ready, 1)
            mask = lambda t: route[:, 0, t * N_EXP:(t + 1) * N_EXP]
            tri = cst[:, C_TRI:C_TRI + P]
            pe.matmul(bank[5][:, 0:8], tri, mask(0), start=True, stop=True)
            pe.matmul(bank[5][:, 8:16], ones[:, :], mask(0), start=True, stop=False)
            pe.matmul(bank[5][:, 8:16], tri, mask(1), start=False, stop=True)
            pe.matmul(bank[5][:, 16:24], ones[:, :], mask(0), start=True, stop=False)
            pe.matmul(bank[5][:, 16:24], ones[:, :], mask(1), start=False, stop=True).then_inc(counted, 1)

            pe.wait_ge(route_ready, 1)
            over = pe.value_load(ids[0:1, 3:4], min_val=0, max_val=OVER)
            slots = over + N_EXP
            pe.wait_ge(slot_ready, 1)

            def gather():
                for k in range(KD):
                    for t in range(TB):
                        mm = pe.matmul(bank[2 + k // 4][:, (k % 4) * P:(k % 4 + 1) * P],
                                       h[:, t, k * P:(k + 1) * P], oh[:, t, 0:CAP],
                                       start=(t == 0), stop=(t == 1))
                    if k % 4 == 3:
                        mm.then_inc(gathered, 1)

            def quarter(s, q):
                kind, c = order[q // 4 % len(order)]
                j = q % 4
                place = (NQ + q) % SPLITS
                pe.wait_ge(lo_ready, s * EQ + (NQ + q + 1))
                for m in range(2):
                    at = m * NW
                    wh, wl = w_hi[:, place, at:at + NW], w_lo[:, place, at:at + NW]
                    if kind == "down":
                        half = slice(c % 2 * CAP, (c % 2 + 1) * CAP)
                        mm = three(bank[4 + m][:, :], aT_hi[:, j, half], aT_lo[:, j, half], wh, wl,
                                   c == 0 and j == 0, c == NCH - 1 and j == 3)
                    else:
                        k = 2 * j + m
                        b = 2 * (c % 2) + (kind == "up")
                        mm = three(bank[b][:, :], hT_hi[:, k, 0:CAP], hT_lo[:, k, 0:CAP], wh, wl,
                                   k == 0, k == KD - 1)
                mm.then_inc(quarter_used, 1)

            gather()
            pe.wait_ge(e_lo, 2)
            quarter(0, 0)
            with pe.Fori(0, slots) as s:
                def turn(c):
                    pe.wait_ge(e_hidden, s * NCH + (c + 1))
                    for b in range(4):
                        mm = pe.transpose(bank[6 + c % 2][:, b * P:(b + 1) * P],
                                          y[:, (c % 2) * NW + b * P:(c % 2) * NW + (b + 1) * P], ident)
                    mm.then_inc(e_turned, 1)

                for i, (kind, c) in enumerate(order):
                    if kind != "down" and c == 1:
                        pe.wait_ge(e_added, s * 4 + (1 + (kind == "up")))
                    if kind == "down":
                        pe.wait_ge(e_aT_lo, s * NCH + (c + 1))
                    for j in range(4):
                        if i or j:
                            quarter(s, 4 * i + j)
                        if kind == "down" and c == NCH - 2 and j == 1:
                            turn(NCH - 1)
                    if kind == "gate" and c == 0:
                        pe.wait_ge(slot_ready, s + 2)
                        pe.wait_ge(e_added, s * 4 + 4)
                        for t in range(TB):
                            mm = pe.transpose(bank[7][:, t * P:(t + 1) * P], oh[:, t, CAP:2 * CAP], ident)
                        mm.then_inc(weight_turned, 1)
                    if kind == "up" and c == NCH - 1:
                        gather()
                    if kind == "gate" and c:
                        if c == 2:
                            pe.wait_ge(wT_ready, s + 1)
                        turn(c - 1)
                pe.wait_ge(e_lo, s * 2 + 4)
                quarter(s, EQ)
                pe.wait_ge(y_act, s + 1)
                pe.wait_ge(y_dve, s + 1)
                for t in range(TB):
                    for half in range(2):
                        pe.matmul(bank[2 + 4 * t + half][:, :], wT[:, t, :],
                                  y[:, half * NW:(half + 1) * NW], start=True, stop=True).then_inc(combined, 1)

        @block.tensor
        def _(pe):
            def three(dst, hi, lo, whi, wlo, first, final):
                pe.matmul(dst, hi, whi, start=first, stop=False)
                pe.matmul(dst, lo, whi, start=False, stop=False)
                return pe.matmul(dst, hi, wlo, start=False, stop=final)

            def product(q, dst, s_hi, s_lo):
                n, k0, kn = quarters[q]
                p = pieces[n]
                pe.wait_ge(lo_ready, q + 1)
                for k in range(k0, k0 + kn):
                    for t in range(TB):
                        for o in range(0, p["n"], NW):
                            m = min(NW, p["n"] - o)
                            at = (k - k0) * p["n"] + o
                            mm = three(dst(t, o // NW)[:, 0:m], s_hi(k, t), s_lo(k, t),
                                       w_hi[:, q % SPLITS, at:at + m], w_lo[:, q % SPLITS, at:at + m],
                                       *flags(p, k))
                mm.then_inc(quarter_used, 1)
                return mm

            def flags(p, k):
                if p["kind"] != "down":
                    return k == 0, k == p["nk"] - 1
                lastc = max(x["c"] for x in pieces if x["kind"] == "down")
                return k == 0 and p["c"] == 0, k == p["nk"] - 1 and p["c"] == lastc

            def sT(buf):
                return lambda k, t: buf[:, k, t * P:(t + 1) * P]

            def turn_norm(n):
                pe.wait_ge(h_ready_dve, n + 1)
                pe.wait_ge(h_ready_act, n + 1)
                for b in range(4):
                    for kk in range(2):
                        for t in range(TB):
                            k = 2 * b + kk
                            at = kk * SEQ + t * P
                            mm = pe.transpose(bank[b][:, at:at + P], h[:, t, k * P:(k + 1) * P], ident)
                    mm.then_inc(hT_turned, 1)

            def projection(stage, s_hi, s_lo):
                for i, c in stage_lin(stage):
                    if i >= 2:
                        prev = lin[i - 2]
                        pe.wait_ge(copied_act, prev["na"])
                        pe.wait_ge(copied_dve, prev["nd"])
                    p = pieces[c["piece"]]
                    for q in range(p["q0"], p["q1"]):
                        product(q, lambda t, half: bank[4 + 2 * (i % 2) + t], s_hi, s_lo)

            def attention(g0, g1):
                for i in range(g0, g1 + 4):
                    if i < g1:
                        qs, ks, _, w = sources(i)
                        if i >= HEADS0:
                            pe.wait_ge(k_ready, i - HEADS0 + 1)
                        for j, src in enumerate((qs(0), qs(1), ks(0), ks(1))):
                            mm = pe.transpose(bank[i % 2][0:w, j * P:(j + 1) * P], src, ident)
                        mm.then_inc(qk_turned, 1)
                    j = i - 1
                    if g0 <= j < g1:
                        w = sources(j)[3]
                        pe.wait_ge(qkT_ready, j + 1)
                        if j >= 2:
                            pe.wait_ge(max_ready, j - 1)
                        s = bank[2 + j % 2]
                        buf = qkT[0:w, j % 2, :]
                        pe.matmul(s[:, 0:P], buf[:, 0:P], buf[:, SEQ:SEQ + P], start=True, stop=True)
                        pe.matmul(s[:, P:LANES], buf[:, P:SEQ], buf[:, SEQ:2 * SEQ], start=True, stop=True)\
                          .then_inc(scored, 1)
                    j = i - 3
                    if g0 <= j < g1:
                        pe.wait_ge(p_ready, j + 1)
                        for m in range(3):
                            mm = pe.transpose(bank[4 + j % 2][:, m * P:(m + 1) * P],
                                              pn[:, j % 2, m * P:(m + 1) * P], ident)
                        mm.then_inc(p_turned, 1)
                    j = i - 4
                    if g0 <= j < g1:
                        vs = sources(j)[2]
                        pe.wait_ge(pT_ready, j + 1)
                        if j >= 2:
                            pe.wait_ge(o_lo, j - 1)
                        o = o_psum(j)
                        pe.matmul(o, vs(0), pT[:, j % 2, 0:SEQ], start=True, stop=False)
                        pe.matmul(o[:, P:SEQ], vs(1), pT[:, j % 2, SEQ:LANES], start=False, stop=True)\
                          .then_inc(pv_done, 1)

            def ffn():
                chunks = max(pieces[n]["c"] for n in stage_pieces("ffn")) + 1
                width = [min(NW, D_FF - c * NW) for c in range(chunks)]

                def turn(c):
                    pe.wait_ge(hidden_ready, c + 1)
                    for b in range(width[c] // P):
                        for t in range(TB):
                            at = (b % 2) * SEQ + t * P
                            mm = pe.transpose(bank[2 * (c % 2) + b // 2][:, at:at + P],
                                              act_t[:, t, b * P:(b + 1) * P], ident)
                    mm.then_inc(hidden_turned, 1)

                for n in stage_pieces("ffn"):
                    p = pieces[n]
                    c = p["c"]
                    if p["kind"] == "gate" and c >= 1:
                        pe.wait_ge(hidden_ready, c)
                    if p["kind"] == "up" and c >= 1:
                        pe.wait_ge(aT_lo_ready, c)
                    if p["kind"] == "down":
                        if c == chunks - 1:
                            turn(c)
                        pe.wait_ge(aT_lo_ready, c + 1)
                    base = {"gate": 2 * (c % 2), "up": 2 - 2 * (c % 2), "down": 4}[p["kind"]]
                    for q in range(p["q0"], p["q1"]):
                        if p["kind"] == "down":
                            product(q, lambda t, half: bank[4 + 2 * t + half], sT(aT_hi), sT(aT_lo))
                        else:
                            product(q, lambda t, half: bank[base + t], sT(hT_hi), sT(hT_lo))
                    if p["kind"] == "up" and c == 0 or p["kind"] == "down" and c < chunks - 2:
                        turn(c if p["kind"] == "up" else c + 1)

            pe.wait_ge(consts_loaded, 16)
            pe.wait_ge(gains_loaded, 16 * 11)
            pe.transpose(bank[7][:, 0:35], g_rows[:, :], ident[0:35, 0:35]).then_inc(gains_turned, 1)

            turn_norm(0)
            pe.wait_ge(hT_lo_ready, KD)
            projection("in", sT(hT_hi), sT(hT_lo))
            pe.wait_ge(normed_dve, 1)
            pe.wait_ge(normed_pool, 1)
            attention(0, HEADS0)
            pe.wait_ge(o_lo, HEADS0)
            projection("out", sT(hT_hi), sT(hT_lo))
            if last >= 2:
                turn_norm(1)
                pe.wait_ge(hT_lo_ready, 2 * KD)
                ffn()
            if last >= 3:
                turn_norm(2)
                pe.wait_ge(hT_lo_ready, 3 * KD)
                projection("dq", sT(hT_hi), sT(hT_lo))
                projection("dkv", sT(hT_hi), sT(hT_lo))
                pe.wait_ge(lat_ready, 1)
                for k in range(5):
                    for t in range(TB):
                        src = lat[:, t, k * P:(k + 1) * P] if k < 3 else lkv[:, t, (k - 3) * P:(k - 2) * P]
                        mm = pe.transpose(bank[k // 2][:, (k % 2) * SEQ + t * P:(k % 2) * SEQ + (t + 1) * P],
                                          src, ident)
                mm.then_inc(lat_turned, 1)
                pe.wait_ge(lat_lo, 5)
                projection("uq", sT(aT_hi), sT(aT_lo))
                projection("ukv", lambda k, t: aT_hi[:, 3 + k, t * P:(t + 1) * P],
                           lambda k, t: aT_lo[:, 3 + k, t * P:(t + 1) * P])
                pe.wait_ge(normed_dve, 2)
                attention(HEADS0, HEADS)
                pe.wait_ge(o_lo, HEADS)
                projection("o", sT(hT_hi), sT(hT_lo))
            if last >= 4:
                experts_pe(pe, three)

        def experts_act(act, norm):
            act.wait_ge(gain_row_loaded, 32)
            act.activation(aT_hi[:, 0, 0:KD * N_EXP], router, ACT.Copy)\
               .then_inc(e_once, 1)
            norm(3)
            act.wait_ge(mask_ready, 1)
            act.activation(route[:, 13, 0:TB], route[:, 12, 0:TB], ACT.Exp).then_inc(e_once, 1)
            act.wait_ge(route_ready, 1)
            over = act.value_load(ids[0:1, 3:4], min_val=0, max_val=OVER)
            slots = over + N_EXP

            def take_gathered(first):
                for m in range(2):
                    act.wait_ge(gathered, first + m)
                    act.activation(hT_hi[:, 4 * m:4 * m + 4, 0:CAP],
                                   bank[2 + m][:, :].rearrange("p (a n) -> p a n", a=4), ACT.Copy)\
                       .then_inc(e_hi, 1)

            take_gathered(1)
            for q in range(LEAD - 1):
                if q == 0:
                    act.wait_ge(arrived[0], 16 * (uses[0] + 1))
                act.wait_ge(quarter_used, NQ + q - SPLITS + 1)
                act.activation(w_hi[:, (NQ + q) % SPLITS, :], ring[:, 0, q * QUARTER:(q + 1) * QUARTER], ACT.Copy)\
                   .then_inc(hi_ready, 1)
            with act.Fori(0, slots) as s:
                def split(q):
                    i, j = q // 4, q % 4
                    if j == 0:
                        turn = i // RING + 1
                        act.wait_ge(arrived[i % RING], s * (16 * len(order) // RING) + 16 * (uses[i % RING] + turn))
                    act.wait_ge(quarter_used, s * EQ + (NQ + q - SPLITS + 1))
                    act.activation(w_hi[:, (NQ + q) % SPLITS, :], ring[:, i % RING, j * QUARTER:(j + 1) * QUARTER],
                                   ACT.Copy).then_inc(hi_ready, 1)

                def turned(c):
                    act.wait_ge(e_turned, s * NCH + (c + 1))
                    act.activation(aT_hi[:, 0:4, c % 2 * CAP:(c % 2 + 1) * CAP], bank[6 + c % 2][:, :].rearrange("p (a n) -> p a n", a=4),
                                   ACT.Copy).then_inc(e_aT_hi, 1)

                for i, (kind, c) in enumerate(order):
                    for j in range(4):
                        if kind == "down" and c == NCH - 2 and j == 3:
                            turned(NCH - 1)
                        split(4 * i + j + LEAD - 1)
                    if kind == "gate":
                        act.wait_ge(quarter_used, s * EQ + (NQ + 4 * (i + 1)))
                        act.activation(gsf[:, (c % 2) * NW:(c % 2 + 1) * NW], bank[2 * (c % 2)][:, :], ACT.Silu)\
                           .then_inc(e_silu, 1)
                    if kind == "up" and c == NCH - 1:
                        take_gathered(s * 2 + 3)
                    if kind == "gate" and c:
                        turned(c - 1)
                act.wait_ge(quarter_used, s * EQ + (NQ + EQ))
                act.activation(y[:, 0:NW], bank[4][:, :], ACT.Copy).then_inc(y_act, 1)

        @block.scalar
        def _(act):
            for dst, keys in ((bias0, P), (bias1, 2 * P)):
                src = bass.AP(a["ev_b_rel_bias"].tensor, MAX_REL + 1 - P,
                              [[1, P], [2 * MAX_REL + 1, B_HEADS], [1, keys]])
                act.dma_start(dst, src).then_inc(braw_loaded, 16)
            act.dma_start(sinks[:, :], a["ev_a_sinks"].to_broadcast([P, A_HEADS])).then_inc(rows_loaded, 16)
            act.dma_start(gq[:, :], a["od_q_norm"].to_broadcast([P, C_QK])).then_inc(rows_loaded, 16)
            act.dma_start(gk[:, :], a["od_k_norm"].to_broadcast([P, C_QK])).then_inc(rows_loaded, 16)
            step = [0]

            def link(ins):
                step[0] += 1
                ins.then_inc(act_step, 1)
                act.wait_ge(act_step, step[0])

            split = [0]

            def split_to(q1):
                while split[0] < min(q1, NQ):
                    q = split[0]
                    n, k0, kn = quarters[q]
                    p = pieces[n]
                    if k0 == 0:
                        act.wait_ge(arrived[p["place"]], 16 * (p["turn"] + 1))
                    if q >= SPLITS:
                        act.wait_ge(quarter_used, q - SPLITS + 1)
                    m = kn * p["n"]
                    at = k0 * p["n"]
                    act.activation(w_hi[:, q % SPLITS, 0:m], ring[:, p["place"], at:at + m], ACT.Copy)\
                       .then_inc(hi_ready, 1)
                    split[0] += 1

            def norm(n):
                if n == 0:
                    act.wait_ge(x_loaded, 16)
                    act.wait_ge(ones_set, 1)
                else:
                    act.wait_ge(x_added, X_ADDS[n])
                for t in range(TB):
                    last_ = act.activation(h[:, t, :], xres[:, t, :], ACT.Square, accum_out=ss[:, t:t + 1])
                link(last_)
                act.activation(rt[:, 0:TB], ss[:, 0:TB], ACT.Sqrt, bias=eps[:, 0:1], scale=1.0 / D)\
                   .then_inc(norm_sqrt, 1)
                if n < 3:
                    act.wait_ge(rinv_ready, n + 1)
                    act.activation(h[:, 1, :], xres[:, 1, :], ACT.Copy, scale=rinv[:, 1:2])\
                       .then_inc(h_ready_act, 1)
                    if n == 0:
                        act.wait_ge(gain_cols_ready, 1)
                for k in range(KD):
                    if k % 2 == 0:
                        act.wait_ge(hT_turned, 4 * n + k // 2 + 1)
                    src = bank[k // 2][:, (k % 2) * SEQ:(k % 2 + 1) * SEQ]
                    gain = 1.0 if n == 3 else g_cols[:, g_fwd[n] + k:g_fwd[n] + k + 1]
                    act.activation(hT_hi[:, k, :], src, ACT.Copy, scale=gain).then_inc(hT_hi_ready, 1)

            def projection(stage):
                for i, c in stage_lin(stage):
                    p = pieces[c["piece"]]
                    for q in range(p["q0"], p["q1"]):
                        split_to(q + LEAD)
                    if not c["add"]:
                        act.wait_ge(quarter_used, p["q1"])
                        act.activation(dest[stage](0, c["j"], c["n"]), bank[4 + 2 * (i % 2)][:, 0:c["n"]],
                                       ACT.Copy).then_inc(copied_act, 1)

            def attention(g0, g1):
                act.wait_ge(rows_loaded, 48)
                for i in range(g0, g1 + 4):
                    if i < g1:
                        w = sources(i)[3]
                        q_col, k_col = ((G_AQ, G_AK) if i < A_HEADS else (G_BQ, G_BK) if i < HEADS0
                                        else (G_CQ, G_CK))
                        act.wait_ge(qk_turned, i + 1)
                        for at, col in ((0, q_col), (SEQ, k_col)):
                            o = act.activation(qkT[0:w, i % 2, at:at + SEQ], bank[i % 2][0:w, at:at + SEQ],
                                               ACT.Copy, scale=g_cols[0:w, col:col + 1])
                        o.then_inc(qkT_ready, 1)
                    j = i - 2
                    if g0 <= j < g1:
                        act.wait_ge(max_ready, j + 1)
                        b = j % 2
                        act.activation(sc[:, b, 0:P], sc[:, b, 0:P], ACT.Exp, bias=nmax[:, b, 0:1],
                                       accum_out=esum[:, b, 0:1])
                        e = act.activation(sc[:, b, P:LANES], sc[:, b, P:LANES], ACT.Exp, bias=nmax[:, b, 1:2],
                                           accum_out=esum[:, b, 1:2])
                        if j < A_HEADS:
                            e = act.activation(esum[:, b, 2:4], nmax[:, b, 0:2], ACT.Exp,
                                               bias=sinks[:, j:j + 1])
                        e.then_inc(exp_ready, 1)
                    j = i - 3
                    if g0 <= j < g1:
                        act.wait_ge(p_turned, j + 1)
                        act.activation(pT[:, j % 2, :], bank[4 + j % 2][:, 0:LANES], ACT.Copy)\
                           .then_inc(pT_ready, 1)
                    j = i - 4
                    if g0 <= j < g1:
                        act.wait_ge(pv_done, j + 1)
                        act.activation(o_place(hT_hi, j), o_psum(j), ACT.Copy).then_inc(o_hi, 1)

            def ffn():
                for n in stage_pieces("ffn"):
                    p = pieces[n]
                    c = p["c"]
                    if p["kind"] == "down" and p["q1"] == pieces[stage_pieces("ffn")[-1]]["q1"]:
                        turned(c)
                    for q in range(p["q0"], p["q1"]):
                        split_to(q + LEAD)
                    if p["kind"] == "gate":
                        act.wait_ge(quarter_used, p["q1"])
                        for t in range(TB):
                            s = act.activation(gs[:, t, 0:p["n"]], bank[2 * (c % 2) + t][:, 0:p["n"]], ACT.Silu)
                        s.then_inc(silu_ready, 1)
                    if p["kind"] == "up" and c == 0 or p["kind"] == "down" and c < ffn_chunks - 2:
                        turned(c if p["kind"] == "up" else c + 1)

            ffn_chunks = (D_FF + NW - 1) // NW

            def turned(c):
                act.wait_ge(hidden_turned, c + 1)
                for m in range(min(NW, D_FF - c * NW) // (2 * P)):
                    o = act.activation(aT_hi[:, 2 * m:2 * m + 2, :].rearrange("p a n -> p (a n)"),
                                       bank[2 * (c % 2) + m][:, :], ACT.Copy)
                o.then_inc(aT_hi_ready, 1)

            norm(0)
            projection("in")
            act.wait_ge(copied_dve, lin[stage_lin("in")[-1][0]]["nd"])
            act.wait_ge(copied_act, lin[stage_lin("in")[-1][0]]["na"])
            for t in range(TB):
                j0, j1 = (hf[:, 0:640], hf[:, 640:1664]) if t == 0 else (gsf[:, 0:640], y[:, 0:1024])
                act.activation(j0, proj[:, t, 0:A_V], ACT.Square).then_inc(squared, 1)
                act.activation(j1, proj[:, t, B_Q:B_V], ACT.Square).then_inc(squared, 1)
            act.wait_ge(head_ss, 1)
            act.activation(rt[:, 0:52], ss[:, 0:52], ACT.Sqrt, bias=eps[:, 0:1], scale=1.0 / HD)\
               .then_inc(head_sqrt, 1)
            attention(0, HEADS0)
            projection("out")
            if last >= 2:
                norm(1)
                ffn()
            if last >= 3:
                norm(2)
                projection("dq")
                projection("dkv")
                act.wait_ge(copied_dve, lin[stage_lin("dkv")[-1][0]]["nd"])
                act.wait_ge(copied_act, lin[stage_lin("dkv")[-1][0]]["na"])
                for t in range(TB):
                    act.activation(hf[:, 0:Q_LORA], lat[:, t, :], ACT.Square, accum_out=ss[:, 2 + t:3 + t])
                    link(act.activation(hf[:, 384:384 + KV_LORA], lkv[:, t, 0:KV_LORA], ACT.Square,
                                        accum_out=ss[:, 4 + t:5 + t]))
                    link(act.activation(hf[:, 0:C_ROPE], lkv[:, t, KV_LORA:], ACT.Square,
                                        accum_out=ss[:, 64 + t:65 + t]))
                act.activation(rt[:, 2:4], ss[:, 2:4], ACT.Sqrt, bias=eps[:, 0:1], scale=1.0 / Q_LORA)
                act.activation(rt[:, 4:6], ss[:, 4:6], ACT.Sqrt, bias=eps[:, 0:1], scale=1.0 / KV_LORA)\
                   .then_inc(lat_ss, 1)
                act.wait_ge(lat_turned, 1)
                for k in range(5):
                    col = G_QA + k
                    act.activation(aT_hi[:, k, :], bank[k // 2][:, (k % 2) * SEQ:(k % 2 + 1) * SEQ], ACT.Copy,
                                   scale=g_cols[:, col:col + 1]).then_inc(lat_hi, 1)
                projection("uq")
                projection("ukv")
                act.wait_ge(copied_dve, lin[stage_lin("ukv")[-1][0]]["nd"])
                act.wait_ge(copied_act, lin[stage_lin("ukv")[-1][0]]["na"])
                act.wait_ge(lat_lo, 5)
                for t in range(TB):
                    if t:
                        act.wait_ge(head_ss, 2)
                    act.activation(hf[:, 0:1536], qc[:, t, :], ACT.Square).then_inc(squared, 1)
                    nope = kv[:, t, :].rearrange("p (h n) -> p h n", h=C_HEADS)[:, :, 0:C_NOPE]
                    act.activation(acf[:, 0:1024].rearrange("p (h n) -> p h n", h=C_HEADS), nope, ACT.Square)\
                       .then_inc(squared, 1)
                act.wait_ge(head_ss, 3)
                act.activation(rt[:, 0:64], ss[:, 0:64], ACT.Sqrt, bias=eps[:, 0:1], scale=1.0 / C_QK)\
                   .then_inc(head_sqrt, 1)
                attention(HEADS0, HEADS)
                projection("o")
            if last >= 4:
                experts_act(act, norm)

        def experts_dve(dve, norm, link):
            R = lambda i: route[:, i, :].rearrange("p (t e) -> p t e", e=N_EXP)
            dve.wait_ge(e_once, 1)
            dve.tensor_tensor(aT_lo[:, 0, 0:KD * N_EXP], router, aT_hi[:, 0, 0:KD * N_EXP].bitcast(F32), ALU.subtract)
            norm(3)
            dve.wait_ge(logits_done, 1)
            link(dve.tensor_copy(route[:, 1, :], bank[4][:, 0:TB * N_EXP]))
            below = cst[:, C_IOTA:C_IOTA + N_EXP].unsqueeze(1).to_broadcast([P, TB, N_EXP])
            link(dve.tensor_scalar(R(14), below, -float(N_EXP), None, ALU.add))
            wide = lambda v: v.unsqueeze(2).to_broadcast([P, TB, N_EXP])
            for n, (src, hot, top) in enumerate(((1, 2, 10), (3, 4, 11))):
                m = route[:, top, 0:TB]
                first = route[:, top, TB:2 * TB]
                link(dve.tensor_reduce(m, R(src), AX.X, ALU.max))
                link(dve.tensor_tensor(R(5), R(src), wide(m), ALU.is_equal))
                link(dve.tensor_tensor(R(5), R(5), R(14), ALU.mult))
                link(dve.tensor_reduce(first, R(5), AX.X, ALU.min))
                link(dve.tensor_tensor(R(hot), R(14), wide(first), ALU.is_equal))
                if n == 0:
                    link(dve.scalar_tensor_tensor(R(3), R(2), -3e38, R(1), ALU.mult, ALU.add))
            dve.tensor_tensor(R(0), R(2), R(4), ALU.add)
            dve.tensor_tensor(route[:, 12, 0:TB], route[:, 11, 0:TB], route[:, 10, 0:TB], ALU.subtract)\
               .then_inc(mask_ready, 1)
            dve.wait_ge(e_once, 2)
            w1, w2 = route[:, 15, 0:TB], route[:, 15, TB:2 * TB]
            link(dve.tensor_scalar(w1, route[:, 13, 0:TB], 1.0, None, ALU.add))
            link(dve.reciprocal(w1, w1))
            link(dve.tensor_tensor(w2, route[:, 13, 0:TB], w1, ALU.mult))
            dve.tensor_tensor(R(6), R(2), wide(w1), ALU.mult)
            link(dve.tensor_tensor(R(7), R(4), wide(w2), ALU.mult))
            link(dve.tensor_tensor(R(6), R(6), R(7), ALU.add))
            dve.wait_ge(counted, 1)
            link(dve.tensor_tensor(R(8), bank[5][:, 0:TB * N_EXP].rearrange("p (t e) -> p t e", e=N_EXP), R(0),
                                   ALU.mult))
            link(dve.tensor_tensor(R(8), R(8), R(0), ALU.add))
            link(dve.tensor_scalar(R(8), R(8), -1.0, None, ALU.add))
            link(dve.tensor_copy(cnt[:, 0, :], bank[5][:, 16:24]))
            link(dve.tensor_scalar(cnt[:, 1, :], cnt[:, 0, :], float(CAP) + 0.5, None, ALU.is_gt))
            link(dve.memset(cnt[:, 2, :], 0.0))
            for e in range(1, N_EXP):
                link(dve.tensor_tensor(cnt[:, 2, e:e + 1], cnt[:, 2, e - 1:e], cnt[:, 1, e - 1:e], ALU.add))
            dve.tensor_copy(pos_t[:, :, 0:N_EXP], R(8))
            dve.memset(pos_t[:, :, SLOTS:], -1.0)
            dve.tensor_copy(gate_t[:, :, 0:N_EXP], R(6))
            for o in range(OVER):
                link(dve.tensor_scalar(cnt[:, 3, :], cnt[:, 2, :], float(o), None, ALU.is_equal))
                link(dve.tensor_tensor(cnt[:, 3, :], cnt[:, 3, :], cnt[:, 1, :], ALU.mult))
                pick = cnt[:, 3, :].unsqueeze(1).to_broadcast([P, TB, N_EXP])
                link(dve.scalar_tensor_tensor(R(9), R(8), 1.0 - CAP, pick, ALU.add, ALU.mult))
                link(dve.tensor_reduce(pos_t[:, :, N_EXP + o], R(9), AX.X, ALU.add))
                link(dve.tensor_scalar(pos_t[:, :, N_EXP + o], pos_t[:, :, N_EXP + o],
                                       -1.0, None, ALU.add))
                link(dve.tensor_tensor(R(9), R(6), pick, ALU.mult))
                link(dve.tensor_reduce(gate_t[:, :, N_EXP + o], R(9), AX.X, ALU.add))
                link(dve.tensor_tensor(cnt[:, 3, :], cnt[:, 3, :], cst[:, C_IOTA:C_IOTA + N_EXP], ALU.mult))
                link(dve.tensor_reduce(ids_f[:, o:o + 1], cnt[:, 3, :], AX.X, ALU.add))
            link(dve.tensor_reduce(ids_f[:, 3:4], cnt[:, 1, :], AX.X, ALU.add))
            dve.tensor_copy(ids[0:1, :], ids_f[0:1, :]).then_inc(route_ready, 1)
            dve.wait_ge(route_ready, 1)
            over = dve.value_load(ids[0:1, 3:4], min_val=0, max_val=OVER)
            slots = over + N_EXP
            iota = cst[:, C_IOTA:C_IOTA + CAP]
            for t in range(TB):
                o = dve.tensor_scalar(oh[:, t, 0:CAP], iota, pos_t[:, t, 0:1], None, ALU.is_equal)
            o.then_inc(slot_ready, 1)

            def take_gathered(first):
                for m in range(2):
                    dve.wait_ge(e_hi, first + m)
                    dve.tensor_tensor(hT_lo[:, 4 * m:4 * m + 4, 0:CAP],
                                      bank[2 + m][:, :].rearrange("p (a n) -> p a n", a=4),
                                      hT_hi[:, 4 * m:4 * m + 4, 0:CAP].bitcast(F32), ALU.subtract).then_inc(e_lo, 1)

            take_gathered(1)
            for q in range(LEAD - 1):
                dve.wait_ge(hi_ready, NQ + q + 1)
                place = (NQ + q) % SPLITS
                dve.tensor_tensor(w_lo[:, place, :], ring[:, 0, q * QUARTER:(q + 1) * QUARTER],
                                  w_hi[:, place, :].bitcast(F32), ALU.subtract).then_inc(lo_ready, 1)
            dve.memset(ids_f[:, 0:1], 0.0).then_inc(e_added, 4)
            with dve.Fori(0, slots) as s:
                def split(q):
                    i, j = q // 4, q % 4
                    place = (NQ + q) % SPLITS
                    dve.wait_ge(hi_ready, s * EQ + (NQ + q + 1))
                    dve.tensor_tensor(w_lo[:, place, :], ring[:, i % RING, j * QUARTER:(j + 1) * QUARTER],
                                      w_hi[:, place, :].bitcast(F32), ALU.subtract).then_inc(lo_ready, 1)

                def turned(c):
                    dve.wait_ge(e_aT_hi, s * NCH + (c + 1))
                    half = slice(c % 2 * CAP, (c % 2 + 1) * CAP)
                    dve.tensor_tensor(aT_lo[:, 0:4, half], bank[6 + c % 2][:, :].rearrange("p (a n) -> p a n", a=4),
                                      aT_hi[:, 0:4, half].bitcast(F32), ALU.subtract).then_inc(e_aT_lo, 1)

                dve.tensor_copy(cur[:, 0, :].unsqueeze(2), pos_t[:, :, bass.ds(s, 1)])
                dve.tensor_copy(cur[:, 1, :].unsqueeze(2), gate_t[:, :, bass.ds(s, 1)])
                dve.tensor_copy(cur[:, 2, :].unsqueeze(2), pos_t[:, :, bass.ds(s + 1, 1)]).then_inc(cur_ready, 1)
                dve.wait_ge(cur_ready, s + 1)
                for t in range(TB):
                    dve.tensor_scalar(oh[:, t, CAP:2 * CAP], iota, cur[:, 0, t:t + 1], cur[:, 1, t:t + 1],
                                      ALU.is_equal, ALU.mult)
                    o = dve.tensor_scalar(oh[:, t, 0:CAP], iota, cur[:, 2, t:t + 1], None, ALU.is_equal)
                o.then_inc(slot_ready, 1)
                for i, (kind, c) in enumerate(order):
                    for j in range(4):
                        if kind == "down" and c == NCH - 2 and j == 3:
                            turned(NCH - 1)
                        split(4 * i + j + LEAD - 1)
                    if kind == "up":
                        dve.wait_ge(quarter_used, s * EQ + (NQ + 4 * (i + 1)))
                        dve.wait_ge(e_silu, s * NCH + (c + 1))
                        at = slice((c % 2) * NW, (c % 2 + 1) * NW)
                        dve.tensor_tensor(y[:, at], gsf[:, at], bank[2 * (c % 2) + 1][:, :], ALU.mult)\
                           .then_inc(e_hidden, 1)
                    if kind == "gate" and c == 0:
                        dve.wait_ge(weight_turned, s + 1)
                        dve.tensor_copy(wT, bank[7][:, 0:SEQ].rearrange("p (t n) -> p t n", t=TB))\
                           .then_inc(wT_ready, 1)
                    if kind == "up" and c == NCH - 1:
                        take_gathered(s * 2 + 3)
                    if kind == "gate" and c:
                        turned(c - 1)
                dve.wait_ge(quarter_used, s * EQ + (NQ + EQ))
                dve.tensor_copy(y[:, NW:2 * NW], bank[5][:, :]).then_inc(y_dve, 1)
                for t in range(TB):
                    for half in range(2):
                        xs = xres[:, t, half * NW:(half + 1) * NW]
                        dve.wait_ge(combined, s * 4 + (2 * t + half + 1))
                        dve.tensor_tensor(xs, xs, bank[2 + 4 * t + half][:, :], ALU.add).then_inc(e_added, 1)

        @block.vector
        def _(dve):
            step = [0]

            def link(ins):
                step[0] += 1
                ins.then_inc(dve_step, 1)
                dve.wait_ge(dve_step, step[0])

            split = [0]

            def split_to(q1):
                while split[0] < min(q1, NQ):
                    q = split[0]
                    n, k0, kn = quarters[q]
                    p = pieces[n]
                    m = kn * p["n"]
                    at = k0 * p["n"]
                    dve.wait_ge(hi_ready, q + 1)
                    dve.tensor_tensor(w_lo[:, q % SPLITS, 0:m], ring[:, p["place"], at:at + m],
                                      w_hi[:, q % SPLITS, 0:m].bitcast(F32), ALU.subtract).then_inc(lo_ready, 1)
                    split[0] += 1

            def norm(n):
                dve.wait_ge(norm_sqrt, n + 1)
                dve.reciprocal(rinv[:, 0:TB], rt[:, 0:TB]).then_inc(rinv_ready, 1)
                dve.wait_ge(rinv_ready, n + 1)
                if n < 3:
                    dve.tensor_scalar(h[:, 0, :], xres[:, 0, :], rinv[:, 0:1], None, ALU.mult)\
                       .then_inc(h_ready_dve, 1)
                else:
                    dve.wait_ge(gain_row_loaded, 32)
                    for t in range(TB):
                        o = dve.scalar_tensor_tensor(h[:, t, :], xres[:, t, :], rinv[:, t:t + 1], acf[:, 0:D],
                                                     ALU.mult, ALU.mult)
                    o.then_inc(h_ready_dve, 1)
                if n == 0:
                    dve.wait_ge(gains_turned, 1)
                    link(dve.tensor_copy(g_cols[:, :], bank[7][:, 0:35]))
                    dve.tensor_scalar(g_cols[:, G_AQ:G_AQ + 1], g_cols[:, G_AQ:G_AQ + 1], HD ** -0.5, None, ALU.mult)
                    dve.tensor_scalar(g_cols[:, G_BQ:G_BQ + 1], g_cols[:, G_BQ:G_BQ + 1], HD ** -0.5, None, ALU.mult)\
                       .then_inc(gain_cols_ready, 1)
                    dve.wait_ge(gain_cols_ready, 1)
                for k in range(KD):
                    dve.wait_ge(hT_hi_ready, KD * n + 2 * (k // 2) + 2)
                    src = bank[k // 2][:, (k % 2) * SEQ:(k % 2 + 1) * SEQ]
                    hi = hT_hi[:, k, :].bitcast(F32)
                    if n == 3:
                        o = dve.tensor_tensor(hT_lo[:, k, :], src, hi, ALU.subtract)
                    else:
                        o = dve.scalar_tensor_tensor(hT_lo[:, k, :], src, g_cols[:, g_fwd[n] + k:g_fwd[n] + k + 1],
                                                     hi, ALU.mult, ALU.subtract)
                    o.then_inc(hT_lo_ready, 1)

            def projection(stage):
                for i, c in stage_lin(stage):
                    p = pieces[c["piece"]]
                    for q in range(p["q0"], p["q1"]):
                        split_to(q + LEAD)
                    dve.wait_ge(quarter_used, p["q1"])
                    if not c["add"]:
                        dve.tensor_copy(dest[stage](1, c["j"], c["n"]), bank[5 + 2 * (i % 2)][:, 0:c["n"]])\
                           .then_inc(copied_dve, 1)
                    else:
                        for t in range(TB):
                            xs = xres[:, t, c["j"] * NW:(c["j"] + 1) * NW]
                            dve.tensor_tensor(xs, xs, bank[4 + 2 * (i % 2) + t][:, :], ALU.add).then_inc(x_added, 1)

            def attention(g0, g1):
                dve.wait_ge(rows_loaded, 48)
                for i in range(g0, g1 + 4):
                    j = i - 3
                    if g0 <= j < g1:
                        b = j % 2
                        dve.wait_ge(exp_ready, j + 1)
                        if j >= 2:
                            dve.wait_ge(p_turned, j - 1)
                        if j < A_HEADS:
                            link(dve.tensor_tensor(esum[:, b, 0:2], esum[:, b, 0:2], esum[:, b, 2:4], ALU.add))
                        link(dve.reciprocal(den[:, b, :], esum[:, b, 0:2]))
                        dve.tensor_scalar(pn[:, b, 0:P], sc[:, b, 0:P], den[:, b, 0:1], None, ALU.mult)
                        dve.tensor_scalar(pn[:, b, P:LANES], sc[:, b, P:LANES], den[:, b, 1:2], None, ALU.mult)\
                           .then_inc(p_ready, 1)
                    j = i - 1
                    if g0 <= j < g1:
                        b = j % 2
                        if j >= 2:
                            dve.wait_ge(p_ready, j - 1)
                        dve.wait_ge(scored, j + 1)
                        s = bank[2 + b][:, 0:LANES]
                        if j < A_HEADS:
                            o = dve.scalar_tensor_tensor(sc[:, b, :], cst[:, C_DIST:C_DIST + LANES],
                                                         2.0 ** (-8.0 * (j + 1) / A_HEADS), s, ALU.mult, ALU.add)
                        elif j < HEADS0:
                            dve.wait_ge(bias_ready, 1)
                            hb = j - A_HEADS
                            dve.tensor_tensor(sc[:, b, 0:P], s[:, 0:P], bias0[:, hb, ::-1], ALU.add)
                            o = dve.tensor_tensor(sc[:, b, P:], s[:, P:], bias1[:, hb, ::-1], ALU.add)
                        else:
                            o = dve.scalar_tensor_tensor(sc[:, b, :], s, C_QK ** -0.5,
                                                         cst[:, C_MASK:C_MASK + LANES], ALU.mult, ALU.add)
                        link(o)
                        dve.tensor_reduce(mx[:, b, 0:1], sc[:, b, 0:P], AX.X, ALU.max)
                        link(dve.tensor_reduce(mx[:, b, 1:2], sc[:, b, P:LANES], AX.X, ALU.max))
                        if j < A_HEADS:
                            link(dve.tensor_scalar(mx[:, b, :], mx[:, b, :], sinks[:, j:j + 1], None, ALU.max))
                        dve.tensor_scalar(nmax[:, b, 0:2], mx[:, b, :], -1.0, None, ALU.mult).then_inc(max_ready, 1)
                    j = i - 4
                    if g0 <= j < g1:
                        dve.wait_ge(o_hi, j + 1)
                        dve.tensor_tensor(o_place(hT_lo, j), o_psum(j), o_place(hT_hi, j).bitcast(F32),
                                          ALU.subtract).then_inc(o_lo, 1)

            ffn_chunks = (D_FF + NW - 1) // NW

            def turned(c):
                dve.wait_ge(aT_hi_ready, c + 1)
                for m in range(min(NW, D_FF - c * NW) // (2 * P)):
                    two = lambda b: b[:, 2 * m:2 * m + 2, :].rearrange("p a n -> p (a n)")
                    o = dve.tensor_tensor(two(aT_lo), bank[2 * (c % 2) + m][:, :], two(aT_hi).bitcast(F32),
                                          ALU.subtract)
                o.then_inc(aT_lo_ready, 1)

            def ffn():
                for n in stage_pieces("ffn"):
                    p = pieces[n]
                    c = p["c"]
                    if p["kind"] == "down" and n == stage_pieces("ffn")[-1]:
                        turned(c)
                    for q in range(p["q0"], p["q1"]):
                        split_to(q + LEAD)
                    if p["kind"] == "up":
                        dve.wait_ge(quarter_used, p["q1"])
                        dve.wait_ge(silu_ready, c + 1)
                        for t in range(TB):
                            o = dve.tensor_tensor(act_t[:, t, 0:p["n"]], gs[:, t, 0:p["n"]],
                                                  bank[2 - 2 * (c % 2) + t][:, 0:p["n"]], ALU.mult)
                        o.then_inc(hidden_ready, 1)
                    if p["kind"] == "up" and c == 0 or p["kind"] == "down" and c < ffn_chunks - 2:
                        turned(c if p["kind"] == "up" else c + 1)
                dve.wait_ge(quarter_used, p["q1"])
                for t in range(TB):
                    for half in range(2):
                        xs = xres[:, t, half * NW:(half + 1) * NW]
                        dve.tensor_tensor(xs, xs, bank[4 + 2 * t + half][:, :], ALU.add).then_inc(x_added, 1)

            dve.memset(eps[:, :], EPS)
            dve.memset(ones[:, :], 1.0).then_inc(ones_set, 1)
            dve.wait_ge(x_loaded, 16)
            dve.wait_ge(consts_loaded, 16)
            norm(0)
            projection("in")
            for t in range(TB):
                j0, j1 = (hf[:, 0:640], hf[:, 640:1664]) if t == 0 else (gsf[:, 0:640], y[:, 0:1024])
                dve.wait_ge(squared, 2 * t + 1)
                dve.tensor_reduce(ss[:, 26 * t:26 * t + 10], j0.rearrange("p (h n) -> p h n", n=HD), AX.X, ALU.add)
                dve.wait_ge(squared, 2 * t + 2)
                o = dve.tensor_reduce(ss[:, 26 * t + 10:26 * t + 26], j1.rearrange("p (h n) -> p h n", n=HD),
                                      AX.X, ALU.add)
            o.then_inc(head_ss, 1)
            dve.wait_ge(head_sqrt, 1)
            dve.reciprocal(rinv[:, 0:52], rt[:, 0:52]).then_inc(head_rinv, 1)
            dve.wait_ge(head_rinv, 1)
            for c0, hs, r0 in ((A_Q, 10, 0), (B_Q, 16, 10)):
                v = proj[:, 0, c0:c0 + hs * HD].rearrange("p (h n) -> p h n", n=HD)
                o = dve.tensor_tensor(v, v, rinv[:, r0:r0 + hs].unsqueeze(2).to_broadcast([P, hs, HD]), ALU.mult)
            o.then_inc(normed_dve, 1)
            attention(0, HEADS0)
            projection("out")
            if last >= 2:
                norm(1)
                ffn()
            if last >= 3:
                norm(2)
                projection("dq")
                projection("dkv")
                dve.wait_ge(lat_ss, 1)
                dve.reciprocal(rinv[:, 2:6], rt[:, 2:6]).then_inc(lat_rinv, 1)
                dve.wait_ge(lat_rinv, 1)
                for t in range(TB):
                    dve.tensor_scalar(lat[:, t, :], lat[:, t, :], rinv[:, 2 + t:3 + t], None, ALU.mult)
                    o = dve.tensor_scalar(lkv[:, t, 0:KV_LORA], lkv[:, t, 0:KV_LORA], rinv[:, 4 + t:5 + t], None,
                                          ALU.mult)
                o.then_inc(lat_ready, 1)
                for t in range(TB):
                    cos, sin = (cst[:, C_ROT + 64 * t + c:C_ROT + 64 * t + c + 16] for c in (0, C_ROPE))
                    src = lkv[:, t, KV_LORA:]
                    dve.wait_ge(gains_loaded, 16 * 11)
                    link(dve.tensor_tensor(src, src, gk[:, C_NOPE:], ALU.mult))
                    k1, k2 = src[:, 0:16], src[:, 16:32]
                    for m, (u, v) in enumerate(((k1, cos), (k2, sin), (k2, cos), (k1, sin))):
                        o = dve.tensor_tensor(kr_t[:, m, :], u, v, ALU.mult)
                    link(o)
                    dve.tensor_tensor(kr[:, t, 0:16], kr_t[:, 0, :], kr_t[:, 1, :], ALU.subtract)
                    link(dve.tensor_tensor(kr[:, t, 16:32], kr_t[:, 2, :], kr_t[:, 3, :], ALU.add))
                for k in range(5):
                    dve.wait_ge(lat_hi, min(5, 2 * (k // 2) + 2))
                    col = G_QA + k
                    dve.scalar_tensor_tensor(aT_lo[:, k, :], bank[k // 2][:, (k % 2) * SEQ:(k % 2 + 1) * SEQ],
                                             g_cols[:, col:col + 1], aT_hi[:, k, :].bitcast(F32), ALU.mult,
                                             ALU.subtract).then_inc(lat_lo, 1)
                projection("uq")
                projection("ukv")
                for t in range(TB):
                    dve.wait_ge(squared, 4 + 2 * t + 1)
                    dve.tensor_reduce(ss[:, 16 * t:16 * t + 16],
                                      hf[:, 0:1536].rearrange("p (h n) -> p h n", n=C_QK), AX.X, ALU.add)
                    dve.wait_ge(squared, 4 + 2 * t + 2)
                    link(dve.tensor_reduce(ss[:, 32 + 16 * t:48 + 16 * t],
                                           acf[:, 0:1024].rearrange("p (h n) -> p h n", n=C_NOPE), AX.X, ALU.add))
                    dve.tensor_scalar(ss[:, 32 + 16 * t:48 + 16 * t], ss[:, 32 + 16 * t:48 + 16 * t],
                                      ss[:, 64 + t:65 + t], None, ALU.add).then_inc(head_ss, 1)
                dve.wait_ge(head_sqrt, 2)
                dve.reciprocal(rinv[:, 0:64], rt[:, 0:64]).then_inc(head_rinv, 1)
                dve.wait_ge(head_rinv, 2)
                half = C_ROPE // 2
                for t in range(TB):
                    v = qc[:, t, :].rearrange("p (h n) -> p h n", n=C_QK)
                    link(dve.tensor_tensor(v, v, rinv[:, 16 * t:16 * t + 16].unsqueeze(2).to_broadcast(
                        [P, C_HEADS, C_QK]), ALU.mult))
                    vr = v[:, :, C_NOPE:]
                    link(dve.tensor_tensor(vr, vr, gq[:, C_NOPE:].unsqueeze(1).to_broadcast([P, C_HEADS, C_ROPE]),
                                           ALU.mult))
                    cos, sin = (cst[:, C_ROT + 64 * t + c:C_ROT + 64 * t + c + 16].unsqueeze(1).to_broadcast(
                        [P, C_HEADS, half]) for c in (0, C_ROPE))
                    q1, q2 = v[:, :, C_NOPE:C_NOPE + half], v[:, :, C_NOPE + half:]
                    tmp = acf[:, :].rearrange("p (m h n) -> p m h n", m=4, h=C_HEADS)
                    for m, (u, w) in enumerate(((q1, cos), (q2, sin), (q2, cos), (q1, sin))):
                        o = dve.tensor_tensor(tmp[:, m], u, w, ALU.mult)
                    link(o)
                    dve.tensor_tensor(q1, tmp[:, 0], tmp[:, 1], ALU.subtract)
                    o = dve.tensor_tensor(q2, tmp[:, 2], tmp[:, 3], ALU.add)
                    if t == 0:
                        link(o)
                o.then_inc(normed_dve, 1)
                attention(HEADS0, HEADS)
                projection("o")
            if last >= 4:
                experts_dve(dve, norm, link)

        @block.gpsimd
        def _(pool):
            pool.memset(g_rows[:, :], 1.0).then_inc(rows_cleared, 1)
            pool.wait_ge(consts_loaded, 16)
            pool.wait_ge(braw_loaded, 32)
            for raw, c0, keys in ((bias0, C_MASK, P), (bias1, C_MASK + P, 2 * P)):
                m = cst[:, c0:c0 + keys][:, ::-1].unsqueeze(1).to_broadcast([P, B_HEADS, keys])
                o = pool.tensor_tensor(raw, raw, m, ALU.add)
            o.then_inc(bias_ready, 1)

            pool.wait_ge(head_rinv, 1)
            for c0, hs, r0 in ((A_Q, 10, 26), (B_Q, 16, 36)):
                v = proj[:, 1, c0:c0 + hs * HD].rearrange("p (h n) -> p h n", n=HD)
                o = pool.tensor_tensor(v, v, rinv[:, r0:r0 + hs].unsqueeze(2).to_broadcast([P, hs, HD]), ALU.mult)
            o.then_inc(normed_pool, 1)
            if last >= 3:
                def make_k(c):
                    if c >= KBUFS:
                        pool.wait_ge(qk_turned, HEADS0 + c - KBUFS + 1)
                    b = (HEADS0 + c) % KBUFS
                    for t in range(TB):
                        r = rinv[:, 32 + 16 * t + c:33 + 16 * t + c]
                        pool.tensor_scalar(kbuf[:, b, t, 0:C_NOPE], kv[:, t, c * 128:c * 128 + C_NOPE], r, None,
                                           ALU.mult)
                        o = pool.tensor_scalar(kbuf[:, b, t, C_NOPE:], kr[:, t, :], r, None, ALU.mult)
                    o.then_inc(k_ready, 1)

                pool.wait_ge(rows_loaded, 48)
                pool.wait_ge(head_rinv, 2)
                for c in range(C_HEADS):
                    make_k(c)
            if last >= 4:
                pool.wait_ge(pv_done, HEADS)
                pool.dma_start(acf[:, 0:D], a["od_ffn_norm"].to_broadcast([P, D])).then_inc(gain_row_loaded, 16)
                pool.dma_start(router.rearrange("p (k e) -> p k e", e=N_EXP),
                               a["od_router"][0].rearrange("(k p) e -> p k e", p=P)).then_inc(gain_row_loaded, 16)

    return


_INS = ["x", "ev_attn_norm", "ev_w_in", "ev_a_q_norm", "ev_a_k_norm", "ev_a_sinks", "ev_b_q_norm", "ev_b_k_norm",
        "ev_b_rel_bias", "ev_w_out", "ev_ffn_norm", "ev_w_gate", "ev_w_up", "ev_w_down", "od_attn_norm", "od_w_dq",
        "od_q_a_norm", "od_w_uq", "od_w_dkv", "od_kv_a_norm", "od_w_ukv", "od_q_norm", "od_k_norm", "od_w_o",
        "od_ffn_norm", "od_router", "od_e_gate", "od_e_up", "od_e_down"]


def kernel(**inputs):
    import concourse.bacc as _bacc
    from concourse.bass_utils import run_bass_kernel_spmd as _run

    nc = _bacc.Bacc("TRN2", target_bir_lowering=False, num_devices=1)
    arrays, args = {}, {}
    given = {name: np.ascontiguousarray(inputs[name]) for name in _INS}
    given["const"] = constants()
    for name, v in given.items():
        arrays[f"in_{name}_dram"] = v
        args[name] = nc.dram_tensor(f"in_{name}_dram", v.shape, mybir.dt.from_np(v.dtype), kind="ExternalInput").ap()
    out = nc.dram_tensor("out_0_dram", (1, SEQ, D), F32, kind="ExternalOutput").ap()
    trunk(nc, args, out)
    r = _run(nc, [arrays], core_ids=[0])
    return r.results[0]["out_0_dram"]
```

```python
from contextlib import ExitStack

import numpy as np

import concourse.bass as bass
from concourse import mybir

ALU = mybir.AluOpType
ACT = mybir.ActivationFunctionType
AX = mybir.AxisListType
F32 = mybir.dt.float32
F32R = mybir.dt.float32r
I32 = mybir.dt.int32

P = 128
D = 1024
KD = D // P
SEQ = 256
TB = SEQ // P
CHUNK = 64
EPS = 1e-6
NEG = -1e30
HD = 64
A_HEADS, A_KV, B_HEADS = 8, 2, 8
IN_W = 2304
MAX_REL = 256
C_HEADS, C_NOPE, C_ROPE, C_V = 16, 64, 32, 64
C_QK = C_NOPE + C_ROPE
Q_LORA, KV_LORA = 384, 256
D_FF = 2816
N_EXP = 8
E_FF = 3584
CAP = 128
OVER = 3
SLOTS = N_EXP + OVER
NW = 512
RING = 7
PIECE = KD * NW
SPLITS = 4
QUARTER = PIECE // 4
LEAD = SPLITS
HEADS0 = A_HEADS + B_HEADS
HEADS = HEADS0 + C_HEADS
KBUFS = 4
LANES = 128 + 256

A_Q, A_K, A_V, B_Q, B_K, B_V = 0, 512, 640, 768, 1280, 1792
C_ID, C_TRI, C_IOTA, C_DIST, C_MASK, C_ROT = 0, 128, 256, 384, 768, 1152
C_ALL = C_ROT + TB * 2 * C_ROPE


G_FWD = {0: 0, 1: KD, 2: 2 * KD, 3: 3 * KD}
G_QA = 4 * KD
G_KVA = G_QA + Q_LORA // P
G_AQ = G_KVA + KV_LORA // P
G_AK, G_BQ, G_BK, G_CQ, G_CK = (G_AQ + i for i in range(1, 6))
G_ALL = G_CK + 1


def gain_rows(inputs):
    g = np.ones((G_ALL, P), np.float32)
    for n, name in enumerate(("ev_attn_norm", "ev_ffn_norm", "od_attn_norm", "od_ffn_norm")):
        g[G_FWD[n]:G_FWD[n] + KD] = inputs[name].reshape(KD, P)
    g[G_QA:G_KVA] = inputs["od_q_a_norm"].reshape(-1, P)
    g[G_KVA:G_AQ] = inputs["od_kv_a_norm"].reshape(-1, P)
    for row, name in ((G_AQ, "ev_a_q_norm"), (G_AK, "ev_a_k_norm"), (G_BQ, "ev_b_q_norm"), (G_BK, "ev_b_k_norm")):
        g[row, 0:HD] = inputs[name][0]
    for row, name in ((G_CQ, "od_q_norm"), (G_CK, "od_k_norm")):
        g[row, 0:C_NOPE] = inputs[name][0, 0:C_NOPE]
    return g


def constants():
    c = np.zeros((P, C_ALL), np.float32)
    c[:, C_ID:C_ID + P] = np.eye(P)
    c[:, C_TRI:C_TRI + P] = np.triu(np.ones((P, P)), 1)
    c[:, C_IOTA:C_IOTA + P] = np.arange(P)
    for b, at, keys in ((0, 0, P), (1, P, 2 * P)):
        q = (b * P + np.arange(P))[:, None]
        k = np.arange(keys)[None, :]
        qc, kc = q // CHUNK, k // CHUNK
        c[:, C_DIST + at:C_DIST + at + keys] = np.where((kc <= qc) & (kc >= qc - 1), -np.abs(q - k), NEG)
        c[:, C_MASK + at:C_MASK + at + keys] = np.where(kc <= qc, 0.0, NEG)
    pos = np.arange(SEQ, dtype=np.float32)
    power = np.arange(0, C_ROPE, 2, dtype=np.float32) / np.float32(C_ROPE)
    inv = (np.float32(1.0) / (np.float32(10000.0) ** power)).astype(np.float32)
    ang = (pos[:, None] * inv[None, :]).astype(np.float32)
    ang = np.concatenate([ang, ang], axis=-1)
    rot = np.stack([np.cos(ang), np.sin(ang)], axis=1).reshape(TB, P, 2 * C_ROPE)
    c[:, C_ROT:] = rot.transpose(1, 0, 2).reshape(P, -1)
    return c


def plan(w):
    pieces, quarters = [], []

    def add(stage, src, nk, n, place, kind="", c=0):
        per = 2 if n <= NW else 1
        first = len(quarters)
        for k in range(0, nk, per):
            quarters.append((len(pieces), k, min(per, nk - k)))
        pieces.append(dict(stage=stage, src=src, nk=nk, n=n, place=place, kind=kind, c=c, per=per,
                           q0=first, q1=len(quarters)))

    def cols(ap, c0, n):
        return ap[0, :, c0:c0 + n].rearrange("(k p) n -> p k n", p=P)

    for j, c0 in enumerate(range(0, IN_W, NW)):
        add("in", cols(w["w_in"], c0, min(NW, IN_W - c0)), KD, min(NW, IN_W - c0), j)
    for j in range(2):
        add("out", cols(w["w_out"], j * NW, NW), KD, NW, j)
    place = 2
    chunks = [(c0, min(NW, D_FF - c0)) for c0 in range(0, D_FF, NW)]
    down = lambda c: w["w_down"][0, chunks[c][0]:sum(chunks[c]), :].rearrange("(k p) n -> p k n", p=P)
    for c, (c0, n) in enumerate(chunks):
        for kind, name in (("gate", "w_gate"), ("up", "w_up")):
            add("ffn", cols(w[name], c0, n), KD, n, place % RING, kind, c)
            place += 1
        for d in [c - 1] * (c > 0) + [c] * (c == len(chunks) - 1):
            add("ffn", down(d), chunks[d][1] // P, D, place % RING, "down", d)
            place += 1
    small = [("dq", cols(w["w_dq"], 0, Q_LORA), KD, Q_LORA),
             ("dkv", cols(w["w_dkv"], 0, KV_LORA + C_ROPE), KD, KV_LORA + C_ROPE)]
    small += [("uq", cols(w["w_uq"], j * NW, NW), Q_LORA // P, NW) for j in range(3)]
    small += [("ukv", cols(w["w_ukv"], j * NW, NW), KV_LORA // P, NW) for j in range(4)]
    for j, (stage, src, nk, n) in enumerate(small):
        add(stage, src, nk, n, j % 3)
    for j in range(2):
        add("o", cols(w["w_o"], j * NW, NW), KD, NW, 3 + j)
    return pieces, quarters


def expert_order():
    order = []
    n = E_FF // NW
    for c in range(n):
        order += [("gate", c), ("up", c)]
        order += [("down", c - 1)] * (c > 0) + [("down", c)] * (c == n - 1)
    return order


def trunk(nc, a, out):
    x_in, const = a["x"], a["const"]
    weights = {"w_in": a["ev_w_in"], "w_out": a["ev_w_out"], "w_gate": a["ev_w_gate"], "w_up": a["ev_w_up"],
               "w_down": a["ev_w_down"], "w_dq": a["od_w_dq"], "w_uq": a["od_w_uq"], "w_dkv": a["od_w_dkv"],
               "w_ukv": a["od_w_ukv"], "w_o": a["od_w_o"]}
    pieces, quarters = plan(weights)
    NQ = len(quarters)
    order = expert_order()
    EQ = 4 * len(order)
    NCH = E_FF // NW
    uses = [0] * RING
    for p in pieces:
        p["turn"] = uses[p["place"]]
        uses[p["place"]] += 1
    stage_pieces = lambda s: [n for n, p in enumerate(pieces) if p["stage"] == s]

    with ExitStack() as ctx:
        def sb(name, shape, dt=F32):
            return ctx.enter_context(nc.sbuf_tensor(name, shape, dt))

        def sem(name):
            return ctx.enter_context(nc.semaphore(name))

        ring = sb("ring", [P, RING, PIECE])
        w_hi = sb("w_hi", [P, SPLITS, QUARTER], F32R)
        w_lo = sb("w_lo", [P, SPLITS, QUARTER], F32R)
        xres = sb("xres", [P, TB, D])
        h = sb("h", [P, TB, D])
        hT_hi = sb("hT_hi", [P, KD, SEQ], F32R)
        hT_lo = sb("hT_lo", [P, KD, SEQ], F32R)
        aT_hi = sb("aT_hi", [P, 5, SEQ], F32R)
        aT_lo = sb("aT_lo", [P, 5, SEQ], F32R)
        gs = sb("gs", [P, TB, NW])
        act_t = sb("act_t", [P, TB, NW])
        y = sb("y", [P, D])
        cst = sb("cst", [P, C_ALL])
        ones = sb("ones", [P, P])
        g_rows = sb("g_rows", [G_ALL, P])
        g_cols = sb("g_cols", [P, G_ALL])
        gq = sb("gq", [P, C_QK])
        gk = sb("gk", [P, C_QK])
        sinks = sb("sinks", [P, A_HEADS])
        eps = sb("eps", [P, 1])
        ss = sb("ss", [P, 68])
        rt = sb("rt", [P, 68])
        rinv = sb("rinv", [P, 68])
        nmax = sb("nmax", [P, 2, 4])
        mx = sb("mx", [P, 2, 2])
        esum = sb("esum", [P, 2, 4])
        den = sb("den", [P, 2, 2])
        kr = sb("kr", [P, TB, C_ROPE])

        ident = cst[:, C_ID:C_ID + P]
        NORM = 66

        scratch = ring[:, 5:7, :].rearrange("p a b -> p (a b)")
        proj = scratch[:, 0:TB * IN_W].rearrange("p (t n) -> p t n", t=TB)
        kv = scratch[:, 0:4096].rearrange("p (t n) -> p t n", t=TB)
        qc = scratch[:, 4096:7168].rearrange("p (t n) -> p t n", t=TB)
        kbuf = scratch[:, 7168:7168 + KBUFS * TB * C_QK].rearrange("p (b t n) -> p b t n", b=KBUFS, t=TB)
        hf = h[:, :, :].rearrange("p t n -> p (t n)")
        gsf = gs[:, :, :].rearrange("p t n -> p (t n)")
        acf = act_t[:, :, :].rearrange("p t n -> p (t n)")
        qkT = hf[:, 0:1024].rearrange("p (b n) -> p b n", b=2)
        sc = [hf[:, 1024:1024 + LANES], hf[:, 1024 + LANES:1024 + 2 * LANES], acf[:, 0:LANES]]
        pn = gsf[:, 0:2 * LANES].rearrange("p (b n) -> p b n", b=2)
        pT = y[:, 0:2 * LANES].rearrange("p (b n) -> p b n", b=2)
        kr_t = acf[:, 0:2 * C_ROPE].rearrange("p (m n) -> p m n", m=4)
        bias0 = scratch[:, 4608:4608 + B_HEADS * P].rearrange("p (h n) -> p h n", h=B_HEADS)
        bias1 = scratch[:, 5632:5632 + 2 * B_HEADS * P].rearrange("p (h n) -> p h n", h=B_HEADS)
        lat = y[:, 0:TB * Q_LORA].rearrange("p (t n) -> p t n", t=TB)
        lkv = gsf[:, 0:TB * (KV_LORA + C_ROPE)].rearrange("p (t n) -> p t n", t=TB)

        bank = [ctx.enter_context(nc.psum_tensor(f"bank{i}", [P, NW], F32)) for i in range(8)]

        arrived = [sem(f"arrived{i}") for i in range(RING)]
        hi_ready = sem("hi_ready")
        lo_ready = sem("lo_ready")
        quarter_used = sem("quarter_used")
        x_loaded = [sem("x_loaded_0"), sem("x_loaded_1")]
        consts_loaded = sem("consts_loaded")
        tables_loaded = sem("tables_loaded")
        rows_loaded = sem("rows_loaded")
        gains_loaded = sem("gains_loaded")
        ones_set = sem("ones_set")
        gains_turned = sem("gains_turned")
        gain_cols_ready = sem("gain_cols_ready")
        act_step = sem("act_step")
        dve_step = sem("dve_step")
        norm_sqrt = sem("norm_sqrt")
        rinv_ready = sem("rinv_ready")
        h_ready = sem("h_ready")
        hT_turned = sem("hT_turned")
        hT_hi_ready = sem("hT_hi_ready")
        hT_lo_ready = sem("hT_lo_ready")
        copied_act = sem("copied_act")
        copied_dve = sem("copied_dve")
        x_added = sem("x_added")
        squared = sem("squared")
        head_ss = sem("head_ss")
        head_sqrt = sem("head_sqrt")
        head_rinv = sem("head_rinv")
        queries_ready = sem("queries_ready")
        rotated_pool = sem("rotated_pool")
        dve_rinv = sem("dve_rinv")
        pool_step = sem("pool_step")
        normed_pool = sem("normed_pool")
        braw_loaded = sem("braw_loaded")
        bias_ready = sem("bias_ready")
        k_ready = sem("k_ready")
        qk_turned = sem("qk_turned")
        qkT_ready = sem("qkT_ready")
        scored = sem("scored")
        max_ready = sem("max_ready")
        exp_ready = sem("exp_ready")
        p_ready = sem("p_ready")
        p_turned = sem("p_turned")
        pT_ready = sem("pT_ready")
        pv_done = sem("pv_done")
        o_hi = sem("o_hi")
        o_lo = sem("o_lo")
        silu_ready = sem("silu_ready")
        hidden_ready = sem("hidden_ready")
        hidden_turned = sem("hidden_turned")
        aT_hi_ready = sem("aT_hi_ready")
        aT_lo_ready = sem("aT_lo_ready")
        lat_ss = sem("lat_ss")
        lat_rinv = sem("lat_rinv")
        lat_turned = sem("lat_turned")
        lat_hi = sem("lat_hi")
        lat_lo = sem("lat_lo")
        stored = sem("stored")

        lin = []
        na = nd = 0
        for s in ("in", "out", "dq", "dkv", "uq", "ukv", "o"):
            for j, n in enumerate(stage_pieces(s)):
                add = s in ("out", "o")
                na, nd = na + (not add), nd + (not add)
                lin.append(dict(stage=s, piece=n, j=j, n=pieces[n]["n"], add=add, na=na, nd=nd))
        dest = {"in": lambda t, j, n: proj[:, t, j * NW:j * NW + n], "dq": lambda t, j, n: lat[:, t, :],
                "dkv": lambda t, j, n: lkv[:, t, :], "uq": lambda t, j, n: qc[:, t, j * NW:j * NW + n],
                "ukv": lambda t, j, n: kv[:, t, j * NW:j * NW + n]}
        stage_lin = lambda s: [(i, c) for i, c in enumerate(lin) if c["stage"] == s]

        def sources(g):
            if g < A_HEADS:
                kvh = g // (A_HEADS // A_KV)
                return (lambda t: proj[:, t, A_Q + g * HD:A_Q + (g + 1) * HD],
                        lambda t: proj[:, t, A_K + kvh * HD:A_K + (kvh + 1) * HD],
                        lambda t: proj[:, t, A_V + kvh * HD:A_V + (kvh + 1) * HD], HD)
            if g < HEADS0:
                b = g - A_HEADS
                return (lambda t: proj[:, t, B_Q + b * HD:B_Q + (b + 1) * HD],
                        lambda t: proj[:, t, B_K + b * HD:B_K + (b + 1) * HD],
                        lambda t: proj[:, t, B_V + b * HD:B_V + (b + 1) * HD], HD)
            c = g - HEADS0
            return (lambda t: qc[:, t, c * C_QK:(c + 1) * C_QK],
                    lambda t: kbuf[:, g % KBUFS, t, :],
                    lambda t: kv[:, t, c * 128 + C_NOPE:(c + 1) * 128], C_QK)

        def o_place(dst, g):
            m = g % HEADS0
            r = 64 * (m % 2)
            return dst[r:r + 64, m // 2, :]

        def o_psum(g):
            r = 64 * (g % 2)
            return bank[6 + g % 2][r:r + 64, 0:SEQ]

        route = sb("route", [P, 16, TB * N_EXP])
        pos_t = sb("pos_t", [P, TB, SLOTS + 1])
        gate_t = sb("gate_t", [P, TB, SLOTS])
        cnt = sb("cnt", [P, 4, N_EXP])
        ids_f = sb("ids_f", [P, 4])
        ids = sb("ids", [1, 4], I32)
        cur = sb("cur", [P, 3, TB])
        oh = act_t
        wT = act_t[:, :, 2 * CAP:2 * CAP + P]
        router = y[:, 0:KD * N_EXP]
        logitsT = y[0:N_EXP, NW:NW + SEQ]
        logits_done = sem("logits_done")
        logits_copied = sem("logits_copied")
        spare_ready = sem("spare_ready")
        mask_ready = sem("mask_ready")
        counted = sem("counted")
        route_ready = sem("route_ready")
        gain_row_loaded = sem("gain_row_loaded")
        cur_ready = sem("cur_ready")
        slot_ready = sem("slot_ready")
        gathered = sem("gathered")
        weight_turned = sem("weight_turned")
        e_hi = sem("e_hi")
        e_lo = sem("e_lo")
        wT_ready = sem("wT_ready")
        y_act = sem("y_act")
        y_dve = sem("y_dve")
        combined = sem("combined")
        e_silu = sem("e_silu")
        e_hidden = sem("e_hidden")
        e_turned = sem("e_turned")
        e_aT_hi = sem("e_aT_hi")
        e_aT_lo = sem("e_aT_lo")
        e_added = sem("e_added")
        e_once = sem("e_once")

        FACTOR = {"in": (NORM, rinv_ready, 1), "dq": (NORM, rinv_ready, 3), "dkv": (NORM, rinv_ready, 3),
                  "uq": (2, lat_rinv, 1), "ukv": (4, lat_rinv, 1)}
        X_ADDS = {0: 0, 1: 4, 2: 8, 3: 12}

        block = ctx.enter_context(nc.Block())

        @block.sync
        def _(sp):
            sp.dma_start(cst[:, 0:C_DIST], const[:, 0:C_DIST]).then_inc(consts_loaded, 16)
            for half in range(2):
                cols = slice(half * NW, (half + 1) * NW)
                sp.dma_start(xres[:, :, cols], x_in[0].rearrange("(t p) d -> p t d", p=P)[:, :, cols])\
                  .then_inc(x_loaded[half], 16)
            sp.dma_start(g_rows[:, :], a["gains"]).then_inc(gains_loaded, 16)
            for n, p in enumerate(pieces):
                before = [m for m in range(n) if pieces[m]["place"] == p["place"]]
                if before:
                    sp.wait_ge(lo_ready, pieces[before[-1]]["q1"])
                if p["stage"] == "ffn" and p["place"] >= 5 and all(pieces[m]["stage"] != "ffn" for m in before):
                    sp.wait_ge(pv_done, HEADS0)
                dst = ring[:, p["place"], 0:p["nk"] * p["n"]].rearrange("p (k n) -> p k n", k=p["nk"])
                sp.dma_start(dst, p["src"]).then_inc(arrived[p["place"]], 16)
                if n == 0:
                    sp.dma_start(cst[:, C_DIST:], const[:, C_DIST:]).then_inc(tables_loaded, 16)
            def load(e, i, kind, c):
                if kind == "down":
                    src = a["od_e_down"][0, bass.ds(e, 1), c * NW:(c + 1) * NW, :].rearrange(
                        "o (k p) n -> p (o k) n", p=P)
                else:
                    src = a["od_e_" + kind][0, bass.ds(e, 1), :, c * NW:(c + 1) * NW].rearrange(
                        "o (k p) n -> p (o k) n", p=P)
                dst = ring[:, i % RING, :].rearrange("p (k n) -> p k n", k=src.shape[1])
                sp.dma_start(dst, src).then_inc(arrived[i % RING], 16)

            for i, (kind, c) in enumerate(order):
                if i < RING:
                    before = [m for m in range(len(pieces)) if pieces[m]["place"] == i]
                    sp.wait_ge(lo_ready, pieces[before[-1]]["q1"])
                    if i == 5:
                        sp.wait_ge(pv_done, HEADS)
                else:
                    sp.wait_ge(lo_ready, NQ + 4 * (i - RING + 1))
                load(0, i, kind, c)
            with sp.Fori(1, N_EXP) as e:
                for i, (kind, c) in enumerate(order):
                    sp.wait_ge(lo_ready, e * EQ + (NQ + 4 * (i - RING + 1)))
                    load(e, i, kind, c)
            sp.wait_ge(route_ready, 1)
            over = sp.value_load(ids[0:1, 3:4], min_val=0, max_val=OVER)
            sp.wait_ge(spare_ready, 1)
            with sp.If(over > 0):
                with sp.Fori(0, over) as o:
                    e = sp.value_load(ids[0:1, bass.ds(o, 1)], min_val=0, max_val=N_EXP - 1)
                    for i, (kind, c) in enumerate(order):
                        sp.wait_ge(lo_ready, o * EQ + (N_EXP * EQ + NQ + 4 * (i - RING + 1)))
                        load(e, i, kind, c)
            slots = over + N_EXP
            sp.wait_ge(lo_ready, slots * EQ + (NQ + 4 * (1 - RING)))
            load(0, 0, *order[0])
            sp.wait_ge(e_added, slots * 4 + 4)
            sp.dma_start(out[0].rearrange("(t p) d -> p t d", p=P), xres[:, :, :]).then_inc(stored, 16)
            sp.wait_ge(stored, 16)

        def experts_pe(pe, three, turn_norm):
            turn_norm(3)
            pe.wait_ge(hT_lo_ready, 4 * KD)
            for k in range(KD):
                es = slice(k * N_EXP, (k + 1) * N_EXP)
                mm = three(bank[4][0:N_EXP, 0:SEQ], aT_hi[:, 0, es], aT_lo[:, 0, es], hT_hi[:, k, :], hT_lo[:, k, :],
                           k == 0, k == KD - 1)
            mm.then_inc(logits_done, 1)
            pe.wait_ge(logits_copied, 1)
            for t in range(TB):
                mm = pe.transpose(bank[4][:, SEQ + t * N_EXP:SEQ + (t + 1) * N_EXP],
                                  logitsT[:, t * P:(t + 1) * P], ident[0:N_EXP, 0:N_EXP])
            mm.then_inc(logits_done, 1)
            pe.wait_ge(mask_ready, 1)
            mask = lambda t: route[:, 0, t * N_EXP:(t + 1) * N_EXP]
            tri = cst[:, C_TRI:C_TRI + P]
            pe.matmul(bank[5][:, 0:8], tri, mask(0), start=True, stop=True)
            pe.matmul(bank[5][:, 8:16], ones[:, :], mask(0), start=True, stop=False)
            pe.matmul(bank[5][:, 8:16], tri, mask(1), start=False, stop=True)
            pe.matmul(bank[5][:, 16:24], ones[:, :], mask(0), start=True, stop=False)
            pe.matmul(bank[5][:, 16:24], ones[:, :], mask(1), start=False, stop=True).then_inc(counted, 1)

            pe.wait_ge(route_ready, 1)
            over = pe.value_load(ids[0:1, 3:4], min_val=0, max_val=OVER)
            slots = over + N_EXP
            pe.wait_ge(slot_ready, 1)

            def gather():
                for k in range(KD):
                    for t in range(TB):
                        mm = pe.matmul(bank[2 + k // 4][:, (k % 4) * P:(k % 4 + 1) * P],
                                       h[:, t, k * P:(k + 1) * P], oh[:, t, 0:CAP],
                                       start=(t == 0), stop=(t == 1))
                    if k % 4 == 3:
                        mm.then_inc(gathered, 1)

            def quarter(s, q):
                kind, c = order[q // 4 % len(order)]
                j = q % 4
                place = (NQ + q) % SPLITS
                pe.wait_ge(lo_ready, s * EQ + (NQ + q + 1))
                for m in range(2):
                    at = m * NW
                    wh, wl = w_hi[:, place, at:at + NW], w_lo[:, place, at:at + NW]
                    if kind == "down":
                        half = slice(c % 2 * CAP, (c % 2 + 1) * CAP)
                        mm = three(bank[4 + m][:, :], aT_hi[:, j, half], aT_lo[:, j, half], wh, wl,
                                   c == 0 and j == 0, c == NCH - 1 and j == 3)
                    else:
                        k = 2 * j + m
                        b = 2 * (c % 2) + (kind == "up")
                        mm = three(bank[b][:, :], hT_hi[:, k, 0:CAP], hT_lo[:, k, 0:CAP], wh, wl,
                                   k == 0, k == KD - 1)
                mm.then_inc(quarter_used, 1)

            pe.wait_ge(h_ready, 1)
            gather()
            pe.wait_ge(e_lo, 2)
            quarter(0, 0)
            with pe.Fori(0, slots) as s:
                def turn(c):
                    pe.wait_ge(e_hidden, s * NCH + (c + 1))
                    for b in range(4):
                        mm = pe.transpose(bank[6 + c % 2][:, b * P:(b + 1) * P],
                                          y[:, (c % 2) * NW + b * P:(c % 2) * NW + (b + 1) * P], ident)
                    mm.then_inc(e_turned, 1)

                for i, (kind, c) in enumerate(order):
                    if kind != "down" and c == 1:
                        pe.wait_ge(e_added, s * 4 + (1 + (kind == "up")))
                    if kind == "down":
                        pe.wait_ge(e_aT_lo, s * NCH + (c + 1))
                    for j in range(4):
                        if i or j:
                            quarter(s, 4 * i + j)
                        if kind == "down" and c == NCH - 2 and j == 1:
                            turn(NCH - 1)
                    if kind == "up" and c == 0:
                        pe.wait_ge(slot_ready, s + 2)
                        pe.wait_ge(e_added, s * 4 + 4)
                        for t in range(TB):
                            mm = pe.transpose(bank[7][:, t * P:(t + 1) * P], oh[:, t, CAP:2 * CAP], ident)
                        mm.then_inc(weight_turned, 1)
                    if kind == "up" and c == NCH - 1:
                        gather()
                    if kind == "gate" and c:
                        if c == 2:
                            pe.wait_ge(wT_ready, s + 1)
                        turn(c - 1)
                pe.wait_ge(e_lo, s * 2 + 4)
                quarter(s, EQ)
                pe.wait_ge(y_act, s + 1)
                pe.wait_ge(y_dve, s + 1)
                for t in range(TB):
                    for half in range(2):
                        pe.matmul(bank[2 + 4 * t + half][:, :], wT[:, t, :],
                                  y[:, half * NW:(half + 1) * NW], start=True, stop=True).then_inc(combined, 1)

        @block.tensor
        def _(pe):
            def three(dst, hi, lo, whi, wlo, first, final):
                pe.matmul(dst, hi, whi, start=first, stop=False)
                pe.matmul(dst, lo, whi, start=False, stop=False)
                return pe.matmul(dst, hi, wlo, start=False, stop=final)

            def product(q, dst, s_hi, s_lo):
                n, k0, kn = quarters[q]
                p = pieces[n]
                pe.wait_ge(lo_ready, q + 1)
                for k in range(k0, k0 + kn):
                    for t in range(TB):
                        for o in range(0, p["n"], NW):
                            m = min(NW, p["n"] - o)
                            at = (k - k0) * p["n"] + o
                            mm = three(dst(t, o // NW)[:, 0:m], s_hi(k, t), s_lo(k, t),
                                       w_hi[:, q % SPLITS, at:at + m], w_lo[:, q % SPLITS, at:at + m],
                                       *flags(p, k))
                mm.then_inc(quarter_used, 1)
                return mm

            def flags(p, k):
                if p["kind"] != "down":
                    return k == 0, k == p["nk"] - 1
                lastc = max(x["c"] for x in pieces if x["kind"] == "down")
                return k == 0 and p["c"] == 0, k == p["nk"] - 1 and p["c"] == lastc

            def sT(buf):
                return lambda k, t: buf[:, k, t * P:(t + 1) * P]

            def turn_norm(n):
                for b in range(4):
                    if n == 0:
                        pe.wait_ge(x_loaded[b // 2], 16)
                    else:
                        pe.wait_ge(x_added, X_ADDS[n] - 2 * TB + TB * (b // 2 + 1))
                    for kk in range(2):
                        for t in range(TB):
                            k = 2 * b + kk
                            at = kk * SEQ + t * P
                            mm = pe.transpose(bank[b][:, at:at + P], xres[:, t, k * P:(k + 1) * P], ident)
                    mm.then_inc(hT_turned, 1)

            def projection(stage, s_hi, s_lo):
                for i, c in stage_lin(stage):
                    if i >= 2:
                        prev = lin[i - 2]
                        pe.wait_ge(copied_act, prev["na"])
                        pe.wait_ge(copied_dve, prev["nd"])
                    p = pieces[c["piece"]]
                    for q in range(p["q0"], p["q1"]):
                        product(q, lambda t, half: bank[4 + 2 * (i % 2) + t], s_hi, s_lo)

            def attention(g0, g1):
                for i in range(g0, g1 + 5):
                    if i < g1:
                        qs, ks, _, w = sources(i)
                        if i == A_HEADS:
                            pe.wait_ge(normed_pool, 1)
                        if i >= HEADS0:
                            pe.wait_ge(k_ready, i - HEADS0 + 1)
                        for j, src in enumerate((qs(0), qs(1), ks(0), ks(1))):
                            mm = pe.transpose(bank[i % 2][0:w, j * P:(j + 1) * P], src, ident)
                        mm.then_inc(qk_turned, 1)
                    j = i - 1
                    if g0 <= j < g1:
                        w = sources(j)[3]
                        pe.wait_ge(qkT_ready, j + 1)
                        if j >= 2:
                            pe.wait_ge(max_ready, j - 1)
                        s = bank[2 + j % 2]
                        buf = qkT[0:w, j % 2, :]
                        pe.matmul(s[:, 0:P], buf[:, 0:P], buf[:, SEQ:SEQ + P], start=True, stop=True)
                        pe.matmul(s[:, P:LANES], buf[:, P:SEQ], buf[:, SEQ:2 * SEQ], start=True, stop=True)\
                          .then_inc(scored, 1)
                    j = i - 4
                    if g0 <= j < g1:
                        pe.wait_ge(p_ready, j + 1)
                        for m in range(3):
                            mm = pe.transpose(bank[4 + j % 2][:, m * P:(m + 1) * P],
                                              pn[:, j % 2, m * P:(m + 1) * P], ident)
                        mm.then_inc(p_turned, 1)
                    j = i - 5
                    if g0 <= j < g1:
                        vs = sources(j)[2]
                        pe.wait_ge(pT_ready, j + 1)
                        if j >= 2:
                            pe.wait_ge(o_lo, j - 1)
                        o = o_psum(j)
                        pe.matmul(o, vs(0), pT[:, j % 2, 0:SEQ], start=True, stop=False)
                        pe.matmul(o[:, P:SEQ], vs(1), pT[:, j % 2, SEQ:LANES], start=False, stop=True)\
                          .then_inc(pv_done, 1)

            def ffn():
                chunks = max(pieces[n]["c"] for n in stage_pieces("ffn")) + 1
                width = [min(NW, D_FF - c * NW) for c in range(chunks)]

                def turn(c):
                    pe.wait_ge(hidden_ready, c + 1)
                    for b in range(width[c] // P):
                        for t in range(TB):
                            at = (b % 2) * SEQ + t * P
                            mm = pe.transpose(bank[2 * (c % 2) + b // 2][:, at:at + P],
                                              act_t[:, t, b * P:(b + 1) * P], ident)
                    mm.then_inc(hidden_turned, 1)

                for n in stage_pieces("ffn"):
                    p = pieces[n]
                    c = p["c"]
                    if p["kind"] == "gate" and c >= 1:
                        pe.wait_ge(hidden_ready, c)
                    if p["kind"] == "up" and c >= 1:
                        pe.wait_ge(aT_lo_ready, c)
                    if p["kind"] == "down":
                        if c == chunks - 1:
                            turn(c)
                        pe.wait_ge(aT_lo_ready, c + 1)
                    base = {"gate": 2 * (c % 2), "up": 2 - 2 * (c % 2), "down": 4}[p["kind"]]
                    for q in range(p["q0"], p["q1"]):
                        if p["kind"] == "down":
                            product(q, lambda t, half: bank[4 + 2 * t + half], sT(aT_hi), sT(aT_lo))
                        else:
                            product(q, lambda t, half: bank[base + t], sT(hT_hi), sT(hT_lo))
                    if p["kind"] == "up" and c == 0 or p["kind"] == "down" and c < chunks - 2:
                        turn(c if p["kind"] == "up" else c + 1)

            pe.wait_ge(consts_loaded, 16)
            pe.wait_ge(gains_loaded, 16)
            pe.transpose(bank[7][:, 0:G_ALL], g_rows[:, :], ident[0:G_ALL, 0:G_ALL]).then_inc(gains_turned, 1)

            turn_norm(0)
            pe.wait_ge(hT_lo_ready, KD)
            projection("in", sT(hT_hi), sT(hT_lo))
            pe.wait_ge(queries_ready, 1)
            attention(0, HEADS0)
            pe.wait_ge(o_lo, HEADS0)
            projection("out", sT(hT_hi), sT(hT_lo))
            turn_norm(1)
            pe.wait_ge(hT_lo_ready, 2 * KD)
            ffn()
            turn_norm(2)
            pe.wait_ge(hT_lo_ready, 3 * KD)
            projection("dq", sT(hT_hi), sT(hT_lo))
            projection("dkv", sT(hT_hi), sT(hT_lo))
            pe.wait_ge(copied_act, lin[stage_lin("dkv")[-1][0]]["na"])
            pe.wait_ge(copied_dve, lin[stage_lin("dkv")[-1][0]]["nd"])
            for k in range(5):
                for t in range(TB):
                    src = lat[:, t, k * P:(k + 1) * P] if k < 3 else lkv[:, t, (k - 3) * P:(k - 2) * P]
                    mm = pe.transpose(bank[k // 2][:, (k % 2) * SEQ + t * P:(k % 2) * SEQ + (t + 1) * P],
                                      src, ident)
            mm.then_inc(lat_turned, 1)
            pe.wait_ge(lat_lo, 5)
            projection("uq", sT(aT_hi), sT(aT_lo))
            projection("ukv", lambda k, t: aT_hi[:, 3 + k, t * P:(t + 1) * P],
                       lambda k, t: aT_lo[:, 3 + k, t * P:(t + 1) * P])
            pe.wait_ge(queries_ready, 2)
            pe.wait_ge(rotated_pool, 1)
            attention(HEADS0, HEADS)
            pe.wait_ge(o_lo, HEADS)
            projection("o", sT(hT_hi), sT(hT_lo))
            experts_pe(pe, three, turn_norm)

        def experts_act(act, norm):
            act.wait_ge(gain_row_loaded, 32)
            act.activation(aT_hi[:, 0, 0:KD * N_EXP], router, ACT.Copy)\
               .then_inc(e_once, 1)
            norm(3)
            act.activation(rt[:, 0:1], eps[:, 0:1], ACT.Exp)
            act.wait_ge(mask_ready, 1)
            act.activation(route[:, 13, 0:TB], route[:, 12, 0:TB], ACT.Exp).then_inc(e_once, 1)
            act.wait_ge(route_ready, 1)
            over = act.value_load(ids[0:1, 3:4], min_val=0, max_val=OVER)
            slots = over + N_EXP

            def take_gathered(first):
                for m in range(2):
                    act.wait_ge(gathered, first + m)
                    act.activation(hT_hi[:, 4 * m:4 * m + 4, 0:CAP],
                                   bank[2 + m][:, :].rearrange("p (a n) -> p a n", a=4), ACT.Copy)\
                       .then_inc(e_hi, 1)

            take_gathered(1)
            for q in range(LEAD - 1):
                if q == 0:
                    act.wait_ge(arrived[0], 16 * (uses[0] + 1))
                act.wait_ge(quarter_used, NQ + q - SPLITS + 1)
                act.activation(w_hi[:, (NQ + q) % SPLITS, :], ring[:, 0, q * QUARTER:(q + 1) * QUARTER], ACT.Copy)\
                   .then_inc(hi_ready, 1)
            with act.Fori(0, slots) as s:
                def split(q):
                    i, j = q // 4, q % 4
                    if j == 0:
                        turn = i // RING + 1
                        act.wait_ge(arrived[i % RING], s * (16 * len(order) // RING) + 16 * (uses[i % RING] + turn))
                    act.wait_ge(quarter_used, s * EQ + (NQ + q - SPLITS + 1))
                    act.activation(w_hi[:, (NQ + q) % SPLITS, :], ring[:, i % RING, j * QUARTER:(j + 1) * QUARTER],
                                   ACT.Copy).then_inc(hi_ready, 1)

                def turned(c):
                    act.wait_ge(e_turned, s * NCH + (c + 1))
                    act.activation(aT_hi[:, 0:4, c % 2 * CAP:(c % 2 + 1) * CAP],
                                   bank[6 + c % 2][:, :].rearrange("p (a n) -> p a n", a=4),
                                   ACT.Copy).then_inc(e_aT_hi, 1)

                for i, (kind, c) in enumerate(order):
                    for j in range(4):
                        if kind == "down" and c == NCH - 2 and j == 3:
                            turned(NCH - 1)
                        split(4 * i + j + LEAD - 1)
                    if kind == "gate":
                        act.wait_ge(quarter_used, s * EQ + (NQ + 4 * (i + 1)))
                        act.activation(gsf[:, (c % 2) * NW:(c % 2 + 1) * NW], bank[2 * (c % 2)][:, :], ACT.Silu)\
                           .then_inc(e_silu, 1)
                    if kind == "up" and c == NCH - 1:
                        take_gathered(s * 2 + 3)
                    if kind == "gate" and c:
                        turned(c - 1)
                act.wait_ge(quarter_used, s * EQ + (NQ + EQ))
                act.activation(y[:, 0:NW], bank[4][:, :], ACT.Copy).then_inc(y_act, 1)

        @block.scalar
        def _(act):
            step = [0]

            def link(ins):
                step[0] += 1
                ins.then_inc(act_step, 1)
                act.wait_ge(act_step, step[0])

            split = [0]

            def split_to(q1):
                while split[0] < min(q1, NQ):
                    q = split[0]
                    n, k0, kn = quarters[q]
                    p = pieces[n]
                    if k0 == 0:
                        act.wait_ge(arrived[p["place"]], 16 * (p["turn"] + 1))
                    if q >= SPLITS:
                        act.wait_ge(quarter_used, q - SPLITS + 1)
                    m = kn * p["n"]
                    at = k0 * p["n"]
                    act.activation(w_hi[:, q % SPLITS, 0:m], ring[:, p["place"], at:at + m], ACT.Copy)\
                       .then_inc(hi_ready, 1)
                    split[0] += 1

            def load_rows():
                for dst, keys in ((bias0, P), (bias1, 2 * P)):
                    src = bass.AP(a["ev_b_rel_bias"].tensor, MAX_REL + 1 - P,
                                  [[1, P], [2 * MAX_REL + 1, B_HEADS], [1, keys]])
                    act.dma_start(dst, src).then_inc(braw_loaded, 16)
                act.dma_start(sinks[:, :], a["ev_a_sinks"].to_broadcast([P, A_HEADS])).then_inc(rows_loaded, 16)
                act.dma_start(gq[:, :], a["od_q_norm"].to_broadcast([P, C_QK])).then_inc(rows_loaded, 16)
                act.dma_start(gk[:, :], a["od_k_norm"].to_broadcast([P, C_QK])).then_inc(rows_loaded, 16)

            def norm(n):
                if n == 0:
                    act.wait_ge(gain_cols_ready, 1)
                for k in range(KD):
                    if k % 2 == 0:
                        act.wait_ge(hT_turned, 4 * n + k // 2 + 1)
                    act.activation(hT_hi[:, k, :], bank[k // 2][:, (k % 2) * SEQ:(k % 2 + 1) * SEQ], ACT.Copy,
                                   scale=g_cols[:, G_FWD[n] + k:G_FWD[n] + k + 1]).then_inc(hT_hi_ready, 1)
                if n == 0:
                    split_to(LEAD)
                    load_rows()
                    act.wait_ge(x_loaded[0], 16)
                    act.wait_ge(x_loaded[1], 16)
                    act.wait_ge(ones_set, 1)
                else:
                    act.wait_ge(x_added, X_ADDS[n])
                for t in range(TB):
                    sq = act.activation(h[:, t, :], xres[:, t, :], ACT.Square, accum_out=ss[:, NORM + t:NORM + t + 1])
                link(sq)
                act.activation(rt[:, NORM:NORM + TB], ss[:, NORM:NORM + TB], ACT.Sqrt, bias=eps[:, 0:1],
                               scale=1.0 / D).then_inc(norm_sqrt, 1)

            def projection(stage, then=None):
                for i, c in stage_lin(stage):
                    p = pieces[c["piece"]]
                    for q in range(p["q0"], p["q1"]):
                        split_to(q + LEAD)
                    if not c["add"]:
                        act.wait_ge(quarter_used, p["q1"])
                        scale = 1.0
                        if stage in FACTOR:
                            col, ready, n = FACTOR[stage]
                            act.wait_ge(ready, n)
                            scale = rinv[:, col:col + 1]
                        act.activation(dest[stage](0, c["j"], c["n"]), bank[4 + 2 * (i % 2)][:, 0:c["n"]],
                                       ACT.Copy, scale=scale).then_inc(copied_act, 1)
                    if then is not None:
                        then(c["j"], lin[i])

            def attention(g0, g1):
                act.wait_ge(rows_loaded, 48)
                for i in range(g0, g1 + 5):
                    if i < g1:
                        w = sources(i)[3]
                        q_col, k_col = ((G_AQ, G_AK) if i < A_HEADS else (G_BQ, G_BK) if i < HEADS0
                                        else (G_CQ, G_CK))
                        act.wait_ge(qk_turned, i + 1)
                        for at, col in ((0, q_col), (SEQ, k_col)):
                            o = act.activation(qkT[0:w, i % 2, at:at + SEQ], bank[i % 2][0:w, at:at + SEQ],
                                               ACT.Copy, scale=g_cols[0:w, col:col + 1])
                        o.then_inc(qkT_ready, 1)
                    j = i - 2
                    if g0 <= j < g1:
                        act.wait_ge(max_ready, j + 1)
                        b = j % 2
                        act.activation(sc[j % 3][:, 0:P], sc[j % 3][:, 0:P], ACT.Exp, bias=nmax[:, b, 0:1],
                                       accum_out=esum[:, b, 0:1])
                        e = act.activation(sc[j % 3][:, P:LANES], sc[j % 3][:, P:LANES], ACT.Exp, bias=nmax[:, b, 1:2],
                                           accum_out=esum[:, b, 1:2])
                        if j < A_HEADS:
                            e = act.activation(esum[:, b, 2:4], nmax[:, b, 0:2], ACT.Exp,
                                               bias=sinks[:, j:j + 1])
                        e.then_inc(exp_ready, 1)
                    j = i - 4
                    if g0 <= j < g1:
                        act.wait_ge(p_turned, j + 1)
                        act.activation(pT[:, j % 2, :], bank[4 + j % 2][:, 0:LANES], ACT.Copy)\
                           .then_inc(pT_ready, 1)
                    j = i - 5
                    if g0 <= j < g1:
                        act.wait_ge(pv_done, j + 1)
                        act.activation(o_place(hT_hi, j), o_psum(j), ACT.Copy).then_inc(o_hi, 1)

            def ffn():
                for n in stage_pieces("ffn"):
                    p = pieces[n]
                    c = p["c"]
                    if p["kind"] == "down" and p["q1"] == pieces[stage_pieces("ffn")[-1]]["q1"]:
                        turned(c)
                    for q in range(p["q0"], p["q1"]):
                        split_to(q + LEAD)
                    if p["kind"] == "gate":
                        act.wait_ge(quarter_used, p["q1"])
                        act.wait_ge(rinv_ready, 2)
                        for t in range(TB):
                            s = act.activation(gs[:, t, 0:p["n"]], bank[2 * (c % 2) + t][:, 0:p["n"]], ACT.Silu,
                                               scale=rinv[:, NORM + t:NORM + t + 1])
                        s.then_inc(silu_ready, 1)
                    if p["kind"] == "up" and c == 0 or p["kind"] == "down" and c < ffn_chunks - 2:
                        turned(c if p["kind"] == "up" else c + 1)

            ffn_chunks = (D_FF + NW - 1) // NW

            def turned(c):
                act.wait_ge(hidden_turned, c + 1)
                for m in range(min(NW, D_FF - c * NW) // (2 * P)):
                    o = act.activation(aT_hi[:, 2 * m:2 * m + 2, :].rearrange("p a n -> p (a n)"),
                                       bank[2 * (c % 2) + m][:, :], ACT.Copy)
                o.then_inc(aT_hi_ready, 1)

            norm(0)
            def in_squares(j, chunk):
                if j in (1, 3):
                    act.wait_ge(copied_act, chunk["na"])
                    act.wait_ge(copied_dve, chunk["nd"])
                if j == 1:
                    for t in range(TB):
                        act.activation(hf[:, 640 * t:640 * t + 640], proj[:, t, 0:A_V], ACT.Square)\
                           .then_inc(squared, 1)
                if j == 2:
                    act.wait_ge(head_ss, 1)
                    act.activation(rt[:, 0:20], ss[:, 0:20], ACT.Sqrt, bias=eps[:, 0:1], scale=1.0 / HD)\
                       .then_inc(head_sqrt, 1)
                if j == 3:
                    for t in range(TB):
                        act.activation(hf[:, 1024 * t:1024 * t + 1024], proj[:, t, B_Q:B_V], ACT.Square)\
                           .then_inc(squared, 1)
                if j == 4:
                    act.wait_ge(head_ss, 2)
                    act.activation(rt[:, 20:52], ss[:, 20:52], ACT.Sqrt, bias=eps[:, 0:1], scale=1.0 / HD)\
                       .then_inc(head_sqrt, 1)

            projection("in", in_squares)
            attention(0, HEADS0)
            projection("out")
            norm(1)
            ffn()
            norm(2)
            projection("dq")
            projection("dkv")
            act.wait_ge(lat_turned, 1)
            for k in range(5):
                col = G_QA + k
                act.activation(aT_hi[:, k, :], bank[k // 2][:, (k % 2) * SEQ:(k % 2 + 1) * SEQ], ACT.Copy,
                               scale=g_cols[:, col:col + 1]).then_inc(lat_hi, 1)
            act.wait_ge(copied_dve, lin[stage_lin("dkv")[-1][0]]["nd"])
            act.wait_ge(copied_act, lin[stage_lin("dkv")[-1][0]]["na"])
            for t in range(TB):
                act.activation(hf[:, 0:Q_LORA], lat[:, t, :], ACT.Square, accum_out=ss[:, 2 + t:3 + t])
                link(act.activation(hf[:, 384:384 + KV_LORA], lkv[:, t, 0:KV_LORA], ACT.Square,
                                    accum_out=ss[:, 4 + t:5 + t]))
                link(act.activation(hf[:, 0:C_ROPE], lkv[:, t, KV_LORA:], ACT.Square,
                                    accum_out=ss[:, 64 + t:65 + t]))
            act.activation(rt[:, 2:4], ss[:, 2:4], ACT.Sqrt, bias=eps[:, 0:1], scale=1.0 / Q_LORA)
            act.activation(rt[:, 4:6], ss[:, 4:6], ACT.Sqrt, bias=eps[:, 0:1], scale=1.0 / KV_LORA)\
               .then_inc(lat_ss, 1)
            projection("uq")
            act.wait_ge(copied_dve, lin[stage_lin("uq")[-1][0]]["nd"])
            act.wait_ge(copied_act, lin[stage_lin("uq")[-1][0]]["na"])
            for dst, src in ((hf[:, 0:16 * C_QK], qc[:, 0, :]), (gsf[:, 0:10 * C_QK], qc[:, 1, 0:10 * C_QK]),
                             (y[:, 0:6 * C_QK], qc[:, 1, 10 * C_QK:])):
                act.activation(dst, src, ACT.Square).then_inc(squared, 1)

            def key_squares(j, chunk):
                act.wait_ge(copied_act, chunk["na"])
                act.wait_ge(copied_dve, chunk["nd"])
                if j == 0:
                    act.wait_ge(head_ss, 3)
                for t in range(TB):
                    nope = kv[:, t, j * NW:(j + 1) * NW].rearrange("p (h n) -> p h n", h=4)[:, :, 0:C_NOPE]
                    at = (2 * j + t) * 4 * C_NOPE
                    o = act.activation(hf[:, at:at + 4 * C_NOPE].rearrange("p (h n) -> p h n", h=4), nope,
                                       ACT.Square)
                o.then_inc(squared, 1)

            projection("ukv", key_squares)
            act.wait_ge(head_ss, 4)
            act.activation(rt[:, 0:64], ss[:, 0:64], ACT.Sqrt, bias=eps[:, 0:1], scale=1.0 / C_QK)\
               .then_inc(head_sqrt, 1)
            attention(HEADS0, HEADS)
            projection("o")
            experts_act(act, norm)

        def rope(eng, t, buf, link):
            half = C_ROPE // 2
            v = qc[:, t, :].rearrange("p (h n) -> p h n", n=C_QK)
            vr = v[:, :, C_NOPE:]
            link(eng.tensor_tensor(vr, vr, gq[:, C_NOPE:].unsqueeze(1).to_broadcast([P, C_HEADS, C_ROPE]), ALU.mult))
            cos, sin = (cst[:, C_ROT + 64 * t + c:C_ROT + 64 * t + c + 16].unsqueeze(1).to_broadcast(
                [P, C_HEADS, half]) for c in (0, C_ROPE))
            q1, q2 = v[:, :, C_NOPE:C_NOPE + half], v[:, :, C_NOPE + half:]
            tmp = buf.rearrange("p (m h n) -> p m h n", m=4, h=C_HEADS)
            for m, (u, w) in enumerate(((q1, cos), (q2, sin), (q2, cos), (q1, sin))):
                o = eng.tensor_tensor(tmp[:, m], u, w, ALU.mult)
            link(o)
            eng.tensor_tensor(q1, tmp[:, 0], tmp[:, 1], ALU.subtract)
            return eng.tensor_tensor(q2, tmp[:, 2], tmp[:, 3], ALU.add)

        def experts_dve(dve, norm, link):
            R = lambda i: route[:, i, :].rearrange("p (t e) -> p t e", e=N_EXP)
            dve.wait_ge(gain_row_loaded, 32)
            dve.wait_ge(e_once, 1)
            dve.tensor_tensor(aT_lo[:, 0, 0:KD * N_EXP], router, aT_hi[:, 0, 0:KD * N_EXP].bitcast(F32), ALU.subtract)
            norm(3)
            for t in range(TB):
                o = dve.scalar_tensor_tensor(h[:, t, :], xres[:, t, :], rinv[:, NORM + t:NORM + t + 1], acf[:, 0:D],
                                             ALU.mult, ALU.mult)
            o.then_inc(h_ready, 1)
            dve.wait_ge(logits_done, 1)
            dve.tensor_copy(logitsT, bank[4][0:N_EXP, 0:SEQ]).then_inc(logits_copied, 1)
            dve.wait_ge(logits_done, 2)
            for t in range(TB):
                es = slice(t * N_EXP, (t + 1) * N_EXP)
                o = dve.tensor_scalar(route[:, 1, es], bank[4][:, SEQ + t * N_EXP:SEQ + (t + 1) * N_EXP],
                                      rinv[:, NORM + t:NORM + t + 1], None, ALU.mult)
            link(o)
            below = cst[:, C_IOTA:C_IOTA + N_EXP].unsqueeze(1).to_broadcast([P, TB, N_EXP])
            link(dve.tensor_scalar(R(14), below, -float(N_EXP), None, ALU.add))
            wide = lambda v: v.unsqueeze(2).to_broadcast([P, TB, N_EXP])
            for n, (src, hot, top) in enumerate(((1, 2, 10), (3, 4, 11))):
                m = route[:, top, 0:TB]
                first = route[:, top, TB:2 * TB]
                link(dve.tensor_reduce(m, R(src), AX.X, ALU.max))
                link(dve.tensor_tensor(R(5), R(src), wide(m), ALU.is_equal))
                link(dve.tensor_tensor(R(5), R(5), R(14), ALU.mult))
                link(dve.tensor_reduce(first, R(5), AX.X, ALU.min))
                link(dve.tensor_tensor(R(hot), R(14), wide(first), ALU.is_equal))
                if n == 0:
                    link(dve.scalar_tensor_tensor(R(3), R(2), -3e38, R(1), ALU.mult, ALU.add))
            dve.tensor_tensor(R(0), R(2), R(4), ALU.add)
            dve.tensor_tensor(route[:, 12, 0:TB], route[:, 11, 0:TB], route[:, 10, 0:TB], ALU.subtract)\
               .then_inc(mask_ready, 1)
            dve.wait_ge(e_once, 2)
            w1, w2 = route[:, 15, 0:TB], route[:, 15, TB:2 * TB]
            link(dve.tensor_scalar(w1, route[:, 13, 0:TB], 1.0, None, ALU.add))
            link(dve.reciprocal(w1, w1))
            link(dve.tensor_tensor(w2, route[:, 13, 0:TB], w1, ALU.mult))
            dve.tensor_tensor(R(6), R(2), wide(w1), ALU.mult)
            link(dve.tensor_tensor(R(7), R(4), wide(w2), ALU.mult))
            link(dve.tensor_tensor(R(6), R(6), R(7), ALU.add))
            dve.wait_ge(counted, 1)
            link(dve.tensor_tensor(R(8), bank[5][:, 0:TB * N_EXP].rearrange("p (t e) -> p t e", e=N_EXP), R(0),
                                   ALU.mult))
            link(dve.tensor_tensor(R(8), R(8), R(0), ALU.add))
            link(dve.tensor_scalar(R(8), R(8), -1.0, None, ALU.add))
            link(dve.tensor_copy(cnt[:, 0, :], bank[5][:, 16:24]))
            link(dve.tensor_scalar(cnt[:, 1, :], cnt[:, 0, :], float(CAP) + 0.5, None, ALU.is_gt))
            dve.tensor_copy(pos_t[:, :, 0:N_EXP], R(8))
            dve.memset(pos_t[:, :, SLOTS:], -1.0)
            dve.tensor_copy(gate_t[:, :, 0:N_EXP], R(6))
            link(dve.tensor_reduce(ids_f[:, 3:4], cnt[:, 1, :], AX.X, ALU.add))
            dve.tensor_copy(ids[0:1, 3:4], ids_f[0:1, 3:4]).then_inc(route_ready, 1)
            dve.wait_ge(route_ready, 1)
            over = dve.value_load(ids[0:1, 3:4], min_val=0, max_val=OVER)
            slots = over + N_EXP
            iota = cst[:, C_IOTA:C_IOTA + CAP]
            for t in range(TB):
                o = dve.tensor_scalar(oh[:, t, 0:CAP], iota, pos_t[:, t, 0:1], None, ALU.is_equal)
            o.then_inc(slot_ready, 1)

            def take_gathered(first):
                for m in range(2):
                    dve.wait_ge(e_hi, first + m)
                    dve.tensor_tensor(hT_lo[:, 4 * m:4 * m + 4, 0:CAP],
                                      bank[2 + m][:, :].rearrange("p (a n) -> p a n", a=4),
                                      hT_hi[:, 4 * m:4 * m + 4, 0:CAP].bitcast(F32), ALU.subtract).then_inc(e_lo, 1)

            take_gathered(1)
            for q in range(LEAD - 1):
                dve.wait_ge(hi_ready, NQ + q + 1)
                place = (NQ + q) % SPLITS
                dve.tensor_tensor(w_lo[:, place, :], ring[:, 0, q * QUARTER:(q + 1) * QUARTER],
                                  w_hi[:, place, :].bitcast(F32), ALU.subtract).then_inc(lo_ready, 1)
            dve.memset(mx[:, 0, 0:1], 0.0).then_inc(e_added, 4)
            with dve.Fori(0, slots) as s:
                dve.wait_ge(spare_ready, 1)
                def split(q):
                    i, j = q // 4, q % 4
                    place = (NQ + q) % SPLITS
                    dve.wait_ge(hi_ready, s * EQ + (NQ + q + 1))
                    dve.tensor_tensor(w_lo[:, place, :], ring[:, i % RING, j * QUARTER:(j + 1) * QUARTER],
                                      w_hi[:, place, :].bitcast(F32), ALU.subtract).then_inc(lo_ready, 1)

                def turned(c):
                    dve.wait_ge(e_aT_hi, s * NCH + (c + 1))
                    half = slice(c % 2 * CAP, (c % 2 + 1) * CAP)
                    dve.tensor_tensor(aT_lo[:, 0:4, half], bank[6 + c % 2][:, :].rearrange("p (a n) -> p a n", a=4),
                                      aT_hi[:, 0:4, half].bitcast(F32), ALU.subtract).then_inc(e_aT_lo, 1)

                for i, (kind, c) in enumerate(order):
                    for j in range(4):
                        if kind == "down" and c == NCH - 2 and j == 3:
                            turned(NCH - 1)
                        split(4 * i + j + LEAD - 1)
                    if kind == "up":
                        dve.wait_ge(quarter_used, s * EQ + (NQ + 4 * (i + 1)))
                        dve.wait_ge(e_silu, s * NCH + (c + 1))
                        at = slice((c % 2) * NW, (c % 2 + 1) * NW)
                        dve.tensor_tensor(y[:, at], gsf[:, at], bank[2 * (c % 2) + 1][:, :], ALU.mult)\
                           .then_inc(e_hidden, 1)
                    if kind == "gate" and c == 0:
                        dve.tensor_copy(cur[:, 0, :].unsqueeze(2), pos_t[:, :, bass.ds(s, 1)])
                        dve.tensor_copy(cur[:, 1, :].unsqueeze(2), gate_t[:, :, bass.ds(s, 1)])
                        dve.tensor_copy(cur[:, 2, :].unsqueeze(2), pos_t[:, :, bass.ds(s + 1, 1)])\
                           .then_inc(cur_ready, 1)
                        dve.wait_ge(cur_ready, s + 1)
                        for t in range(TB):
                            dve.tensor_scalar(oh[:, t, CAP:2 * CAP], iota, cur[:, 0, t:t + 1], cur[:, 1, t:t + 1],
                                              ALU.is_equal, ALU.mult)
                            o = dve.tensor_scalar(oh[:, t, 0:CAP], iota, cur[:, 2, t:t + 1], None, ALU.is_equal)
                        o.then_inc(slot_ready, 1)
                    if kind == "up" and c == 0:
                        dve.wait_ge(weight_turned, s + 1)
                        dve.tensor_copy(wT, bank[7][:, 0:SEQ].rearrange("p (t n) -> p t n", t=TB))\
                           .then_inc(wT_ready, 1)
                    if kind == "up" and c == NCH - 1:
                        take_gathered(s * 2 + 3)
                    if kind == "gate" and c:
                        turned(c - 1)
                dve.wait_ge(quarter_used, s * EQ + (NQ + EQ))
                dve.tensor_copy(y[:, NW:2 * NW], bank[5][:, :]).then_inc(y_dve, 1)
                for t in range(TB):
                    for half in range(2):
                        xs = xres[:, t, half * NW:(half + 1) * NW]
                        dve.wait_ge(combined, s * 4 + (2 * t + half + 1))
                        dve.tensor_tensor(xs, xs, bank[2 + 4 * t + half][:, :], ALU.add).then_inc(e_added, 1)

        @block.vector
        def _(dve):
            step = [0]

            def mark(ins):
                step[0] += 1
                ins.then_inc(dve_step, 1)
                return step[0]

            def link(ins):
                step[0] += 1
                ins.then_inc(dve_step, 1)
                dve.wait_ge(dve_step, step[0])

            split = [0]

            def split_to(q1):
                while split[0] < min(q1, NQ):
                    q = split[0]
                    n, k0, kn = quarters[q]
                    p = pieces[n]
                    m = kn * p["n"]
                    at = k0 * p["n"]
                    dve.wait_ge(hi_ready, q + 1)
                    dve.tensor_tensor(w_lo[:, q % SPLITS, 0:m], ring[:, p["place"], at:at + m],
                                      w_hi[:, q % SPLITS, 0:m].bitcast(F32), ALU.subtract).then_inc(lo_ready, 1)
                    split[0] += 1

            def norm(n):
                if n == 0:
                    dve.wait_ge(gains_turned, 1)
                    link(dve.tensor_copy(g_cols[:, :], bank[7][:, 0:G_ALL]))
                    dve.tensor_scalar(g_cols[:, G_AQ:G_AQ + 1], g_cols[:, G_AQ:G_AQ + 1], HD ** -0.5, None, ALU.mult)
                    dve.tensor_scalar(g_cols[:, G_BQ:G_BQ + 1], g_cols[:, G_BQ:G_BQ + 1], HD ** -0.5, None, ALU.mult)\
                       .then_inc(gain_cols_ready, 1)
                    dve.wait_ge(gain_cols_ready, 1)
                for k in range(KD):
                    dve.wait_ge(hT_hi_ready, KD * n + 2 * (k // 2) + 2)
                    dve.scalar_tensor_tensor(hT_lo[:, k, :], bank[k // 2][:, (k % 2) * SEQ:(k % 2 + 1) * SEQ],
                                             g_cols[:, G_FWD[n] + k:G_FWD[n] + k + 1], hT_hi[:, k, :].bitcast(F32),
                                             ALU.mult, ALU.subtract).then_inc(hT_lo_ready, 1)
                if n == 0:
                    split_to(LEAD)
                dve.wait_ge(norm_sqrt, n + 1)
                dve.reciprocal(rinv[:, NORM:NORM + TB], rt[:, NORM:NORM + TB]).then_inc(rinv_ready, 1)
                dve.wait_ge(rinv_ready, n + 1)

            def projection(stage, then=None):
                for i, c in stage_lin(stage):
                    p = pieces[c["piece"]]
                    for q in range(p["q0"], p["q1"]):
                        split_to(q + LEAD)
                    dve.wait_ge(quarter_used, p["q1"])
                    if not c["add"]:
                        d, src = dest[stage](1, c["j"], c["n"]), bank[5 + 2 * (i % 2)][:, 0:c["n"]]
                        if stage in FACTOR:
                            col = FACTOR[stage][0] + 1
                            o = dve.tensor_scalar(d, src, rinv[:, col:col + 1], None, ALU.mult)
                        else:
                            o = dve.tensor_copy(d, src)
                        o.then_inc(copied_dve, 1)
                        if then is not None:
                            then(c["j"])
                    else:
                        for t in range(TB):
                            xs = xres[:, t, c["j"] * NW:(c["j"] + 1) * NW]
                            dve.tensor_tensor(xs, xs, bank[4 + 2 * (i % 2) + t][:, :], ALU.add).then_inc(x_added, 1)

            def attention(g0, g1):
                dve.wait_ge(rows_loaded, 48)
                dve.wait_ge(tables_loaded, 16)
                for i in range(g0, g1 + 5):
                    n, j = i - 3, i - 1
                    norm_, score = g0 <= n < g1, g0 <= j < g1
                    sn, sj, s = sc[n % 3], sc[j % 3], bank[2 + j % 2][:, 0:LANES]
                    en, mj = esum[:, n % 2, :], mx[:, j % 2, :]
                    if norm_:
                        dve.wait_ge(exp_ready, n + 1)
                        if n < A_HEADS:
                            summed = mark(dve.tensor_tensor(en[:, 0:2], en[:, 0:2], en[:, 2:4], ALU.add))
                    if score:
                        if j >= 3:
                            dve.wait_ge(p_ready, j - 2)
                        dve.wait_ge(scored, j + 1)
                        if j < A_HEADS:
                            o = dve.scalar_tensor_tensor(sj, cst[:, C_DIST:C_DIST + LANES],
                                                         2.0 ** (-8.0 * (j + 1) / A_HEADS), s, ALU.mult, ALU.add)
                        else:
                            if j < HEADS0:
                                dve.wait_ge(bias_ready, 1)
                                dve.wait_ge(head_rinv, 1)
                                c0, c1, hb = 20, 36, j - A_HEADS
                                b0, b1 = bias0[:, hb, ::-1], bias1[:, hb, ::-1]
                            else:
                                c0, c1, hb = 0, 16, j - HEADS0
                                b0, b1 = cst[:, C_MASK:C_MASK + P], cst[:, C_MASK + P:C_MASK + LANES]
                            dve.scalar_tensor_tensor(sj[:, 0:P], s[:, 0:P], rinv[:, c0 + hb:c0 + hb + 1], b0,
                                                     ALU.mult, ALU.add)
                            o = dve.scalar_tensor_tensor(sj[:, P:LANES], s[:, P:], rinv[:, c1 + hb:c1 + hb + 1], b1,
                                                         ALU.mult, ALU.add)
                        biased = mark(o)
                    if norm_:
                        if n < A_HEADS:
                            dve.wait_ge(dve_step, summed)
                        inverted = mark(dve.reciprocal(den[:, n % 2, :], en[:, 0:2]))
                    if score:
                        dve.wait_ge(dve_step, biased)
                        dve.tensor_reduce(mj[:, 0:1], sj[:, 0:P], AX.X, ALU.max)
                    if norm_:
                        dve.wait_ge(dve_step, inverted)
                        if n >= 2:
                            dve.wait_ge(p_turned, n - 1)
                        dve.tensor_scalar(pn[:, n % 2, 0:P], sn[:, 0:P], den[:, n % 2, 0:1], None, ALU.mult)
                    if score:
                        most = mark(dve.tensor_reduce(mj[:, 1:2], sj[:, P:LANES], AX.X, ALU.max))
                    if norm_:
                        dve.tensor_scalar(pn[:, n % 2, P:LANES], sn[:, P:LANES], den[:, n % 2, 1:2], None, ALU.mult)\
                           .then_inc(p_ready, 1)
                    if score:
                        dve.wait_ge(dve_step, most)
                        if j < A_HEADS:
                            dve.tensor_scalar(nmax[:, j % 2, 0:2], mj, sinks[:, j:j + 1], -1.0, ALU.max, ALU.mult)\
                               .then_inc(max_ready, 1)
                        else:
                            dve.tensor_scalar(nmax[:, j % 2, 0:2], mj, -1.0, None, ALU.mult).then_inc(max_ready, 1)
                    j = i - 5
                    if g0 <= j < g1:
                        dve.wait_ge(o_hi, j + 1)
                        dve.tensor_tensor(o_place(hT_lo, j), o_psum(j), o_place(hT_hi, j).bitcast(F32),
                                          ALU.subtract).then_inc(o_lo, 1)

            ffn_chunks = (D_FF + NW - 1) // NW

            def turned(c):
                dve.wait_ge(aT_hi_ready, c + 1)
                for m in range(min(NW, D_FF - c * NW) // (2 * P)):
                    two = lambda b: b[:, 2 * m:2 * m + 2, :].rearrange("p a n -> p (a n)")
                    o = dve.tensor_tensor(two(aT_lo), bank[2 * (c % 2) + m][:, :], two(aT_hi).bitcast(F32),
                                          ALU.subtract)
                o.then_inc(aT_lo_ready, 1)

            def ffn():
                for n in stage_pieces("ffn"):
                    p = pieces[n]
                    c = p["c"]
                    if p["kind"] == "down" and n == stage_pieces("ffn")[-1]:
                        turned(c)
                    for q in range(p["q0"], p["q1"]):
                        split_to(q + LEAD)
                    if p["kind"] == "up":
                        dve.wait_ge(quarter_used, p["q1"])
                        dve.wait_ge(silu_ready, c + 1)
                        for t in range(TB):
                            o = dve.scalar_tensor_tensor(act_t[:, t, 0:p["n"]], bank[2 - 2 * (c % 2) + t][:, 0:p["n"]],
                                                         rinv[:, NORM + t:NORM + t + 1], gs[:, t, 0:p["n"]],
                                                         ALU.mult, ALU.mult)
                        o.then_inc(hidden_ready, 1)
                    if p["kind"] == "up" and c == 0 or p["kind"] == "down" and c < ffn_chunks - 2:
                        turned(c if p["kind"] == "up" else c + 1)
                dve.wait_ge(quarter_used, p["q1"])
                for half in range(2):
                    for t in range(TB):
                        xs = xres[:, t, half * NW:(half + 1) * NW]
                        dve.tensor_tensor(xs, xs, bank[4 + 2 * t + half][:, :], ALU.add).then_inc(x_added, 1)

            dve.memset(eps[:, :], EPS)
            dve.memset(ones[:, :], 1.0).then_inc(ones_set, 1)
            dve.wait_ge(x_loaded[0], 16)
            dve.wait_ge(x_loaded[1], 16)
            dve.wait_ge(consts_loaded, 16)
            norm(0)
            def in_sums(j):
                if j == 1:
                    for t in range(TB):
                        dve.wait_ge(squared, t + 1)
                        o = dve.tensor_reduce(ss[:, 10 * t:10 * t + 10],
                                              hf[:, 640 * t:640 * t + 640].rearrange("p (h n) -> p h n", n=HD),
                                              AX.X, ALU.add)
                    o.then_inc(head_ss, 1)
                if j == 2:
                    dve.wait_ge(head_sqrt, 1)
                    link(dve.reciprocal(rinv[:, 0:20], rt[:, 0:20]))
                    for t in range(TB):
                        v = proj[:, t, 0:A_V].rearrange("p (h n) -> p h n", n=HD)
                        o = dve.tensor_tensor(v, v, rinv[:, 10 * t:10 * t + 10].unsqueeze(2).to_broadcast([P, 10, HD]),
                                              ALU.mult)
                    o.then_inc(queries_ready, 1)
                if j == 3:
                    for t in range(TB):
                        dve.wait_ge(squared, TB + t + 1)
                        o = dve.tensor_reduce(ss[:, 20 + 16 * t:36 + 16 * t],
                                              hf[:, 1024 * t:1024 * t + 1024].rearrange("p (h n) -> p h n", n=HD),
                                              AX.X, ALU.add)
                    o.then_inc(head_ss, 1)
                if j == 4:
                    dve.wait_ge(head_sqrt, 2)
                    dve.reciprocal(rinv[:, 20:52], rt[:, 20:52]).then_inc(head_rinv, 1)

            projection("in", in_sums)
            attention(0, HEADS0)
            projection("out")
            norm(1)
            ffn()
            norm(2)
            projection("dq")
            projection("dkv")
            for k in range(5):
                dve.wait_ge(lat_hi, min(5, 2 * (k // 2) + 2))
                col = G_QA + k
                dve.scalar_tensor_tensor(aT_lo[:, k, :], bank[k // 2][:, (k % 2) * SEQ:(k % 2 + 1) * SEQ],
                                         g_cols[:, col:col + 1], aT_hi[:, k, :].bitcast(F32), ALU.mult,
                                         ALU.subtract).then_inc(lat_lo, 1)
            dve.wait_ge(lat_ss, 1)
            dve.reciprocal(rinv[:, 2:6], rt[:, 2:6]).then_inc(lat_rinv, 1)
            dve.wait_ge(lat_rinv, 1)
            for t in range(TB):
                cos, sin = (cst[:, C_ROT + 64 * t + c:C_ROT + 64 * t + c + 16] for c in (0, C_ROPE))
                src = lkv[:, t, KV_LORA:]
                dve.wait_ge(gains_loaded, 16)
                link(dve.tensor_tensor(src, src, gk[:, C_NOPE:], ALU.mult))
                k1, k2 = src[:, 0:16], src[:, 16:32]
                for m, (u, v) in enumerate(((k1, cos), (k2, sin), (k2, cos), (k1, sin))):
                    o = dve.tensor_tensor(kr_t[:, m, :], u, v, ALU.mult)
                link(o)
                dve.tensor_tensor(kr[:, t, 0:16], kr_t[:, 0, :], kr_t[:, 1, :], ALU.subtract)
                link(dve.tensor_tensor(kr[:, t, 16:32], kr_t[:, 2, :], kr_t[:, 3, :], ALU.add))
            projection("uq")
            dve.wait_ge(squared, 5)
            rope(dve, 0, acf, link).then_inc(queries_ready, 1)

            def key_sums(j):
                if j == 0:
                    dve.tensor_reduce(ss[:, 0:16], hf[:, 0:1536].rearrange("p (h n) -> p h n", n=C_QK),
                                      AX.X, ALU.add).then_inc(head_ss, 1)
                    dve.wait_ge(squared, 7)
                    dve.tensor_reduce(ss[:, 16:26], gsf[:, 0:10 * C_QK].rearrange("p (h n) -> p h n", n=C_QK),
                                      AX.X, ALU.add)
                    dve.tensor_reduce(ss[:, 26:32], y[:, 0:6 * C_QK].rearrange("p (h n) -> p h n", n=C_QK),
                                      AX.X, ALU.add)
                dve.wait_ge(squared, 8 + j)
                for t in range(TB):
                    at = (2 * j + t) * 4 * C_NOPE
                    o = dve.tensor_reduce(ss[:, 32 + 16 * t + 4 * j:36 + 16 * t + 4 * j],
                                          hf[:, at:at + 4 * C_NOPE].rearrange("p (h n) -> p h n", n=C_NOPE),
                                          AX.X, ALU.add)
                if j == 3:
                    link(o)
                    for t in range(TB):
                        o = dve.tensor_scalar(ss[:, 32 + 16 * t:48 + 16 * t], ss[:, 32 + 16 * t:48 + 16 * t],
                                              ss[:, 64 + t:65 + t], None, ALU.add)
                    o.then_inc(head_ss, 1)

            projection("ukv", key_sums)
            dve.wait_ge(head_sqrt, 3)
            dve.reciprocal(rinv[:, 32:64], rt[:, 32:64]).then_inc(head_rinv, 1)
            dve.reciprocal(rinv[:, 0:32], rt[:, 0:32]).then_inc(dve_rinv, 1)
            dve.wait_ge(dve_rinv, 1)
            link(dve.tensor_scalar(rinv[:, 0:32], rinv[:, 0:32], C_QK ** -0.5, None, ALU.mult))
            attention(HEADS0, HEADS)
            projection("o")
            experts_dve(dve, norm, link)

        @block.gpsimd
        def _(pool):
            pool.wait_ge(tables_loaded, 16)
            pool.wait_ge(braw_loaded, 32)
            for raw, c0, keys in ((bias0, C_MASK, P), (bias1, C_MASK + P, 2 * P)):
                m = cst[:, c0:c0 + keys][:, ::-1].unsqueeze(1).to_broadcast([P, B_HEADS, keys])
                o = pool.tensor_tensor(raw, raw, m, ALU.add)
            o.then_inc(bias_ready, 1)

            pool.wait_ge(head_rinv, 1)
            for t in range(TB):
                v = proj[:, t, B_K:B_V].rearrange("p (h n) -> p h n", n=HD)
                r = rinv[:, 28 + 16 * t:36 + 16 * t]
                o = pool.tensor_tensor(v, v, r.unsqueeze(2).to_broadcast([P, B_HEADS, HD]), ALU.mult)
            o.then_inc(normed_pool, 1)
            step = [0]

            def link(ins):
                step[0] += 1
                ins.then_inc(pool_step, 1)
                pool.wait_ge(pool_step, step[0])

            def row_sum(dst, src, tmp):
                link(pool.tensor_tensor(tmp[:, :, 0:4], src[:, :, 0:4], src[:, :, 4:8], ALU.add))
                link(pool.tensor_tensor(tmp[:, :, 4:6], tmp[:, :, 0:2], tmp[:, :, 2:4], ALU.add))
                return pool.tensor_tensor(dst.unsqueeze(2), tmp[:, :, 4:5], tmp[:, :, 5:6], ALU.add)

            def make_k(c):
                if c >= KBUFS:
                    pool.wait_ge(qk_turned, HEADS0 + c - KBUFS + 1)
                b = (HEADS0 + c) % KBUFS
                for t in range(TB):
                    r = rinv[:, 32 + 16 * t + c:33 + 16 * t + c]
                    pool.tensor_scalar(kbuf[:, b, t, 0:C_NOPE], kv[:, t, c * 128:c * 128 + C_NOPE], r, None,
                                       ALU.mult)
                    o = pool.tensor_scalar(kbuf[:, b, t, C_NOPE:], kr[:, t, :], r, None, ALU.mult)
                o.then_inc(k_ready, 1)

            pool.wait_ge(rows_loaded, 48)
            pool.wait_ge(squared, 7)
            rope(pool, 1, scratch[:, 7168:8192], link).then_inc(rotated_pool, 1)
            pool.wait_ge(rotated_pool, 1)
            pool.wait_ge(head_rinv, 2)
            for c in range(C_HEADS):
                make_k(c)
            pool.wait_ge(pv_done, HEADS)
            pool.dma_start(acf[:, 0:D], a["od_ffn_norm"].to_broadcast([P, D])).then_inc(gain_row_loaded, 16)
            pool.dma_start(router.rearrange("p (k e) -> p k e", e=N_EXP),
                           a["od_router"][0].rearrange("(k p) e -> p k e", p=P)).then_inc(gain_row_loaded, 16)
            R = lambda i: route[:, i, :].rearrange("p (t e) -> p t e", e=N_EXP)
            pool.wait_ge(route_ready, 1)
            link(pool.memset(cnt[:, 2, :], 0.0))
            for e in range(1, N_EXP):
                link(pool.tensor_tensor(cnt[:, 2, e:e + 1], cnt[:, 2, e - 1:e], cnt[:, 1, e - 1:e], ALU.add))
            for o in range(OVER):
                link(pool.tensor_scalar(cnt[:, 3, :], cnt[:, 2, :], float(o), None, ALU.is_equal))
                link(pool.tensor_tensor(cnt[:, 3, :], cnt[:, 3, :], cnt[:, 1, :], ALU.mult))
                pick = cnt[:, 3, :].unsqueeze(1).to_broadcast([P, TB, N_EXP])
                link(pool.tensor_scalar(R(9), R(8), 1.0 - CAP, None, ALU.add))
                link(pool.tensor_tensor(R(9), R(9), pick, ALU.mult))
                link(row_sum(pos_t[:, :, N_EXP + o], R(9), R(3)))
                link(pool.tensor_scalar(pos_t[:, :, N_EXP + o], pos_t[:, :, N_EXP + o], -1.0, None, ALU.add))
                link(pool.tensor_tensor(R(9), R(6), pick, ALU.mult))
                link(row_sum(gate_t[:, :, N_EXP + o], R(9), R(3)))
                link(pool.tensor_tensor(cnt[:, 3, :], cnt[:, 3, :], cst[:, C_IOTA:C_IOTA + N_EXP], ALU.mult))
                link(row_sum(ids_f[:, o:o + 1], cnt[:, 3:4, :], cnt[:, 0:1, :]))
            pool.tensor_copy(ids[0:1, 0:OVER], ids_f[0:1, 0:OVER]).then_inc(spare_ready, 1)

    return


_INS = ["x", "ev_w_in", "ev_a_sinks", "ev_b_rel_bias", "ev_w_out", "ev_w_gate", "ev_w_up", "ev_w_down", "od_w_dq",
        "od_w_uq", "od_w_dkv", "od_w_ukv", "od_q_norm", "od_k_norm", "od_w_o", "od_ffn_norm", "od_router",
        "od_e_gate", "od_e_up", "od_e_down"]


def kernel(**inputs):
    import concourse.bacc as _bacc
    from concourse.bass_utils import run_bass_kernel_spmd as _run

    nc = _bacc.Bacc("TRN2", target_bir_lowering=False, num_devices=1)
    arrays, args = {}, {}
    given = {name: np.ascontiguousarray(inputs[name]) for name in _INS}
    given["const"] = constants()
    given["gains"] = gain_rows(inputs)
    for name, v in given.items():
        arrays[f"in_{name}_dram"] = v
        args[name] = nc.dram_tensor(f"in_{name}_dram", v.shape, mybir.dt.from_np(v.dtype), kind="ExternalInput").ap()
    out = nc.dram_tensor("out_0_dram", (1, SEQ, D), F32, kind="ExternalOutput").ap()
    trunk(nc, args, out)
    r = _run(nc, [arrays], core_ids=[0])
    return r.results[0]["out_0_dram"]
```
